# Optimizing a Trainium2 kernel written in Bass

```python
import jax, jax.numpy as jnp
from jax import lax
import numpy as np

D_MODEL = 1024
BATCH = 1
SEQ = 512
DEPTH = 1

CHUNK = 64
Q_BLOCK = 128
ROPE_THETA = 500000.0
EPS = 1e-6
NEG = -1e30

MLA_HEADS = 8
MLA_Q_LORA = 384
MLA_KV_LORA = 256
MLA_NOPE = 64
MLA_ROPE = 32
MLA_V = 64

DSA_HEADS = 8
DSA_HEAD_DIM = 64
DSA_ROT = DSA_HEAD_DIM // 4
IDX_HEADS = 8
IDX_DIM = 64
IDX_ROT = IDX_DIM // 4
DSA_TOPK_MAX = 256

N_GROUPS = 8
EXPERTS_PER_GROUP = 4
N_EXPERTS = N_GROUPS * EXPERTS_PER_GROUP
EXPERT_FF = 256
TOPK_IN_GROUP = 2

IN_SIZES = (
    MLA_Q_LORA,
    MLA_KV_LORA,
    MLA_ROPE,
    DSA_HEADS * DSA_HEAD_DIM,
    DSA_HEADS * DSA_HEAD_DIM,
    DSA_HEADS * DSA_HEAD_DIM,
    IDX_HEADS * IDX_DIM,
    IDX_DIM,
    IDX_HEADS,
    D_MODEL,
    D_MODEL,
)
IN_WIDTH = sum(IN_SIZES)


def rmsnorm(x, g):
    xf = x.astype(jnp.float32)
    y = xf * lax.rsqrt(jnp.mean(xf * xf, axis=-1, keepdims=True) + EPS)
    return (y * g.astype(jnp.float32)).astype(x.dtype)

def rope(x, pos, rot_dim):
    half = rot_dim // 2
    inv_freq = ROPE_THETA ** (-jnp.arange(half, dtype=jnp.float32) * 2.0 / rot_dim)
    ang = pos.astype(jnp.float32)[:, None] * inv_freq[None, :]
    cos = jnp.cos(ang)[:, None, :]
    sin = jnp.sin(ang)[:, None, :]
    xr = x[..., :rot_dim].astype(jnp.float32)
    x1, x2 = xr[..., :half], xr[..., half:]
    rot = jnp.concatenate([x1 * cos - x2 * sin, x2 * cos + x1 * sin], axis=-1).astype(x.dtype)
    return jnp.concatenate([rot, x[..., rot_dim:]], axis=-1)

def _to_blocks(a):
    b, s = a.shape[0], a.shape[1]
    return a.reshape(b, s // Q_BLOCK, Q_BLOCK, *a.shape[2:]).swapaxes(0, 1)

def _from_blocks(a):
    a = a.swapaxes(0, 1)
    return a.reshape(a.shape[0], a.shape[1] * a.shape[2], *a.shape[3:])

def chunk_causal_attention(q, k, v, scale):
    s_len = q.shape[1]
    nb = s_len // Q_BLOCK
    key_chunk = jnp.arange(s_len) // CHUNK

    def one_block(args):
        qi, bi = args
        q_chunk = (bi * Q_BLOCK + jnp.arange(Q_BLOCK)) // CHUNK
        mask = key_chunk[None, :] <= q_chunk[:, None]
        s = jnp.einsum('bqhd,bkhd->bhqk', qi, k).astype(jnp.float32) * scale
        s = jnp.where(mask[None, None], s, NEG)
        p = jax.nn.softmax(s, axis=-1).astype(v.dtype)
        return jnp.einsum('bhqk,bkhd->bqhd', p, v)

    out = lax.map(one_block, (_to_blocks(q), jnp.arange(nb)))
    return _from_blocks(out)

def indexed_sparse_attention(q, k, v, q_idx, k_idx, w_idx, top_k):
    s_len = q.shape[1]
    nb = s_len // Q_BLOCK
    key_chunk = jnp.arange(s_len) // CHUNK
    gather = jax.vmap(lambda a, i: a[i])

    def one_block(args):
        qi, qii, wi, bi = args
        q_chunk = (bi * Q_BLOCK + jnp.arange(Q_BLOCK)) // CHUNK
        adm = key_chunk[None, :] <= q_chunk[:, None]
        logits = jnp.einsum('bqhd,bkd->bqhk', qii, k_idx).astype(jnp.float32) * (IDX_DIM ** -0.5)
        score = jnp.einsum('bqh,bqhk->bqk', wi.astype(jnp.float32), jax.nn.relu(logits))
        score = jnp.where(adm[None], score, -jnp.inf)
        _, sel = lax.top_k(score, top_k)
        sel_ok = (sel // CHUNK) <= q_chunk[None, :, None]
        k_sel = gather(k, sel)
        v_sel = gather(v, sel)
        s = jnp.einsum('bqhd,bqkhd->bhqk', qi, k_sel).astype(jnp.float32) * (DSA_HEAD_DIM ** -0.5)
        s = jnp.where(sel_ok[:, None], s, NEG)
        p = jax.nn.softmax(s, axis=-1).astype(v.dtype)
        return jnp.einsum('bhqk,bqkhd->bqhd', p, v_sel)

    out = lax.map(one_block, (_to_blocks(q), _to_blocks(q_idx), _to_blocks(w_idx), jnp.arange(nb)))
    return _from_blocks(out)

def hierarchical_moe(h, w_router_group, b_router_group, w_router_expert, b_router_expert,
                     w_gate, w_up, w_down):
    t = h.shape[0]
    group_logits = jnp.matmul(h, w_router_group).astype(jnp.float32) + b_router_group.astype(jnp.float32)
    p_group = jax.nn.softmax(group_logits, axis=-1)
    g_sel = jnp.argmax(group_logits, axis=-1)
    w_grp = jnp.take_along_axis(p_group, g_sel[:, None], axis=-1)
    exp_logits = (jnp.matmul(h, w_router_expert).astype(jnp.float32)
                  + b_router_expert.astype(jnp.float32)).reshape(t, N_GROUPS, EXPERTS_PER_GROUP)
    in_group = jnp.take_along_axis(exp_logits, g_sel[:, None, None], axis=1)[:, 0]
    top_vals, top_idx = lax.top_k(in_group, TOPK_IN_GROUP)
    w_top = jax.nn.softmax(top_vals, axis=-1) * w_grp
    expert_id = g_sel[:, None] * EXPERTS_PER_GROUP + top_idx
    combine = jnp.sum(jax.nn.one_hot(expert_id, N_EXPERTS, dtype=jnp.float32) * w_top[..., None],
                      axis=1).astype(h.dtype)
    out = jnp.zeros_like(h)
    for e in range(N_EXPERTS):
        hid = jax.nn.silu(jnp.matmul(h, w_gate[e])) * jnp.matmul(h, w_up[e])
        out = out + jnp.matmul(hid, w_down[e]) * combine[:, e:e + 1]
    return out

def hybrid_layer(x, pos, norm_mix_g, w_in, mla_q_norm_g, w_uq, mla_kv_norm_g, w_uk, w_uv,
                 w_o_a, w_o_b, w_out, norm_ffn_g, w_router_group, b_router_group,
                 w_router_expert, b_router_expert, w_gate, w_up, w_down):
    b, s, d = x.shape
    h = rmsnorm(x, norm_mix_g)
    proj = jnp.einsum('bsd,de->bse', h, w_in)
    splits = np.cumsum(IN_SIZES)[:-1].tolist()
    (c_q, c_kv, k_r, q_b, k_b, v_b, q_i, k_i, w_i, g_a, g_b) = jnp.split(proj, splits, axis=-1)

    c_q = rmsnorm(c_q, mla_q_norm_g)
    q_a = jnp.einsum('bsr,re->bse', c_q, w_uq).reshape(b, s, MLA_HEADS, MLA_NOPE + MLA_ROPE)
    q_a = jnp.concatenate([q_a[..., :MLA_NOPE], rope(q_a[..., MLA_NOPE:], pos, MLA_ROPE)], axis=-1)
    c_kv = rmsnorm(c_kv, mla_kv_norm_g)
    k_nope = jnp.einsum('bsr,re->bse', c_kv, w_uk).reshape(b, s, MLA_HEADS, MLA_NOPE)
    v_a = jnp.einsum('bsr,re->bse', c_kv, w_uv).reshape(b, s, MLA_HEADS, MLA_V)
    k_pe = rope(k_r[:, :, None, :], pos, MLA_ROPE)
    k_a = jnp.concatenate([k_nope, jnp.broadcast_to(k_pe, (b, s, MLA_HEADS, MLA_ROPE))], axis=-1)
    o_a = chunk_causal_attention(q_a, k_a, v_a, (MLA_NOPE + MLA_ROPE) ** -0.5)
    y_a = jnp.einsum('bse,ed->bsd', o_a.reshape(b, s, MLA_HEADS * MLA_V), w_o_a)

    q_b = rope(q_b.reshape(b, s, DSA_HEADS, DSA_HEAD_DIM), pos, DSA_ROT)
    k_b = rope(k_b.reshape(b, s, DSA_HEADS, DSA_HEAD_DIM), pos, DSA_ROT)
    v_b = v_b.reshape(b, s, DSA_HEADS, DSA_HEAD_DIM)
    q_i = rope(q_i.reshape(b, s, IDX_HEADS, IDX_DIM), pos, IDX_ROT)
    k_i = rope(k_i[:, :, None, :], pos, IDX_ROT)[:, :, 0, :]
    top_k = min(DSA_TOPK_MAX, s // 4)
    o_b = indexed_sparse_attention(q_b, k_b, v_b, q_i, k_i, w_i * (IDX_HEADS ** -0.5), top_k)
    y_b = jnp.einsum('bse,ed->bsd', o_b.reshape(b, s, DSA_HEADS * DSA_HEAD_DIM), w_o_b)

    y = jax.nn.sigmoid(g_a) * y_a + jax.nn.sigmoid(g_b) * y_b
    x = x + jnp.einsum('bsd,de->bse', y, w_out)

    h2 = rmsnorm(x, norm_ffn_g).reshape(b * s, d)
    m = hierarchical_moe(h2, w_router_group, b_router_group, w_router_expert, b_router_expert,
                         w_gate, w_up, w_down)
    return x + m.reshape(b, s, d)

def first_inputs(seed: int = 0) -> dict:
    key = jax.random.key(seed)
    ks = jax.random.split(key, 20)
    f32 = jnp.float32
    L = DEPTH

    def dense(k, shape, fan_in):
        return jax.random.normal(k, shape, f32) * (fan_in ** -0.5)

    def gain(k, shape):
        return 1.0 + 0.05 * jax.random.normal(k, shape, f32)

    return {
        'x': jax.random.normal(ks[0], (BATCH, SEQ, D_MODEL), f32),
        'norm_mix_g': gain(ks[1], (L, D_MODEL)),
        'w_in': dense(ks[2], (L, D_MODEL, IN_WIDTH), D_MODEL),
        'mla_q_norm_g': gain(ks[3], (L, MLA_Q_LORA)),
        'w_uq': dense(ks[4], (L, MLA_Q_LORA, MLA_HEADS * (MLA_NOPE + MLA_ROPE)), MLA_Q_LORA),
        'mla_kv_norm_g': gain(ks[5], (L, MLA_KV_LORA)),
        'w_uk': dense(ks[6], (L, MLA_KV_LORA, MLA_HEADS * MLA_NOPE), MLA_KV_LORA),
        'w_uv': dense(ks[7], (L, MLA_KV_LORA, MLA_HEADS * MLA_V), MLA_KV_LORA),
        'w_o_a': dense(ks[8], (L, MLA_HEADS * MLA_V, D_MODEL), MLA_HEADS * MLA_V),
        'w_o_b': dense(ks[9], (L, DSA_HEADS * DSA_HEAD_DIM, D_MODEL), DSA_HEADS * DSA_HEAD_DIM),
        'w_out': dense(ks[10], (L, D_MODEL, D_MODEL), D_MODEL),
        'norm_ffn_g': gain(ks[11], (L, D_MODEL)),
        'w_router_group': dense(ks[12], (L, D_MODEL, N_GROUPS), D_MODEL),
        'b_router_group': 0.01 * jax.random.normal(ks[13], (L, N_GROUPS), f32),
        'w_router_expert': dense(ks[14], (L, D_MODEL, N_EXPERTS), D_MODEL),
        'b_router_expert': 0.01 * jax.random.normal(ks[15], (L, N_EXPERTS), f32),
        'w_gate': dense(ks[16], (L, N_EXPERTS, D_MODEL, EXPERT_FF), D_MODEL),
        'w_up': dense(ks[17], (L, N_EXPERTS, D_MODEL, EXPERT_FF), D_MODEL),
        'w_down': dense(ks[18], (L, N_EXPERTS, EXPERT_FF, D_MODEL), EXPERT_FF),
        'final_norm_g': gain(ks[19], (D_MODEL,)),
    }

def first_block(x, norm_mix_g, w_in, mla_q_norm_g, w_uq, mla_kv_norm_g, w_uk, w_uv, w_o_a, w_o_b,
              w_out, norm_ffn_g, w_router_group, b_router_group, w_router_expert, b_router_expert,
              w_gate, w_up, w_down, final_norm_g):
    pos = jnp.arange(x.shape[1], dtype=jnp.int32)
    for l in range(DEPTH):
        x = hybrid_layer(x, pos, norm_mix_g[l], w_in[l], mla_q_norm_g[l], w_uq[l], mla_kv_norm_g[l],
                         w_uk[l], w_uv[l], w_o_a[l], w_o_b[l], w_out[l], norm_ffn_g[l],
                         w_router_group[l], b_router_group[l], w_router_expert[l],
                         b_router_expert[l], w_gate[l], w_up[l], w_down[l])
    return rmsnorm(x, final_norm_g)


N_META = 16
CONV_WIDTH = D_MODEL
CONV_KERNEL = 31
RWKV_HEAD = 64
RWKV_HEADS = D_MODEL // RWKV_HEAD
RWKV_WIDTH = RWKV_HEADS * RWKV_HEAD
DECAY_LORA = 64
ICLR_LORA = 64
GATE_LORA = 160
D_FF = 2816
FFN_KERNEL = 3
ALPHA = (2.0 * DEPTH) ** 0.25
BETA = (8.0 * DEPTH) ** -0.25
LN_EPS = 1e-5
GN_EPS = 64e-5

N_RWKV_COLS = 3 * RWKV_WIDTH + DECAY_LORA + ICLR_LORA + GATE_LORA
N_IN = 2 * CONV_WIDTH + N_RWKV_COLS + 2 * D_MODEL


def layer_norm(x, g, b, eps=LN_EPS):
    xf = x.astype(jnp.float32)
    mu = jnp.mean(xf, axis=-1, keepdims=True)
    xc = xf - mu
    var = jnp.mean(xc * xc, axis=-1, keepdims=True)
    y = xc * lax.rsqrt(var + eps) * g.astype(jnp.float32) + b.astype(jnp.float32)
    return y.astype(x.dtype)

def causal_dwconv(x, w):
    k, c = w.shape
    return lax.conv_general_dilated(
        x, w[:, None, :].astype(x.dtype), window_strides=(1,), padding=[(k - 1, 0)],
        dimension_numbers=("NWC", "WIO", "NWC"), feature_group_count=c)

def token_shift(p):
    return jnp.pad(p, ((0, 0), (1, 0), (0, 0)))[:, :-1]

def rwkv7_recurrence(r, decay, k, v, a, b):
    bsz, _, h, n = r.shape

    def step(s, inp):
        r_t, w_t, k_t, v_t, a_t, b_t = inp
        sa = jnp.einsum("bhvk,bhk->bhv", s, a_t)
        s = s * w_t[:, :, None, :] + sa[..., None] * b_t[:, :, None, :] + v_t[..., None] * k_t[:, :, None, :]
        y = jnp.einsum("bhvk,bhk->bhv", s, r_t)
        return s, y

    xs = tuple(jnp.moveaxis(z, 1, 0) for z in (r, decay, k, v, a, b))
    s0 = jnp.zeros((bsz, h, n, n), jnp.float32)
    _, ys = lax.scan(step, s0, xs)
    return jnp.moveaxis(ys, 0, 1)

def rwkv7_time_mix(p, mu, w0, w_decay_up, a0, a_up, g_up, k_k, k_a, r_k, lnx_g, lnx_b, w_out):
    bsz, t, _ = p.shape
    h, n, wd = RWKV_HEADS, RWKV_HEAD, RWKV_WIDTH
    p = p + (token_shift(p) - p) * mu
    i1, i2, i3 = wd, 2 * wd, 3 * wd
    i4, i5 = i3 + DECAY_LORA, i3 + DECAY_LORA + ICLR_LORA
    r, k, v = p[..., :i1], p[..., i1:i2], p[..., i2:i3]
    xw, xa, xg = p[..., i3:i4], p[..., i4:i5], p[..., i5:]
    w = -jax.nn.softplus(-(w0 + jnp.tanh(xw) @ w_decay_up)) - 0.5
    a = jax.nn.sigmoid(a0 + xa @ a_up)
    g = jax.nn.sigmoid(xg) @ g_up
    heads = lambda z: z.reshape(bsz, t, h, n).astype(jnp.float32)
    kk = heads(k * k_k)
    kk = kk / jnp.maximum(jnp.sqrt(jnp.sum(kk * kk, axis=-1, keepdims=True)), 1e-12)
    k = k * (1.0 + (a - 1.0) * k_a)
    decay = jnp.exp(-jnp.exp(heads(w)))
    rh, kh, vh, ah = heads(r), heads(k), heads(v), heads(a)
    o = rwkv7_recurrence(rh, decay, kh, vh, -kk, kk * ah)
    o = layer_norm(o, lnx_g.reshape(h, n), lnx_b.reshape(h, n), GN_EPS)
    o = o + jnp.sum(rh * kh * r_k.astype(jnp.float32), axis=-1, keepdims=True) * vh
    o = o.reshape(bsz, t, wd).astype(p.dtype) * g
    return o @ w_out

def conformer_conv(p, conv_dw, conv_dw_b, conv_ln_g, conv_ln_b, w_conv_out):
    c = p[..., :CONV_WIDTH] * jax.nn.sigmoid(p[..., CONV_WIDTH:])
    c = causal_dwconv(c, conv_dw) + conv_dw_b
    c = jax.nn.silu(layer_norm(c, conv_ln_g, conv_ln_b))
    return c @ w_conv_out

def conv_gated_mlp(h, ffn_up, ffn_dw, ffn_down):
    u = causal_dwconv(h @ ffn_up, ffn_dw)
    return (jax.nn.silu(u[..., D_FF:]) * u[..., :D_FF]) @ ffn_down

def second_inputs(seed: int = 0) -> dict:
    key = jax.random.key(seed)
    ks = iter(jax.random.split(key, 40))
    L, D = DEPTH, D_MODEL

    def nrm(shape, scale):
        return scale * jax.random.normal(next(ks), shape, jnp.float32)

    def gain(shape):
        return 1.0 + nrm(shape, 0.02)

    def unif(shape, lo, hi):
        return jax.random.uniform(next(ks), shape, jnp.float32, minval=lo, maxval=hi)

    return {
        "x": nrm((BATCH, SEQ, D), 1.0),
        "meta_tokens": nrm((N_META, D), 1.0),
        "ln_in_g": gain((D,)),
        "ln_in_b": nrm((D,), 0.02),
        "w_in": nrm((L, D, N_IN), D ** -0.5),
        "b_gate": nrm((L, 2 * D), 0.02),
        "conv_dw": nrm((L, CONV_KERNEL, CONV_WIDTH), CONV_KERNEL ** -0.5),
        "conv_dw_b": nrm((L, CONV_WIDTH), 0.02),
        "conv_ln_g": gain((L, CONV_WIDTH)),
        "conv_ln_b": nrm((L, CONV_WIDTH), 0.02),
        "w_conv_out": nrm((L, CONV_WIDTH, D), CONV_WIDTH ** -0.5),
        "rwkv_mu": unif((L, N_RWKV_COLS), 0.1, 0.9),
        "w0": unif((L, RWKV_WIDTH), -6.5, -1.5),
        "w_decay_up": nrm((L, DECAY_LORA, RWKV_WIDTH), 0.1 * DECAY_LORA ** -0.5),
        "a0": nrm((L, RWKV_WIDTH), 0.1),
        "a_up": nrm((L, ICLR_LORA, RWKV_WIDTH), 0.1 * ICLR_LORA ** -0.5),
        "g_up": nrm((L, GATE_LORA, RWKV_WIDTH), GATE_LORA ** -0.5),
        "k_k": 0.85 + nrm((L, RWKV_WIDTH), 0.02),
        "k_a": gain((L, RWKV_WIDTH)),
        "r_k": -0.04 + nrm((L, RWKV_HEADS, RWKV_HEAD), 0.02),
        "lnx_g": gain((L, RWKV_WIDTH)),
        "lnx_b": nrm((L, RWKV_WIDTH), 0.02),
        "w_rwkv_out": nrm((L, RWKV_WIDTH, D), RWKV_WIDTH ** -0.5),
        "w_o": nrm((L, D, D), BETA * D ** -0.5),
        "ln1_g": gain((L, D)),
        "ln1_b": nrm((L, D), 0.02),
        "ffn_up": nrm((L, D, 2 * D_FF), D ** -0.5),
        "ffn_dw": nrm((L, FFN_KERNEL, 2 * D_FF), FFN_KERNEL ** -0.5),
        "ffn_down": nrm((L, D_FF, D), BETA * D_FF ** -0.5),
        "ln2_g": gain((L, D)),
        "ln2_b": nrm((L, D), 0.02),
    }

def second_block(x, meta_tokens, ln_in_g, ln_in_b, w_in, b_gate, conv_dw, conv_dw_b, conv_ln_g,
              conv_ln_b, w_conv_out, rwkv_mu, w0, w_decay_up, a0, a_up, g_up, k_k, k_a, r_k,
              lnx_g, lnx_b, w_rwkv_out, w_o, ln1_g, ln1_b, ffn_up, ffn_dw, ffn_down, ln2_g, ln2_b):
    bsz = x.shape[0]
    meta = jnp.broadcast_to(meta_tokens[None].astype(x.dtype), (bsz, N_META, D_MODEL))
    h = layer_norm(jnp.concatenate([meta, x], axis=1), ln_in_g, ln_in_b)
    c_end = 2 * CONV_WIDTH
    r_end = c_end + N_RWKV_COLS
    for l in range(DEPTH):
        p = h @ w_in[l]
        y_conv = conformer_conv(p[..., :c_end], conv_dw[l], conv_dw_b[l], conv_ln_g[l],
                                conv_ln_b[l], w_conv_out[l])
        y_rwkv = rwkv7_time_mix(p[..., c_end:r_end], rwkv_mu[l], w0[l], w_decay_up[l], a0[l],
                                a_up[l], g_up[l], k_k[l], k_a[l], r_k[l], lnx_g[l], lnx_b[l],
                                w_rwkv_out[l])
        gates = jax.nn.sigmoid(p[..., r_end:] + b_gate[l])
        y = gates[..., :D_MODEL] * y_conv + gates[..., D_MODEL:] * y_rwkv
        h = layer_norm(ALPHA * h + y @ w_o[l], ln1_g[l], ln1_b[l])
        h = layer_norm(ALPHA * h + conv_gated_mlp(h, ffn_up[l], ffn_dw[l], ffn_down[l]),
                       ln2_g[l], ln2_b[l])
    return h[:, N_META:]


_first_inputs = second_inputs


def second_inputs(seed=0):
    import zlib

    import numpy as np

    out = dict(_first_inputs(seed))
    spreads = {}
    factors = {'ln_in_b': 2.74,
     'b_gate': 8.0,
     'conv_dw_b': 8.0,
     'conv_ln_g': 8.0,
     'conv_ln_b': 8.0,
     'w_decay_up': 8.0,
     'a0': 8.0,
     'a_up': 8.0,
     'k_k': 8.0,
     'k_a': 8.0,
     'r_k': 8.0,
     'lnx_g': 8.0,
     'lnx_b': 8.0,
     'ln1_g': 2.737,
     'ln1_b': 2.693,
     'ln2_g': 2.933,
     'ln2_b': 2.769}
    for name, (base, spread) in spreads.items():
        noise = np.random.default_rng([zlib.crc32(name.encode()), seed]).standard_normal(out[name].shape)
        drawn = base * np.exp(spread * noise) if base else spread * noise
        out[name] = __import__('jax').numpy.asarray(drawn.astype(out[name].dtype))
    for name, factor in factors.items():
        out[name] = (out[name] * factor).astype(out[name].dtype)
    return out


_narrow_inputs = second_inputs


def second_inputs(seed=0):

    out = dict(_narrow_inputs(seed))
    wider = {'conv_ln_g': 3.93,
     'conv_ln_b': 3.71,
     'k_k': 6.05,
     'k_a': 3.91,
     'lnx_g': 5.37,
     'lnx_b': 5.09,
     'ln2_g': 3.28,
     'ln2_b': 3.3}
    for name, times in wider.items():
        mean = out[name].mean()
        out[name] = (mean + times * (out[name] - mean)).astype(out[name].dtype)
    return out


def setup_inputs(seed=0):
    out = dict(first_inputs(seed))
    for name, value in second_inputs(seed + 1).items():
        if name != "x":
            out[name + "_2"] = value
    return out


def reference(
    x, norm_mix_g, w_in, mla_q_norm_g, w_uq, mla_kv_norm_g, w_uk, w_uv, w_o_a, w_o_b, w_out,
    norm_ffn_g, w_router_group, b_router_group, w_router_expert, b_router_expert, w_gate, w_up,
    w_down, final_norm_g, meta_tokens_2, ln_in_g_2, ln_in_b_2, w_in_2, b_gate_2, conv_dw_2,
    conv_dw_b_2, conv_ln_g_2, conv_ln_b_2, w_conv_out_2, rwkv_mu_2, w0_2, w_decay_up_2, a0_2,
    a_up_2, g_up_2, k_k_2, k_a_2, r_k_2, lnx_g_2, lnx_b_2, w_rwkv_out_2, w_o_2, ln1_g_2,
    ln1_b_2, ffn_up_2, ffn_dw_2, ffn_down_2, ln2_g_2, ln2_b_2,
):
    x = first_block(
        x, norm_mix_g, w_in, mla_q_norm_g, w_uq, mla_kv_norm_g, w_uk, w_uv, w_o_a, w_o_b, w_out,
        norm_ffn_g, w_router_group, b_router_group, w_router_expert, b_router_expert, w_gate,
        w_up, w_down, final_norm_g,
    )
    return second_block(
        x, meta_tokens_2, ln_in_g_2, ln_in_b_2, w_in_2, b_gate_2, conv_dw_2, conv_dw_b_2,
        conv_ln_g_2, conv_ln_b_2, w_conv_out_2, rwkv_mu_2, w0_2, w_decay_up_2, a0_2, a_up_2,
        g_up_2, k_k_2, k_a_2, r_k_2, lnx_g_2, lnx_b_2, w_rwkv_out_2, w_o_2, ln1_g_2, ln1_b_2,
        ffn_up_2, ffn_dw_2, ffn_down_2, ln2_g_2, ln2_b_2,
    )


_drawn_inputs = setup_inputs


def setup_inputs(seed=0):
    import zlib

    import numpy as np

    out = dict(_drawn_inputs(seed))
    spreads = {}
    factors = {'mla_q_norm_g': 2.944, 'b_router_group': 2.857, 'b_router_expert': 3.609}
    for name, (base, spread) in spreads.items():
        noise = np.random.default_rng([zlib.crc32(name.encode()), seed]).standard_normal(out[name].shape)
        drawn = base * np.exp(spread * noise) if base else spread * noise
        out[name] = __import__('jax').numpy.asarray(drawn.astype(out[name].dtype))
    for name, factor in factors.items():
        out[name] = (out[name] * factor).astype(out[name].dtype)
    return out
```

```python
from contextlib import ExitStack

import numpy as np

import concourse.bass as bass
from concourse import mybir

F32 = mybir.dt.float32
ALU = mybir.AluOpType
ACT = mybir.ActivationFunctionType
AX = mybir.AxisListType.X

P = 128
D = 1024
KD = D // P
T1 = 512
META = 16
T2 = T1 + META
RING = 4
NEG = -1e30
TAKEN = -3e38

QL, KVL = 384, 256
HEADS = 8
NOPE, ROPE_D = 64, 32
HD = 64
TOPK = 128
N_EXP, FF = 32, 256
GROUPS = 8
TAPS = 31
D_FF = 2816
NF = D_FF // P
ALPHA = 2.0 ** 0.25
RH = 16
CH = 64

SLAB_COUNTS = [
    ("c_q", 3), ("c_kv", 2), ("q_b", 4), ("k_b", 4), ("q_i", 4), ("k_i", 1), ("k_r", 1),
    ("g_a", 8), ("g_b", 8), ("v_b", 4), ("w_uq", 3), ("w_uk", 2), ("w_uv", 1),
    ("w_o_a", 4), ("w_o_b", 4), ("w_out", 8), ("moe", 6 * N_EXP),
    ("conv_in", 16), ("rw_r", 8), ("rw_k", 8), ("rw_v", 8), ("rw_wa", 1), ("rw_g", 2),
    ("gate_a", 8), ("conv_out", 8), ("wa_up", 1),
    ("g_up", 2), ("gate_b", 8), ("rw_out", 8), ("w_o2", 8), ("ffn_up", 2 * NF), ("ffn_down", NF),
]
SLAB0, _n = {}, 0
for _name, _c in SLAB_COUNTS:
    SLAB0[_name] = _n
    _n += _c
N_SLABS = _n

PARAM_COLS = [
    ("norm_mix_g", 8), ("mla_q_norm_g", 3), ("mla_kv_norm_g", 2), ("norm_ffn_g", 8), ("final_norm_g", 8),
    ("ln_in_g", 8), ("ln_in_b", 8), ("b_gate", 16), ("conv_dw", 8 * TAPS), ("conv_dw_b", 8),
    ("conv_ln_g", 8), ("conv_ln_b", 8), ("mu", 27), ("w0", 8), ("a0", 8), ("k_k", 8), ("k_a", 8),
    ("r_k", 8), ("lnx_g", 8), ("lnx_b", 8), ("ln1_g", 8), ("ln1_b", 8), ("ffn_dw", 3 * 2 * NF),
    ("ln2_g", 8), ("ln2_b", 8), ("router", 8 * 40), ("w_i", 64), ("meta", 8 * META),
]
PCOL, _n = {}, 0
for _name, _c in PARAM_COLS:
    PCOL[_name] = _n
    _n += _c
N_PARAMS = _n

CONST0 = [("ident", P), ("mean1024", P), ("ones64", P), ("mean64", P), ("eps", 4)]
CONST1 = [("mean384", P), ("mean256", P), ("rot64", P), ("rot96", P), ("cos64", T1), ("sin64", T1),
          ("cos96", T1), ("sin96", T1), ("causal", T1), ("rev8", 8), ("rev32", 32)]
CONST2 = [("levels", 6 * P), ("level0_low", P), ("strict", P), ("incl", P), ("resets", T2)]


def offsets(table):
    out, n = {}, 0
    for name, c in table:
        out[name] = n
        n += c
    return out, n


C0, N0 = offsets(CONST0)
C1, N1 = offsets(CONST1)
C2, N2 = offsets(CONST2)
EPS_RMS, EPS_LN, EPS_GN = 0, 1, 2


def shape_constants():
    f = np.float32
    eye = np.eye(P, dtype=f)
    blk = np.kron(np.eye(2, dtype=f), np.ones((64, 64), f))
    c0 = np.zeros((P, N0), f)
    c0[:, C0["ident"]:][:, :P] = eye
    c0[:, C0["mean1024"]:][:, :P] = 1.0 / D
    c0[:, C0["ones64"]:][:, :P] = blk
    c0[:, C0["mean64"]:][:, :P] = blk / 64
    c0[:, C0["eps"]:][:, :4] = np.array([1e-6, 1e-5, 64e-5, 0], f)
    c1 = np.zeros((P, N1), f)
    c1[:, C1["mean384"]:][:, :P] = f(1.0 / QL)
    c1[:, C1["mean256"]:][:, :P] = f(1.0 / KVL)

    def rotation(starts, rot):
        half = rot // 2
        m, cos, sin = np.zeros((P, P), f), np.ones((P, T1), f), np.zeros((P, T1), f)
        inv = (f(500000.0) ** (-np.arange(half, dtype=f) * f(2.0) / f(rot))).astype(f)
        ang = (np.arange(T1, dtype=f)[:, None] * inv[None, :]).astype(f)
        for s in starts:
            for i in range(half):
                m[s + i + half, s + i] = -1.0
                m[s + i, s + i + half] = 1.0
                for r in (s + i, s + i + half):
                    cos[r], sin[r] = np.cos(ang[:, i]), np.sin(ang[:, i])
        return m, cos, sin

    for name, starts, rot in (("64", (0, 64), 16), ("96", (64,), 32)):
        m, cos, sin = rotation(starts, rot)
        c1[:, C1["rot" + name]:][:, :P] = m
        c1[:, C1["cos" + name]:][:, :T1] = cos
        c1[:, C1["sin" + name]:][:, :T1] = sin
    c1[0:64, C1["causal"] + T1 - 64:C1["causal"] + T1] = NEG
    c1[:, C1["rev8"]:][:, :8] = np.arange(8, 0, -1)
    c1[:, C1["rev32"]:][:, :32] = np.arange(32, 0, -1)
    c2 = np.zeros((P, N2), f)
    s, t = np.arange(P)[:, None], np.arange(P)[None, :]
    for l in range(6):
        b = 1 << l
        c2[:, C2["levels"] + l * P:][:, :P] = (s // (2 * b) == t // (2 * b)) & (s // b % 2 == 0) & (t // b % 2 == 1)
    c2[:, C2["level0_low"]:][:, :P] = c2[:, C2["levels"]:][:, :P].T
    c2[:, C2["strict"]:][:, :P] = (s // CH == t // CH) & (s < t)
    c2[:, C2["incl"]:][:, :P] = (s // CH == t // CH) & (s <= t)
    c2[:, C2["resets"]:][:, :T2] = np.arange(T2)[None, :] % CH != 0
    return c0, c1, c2


def blocks(w, width=P, rows=None):
    k, n = w.shape
    kt, nt = -(-k // P), -(-n // width)
    full = np.zeros((kt * P, nt, P), w.dtype)
    padded = np.zeros((kt * P, nt * width), w.dtype)
    padded[:k, :n] = w
    full[:, :, :width] = padded.reshape(kt * P, nt, width)
    b = full.reshape(kt, P, nt, P).transpose(2, 0, 1, 3).reshape(nt * kt, P, P)
    pad = -b.shape[0] % 8
    if pad:
        b = np.concatenate([b, np.zeros((pad, P, P), w.dtype)])
    return b.reshape(-1, 8, P, P).transpose(0, 2, 1, 3).reshape(-1, P, 8 * P)


def rows512(w):
    pad = -w.shape[0] % 256
    w = np.concatenate([w, np.zeros((pad, w.shape[1]), w.dtype)]) if pad else w
    return w.reshape(-1, 2, P, 512).transpose(0, 2, 1, 3).reshape(-1, P, 1024)


def lay_out(a):
    w_in, w2 = a["w_in"][0], a["w_in_2"][0]
    o = np.cumsum([0, QL, KVL, ROPE_D, 512, 512, 512, 512, HD, HEADS, D, D])
    part = [w_in[:, o[i]:o[i + 1]] for i in range(11)]
    c = 2 * D
    s = {"c_q": blocks(part[0]), "c_kv": blocks(part[1]),
         "k_r": blocks(w_in[:, o[2] - 64:o[3]], width=96),
         "q_b": blocks(part[3]), "k_b": blocks(part[4]), "v_b": rows512(part[5]),
         "q_i": blocks(part[6]), "k_i": blocks(np.concatenate([part[7], part[7]], 1)),
         "g_a": blocks(part[9]), "g_b": blocks(part[10]),
         "w_uq": blocks(a["w_uq"][0], width=96), "w_uk": blocks(a["w_uk"][0], width=64),
         "w_uv": rows512(a["w_uv"][0]),
         "w_o_a": blocks(a["w_o_a"][0]), "w_o_b": blocks(a["w_o_b"][0]), "w_out": blocks(a["w_out"][0]),
         "conv_in": blocks(w2[:, :c]).reshape(2, 8, P, 1024).transpose(1, 0, 2, 3).reshape(16, P, 1024),
         "rw_r": blocks(w2[:, c:c + D]), "rw_k": blocks(w2[:, c + D:c + 2 * D]),
         "rw_v": blocks(w2[:, c + 2 * D:c + 3 * D]),
         "rw_wa": blocks(w2[:, c + 3 * D:c + 3 * D + P]),
         "rw_g": blocks(w2[:, c + 3 * D + P:c + 3 * D + P + 160]),
         "gate_a": blocks(w2[:, 5408:5408 + D]), "gate_b": blocks(w2[:, 5408 + D:5408 + 2 * D]),
         "conv_out": blocks(a["w_conv_out_2"][0]),
         "wa_up": np.concatenate([a["w_decay_up_2"][0], a["a_up_2"][0]])[None],
         "g_up": np.concatenate([a["g_up_2"][0], np.zeros((96, D), w2.dtype)]).reshape(2, P, D),
         "rw_out": blocks(a["w_rwkv_out_2"][0]), "w_o2": blocks(a["w_o_2"][0]),
         "ffn_down": blocks(a["ffn_down_2"][0])}
    up = blocks(a["ffn_up_2"][0])
    s["ffn_up"] = up.reshape(2, NF, P, 1024).transpose(1, 0, 2, 3).reshape(2 * NF, P, 1024)
    moe = []
    for e in range(N_EXP):
        g, u = blocks(a["w_gate"][0, e]), blocks(a["w_up"][0, e])
        moe += [g[0:1], u[0:1], g[1:2], u[1:2], blocks(a["w_down"][0, e])]
    s["moe"] = np.concatenate(moe)
    for name, n in SLAB_COUNTS:
        assert s[name].shape == (n, P, 1024), (name, s[name].shape)
    slabs = np.concatenate([s[name] for name, _ in SLAB_COUNTS])

    def col(v):
        v = np.asarray(v).reshape(-1)
        pad = -v.size % P
        v = np.concatenate([v, np.zeros(pad, v.dtype)]) if pad else v
        return v.reshape(-1, P).T

    mu = a["rwkv_mu_2"][0]
    cols = {n: col(a[n]) for n in ("norm_mix_g", "mla_q_norm_g", "mla_kv_norm_g", "norm_ffn_g", "final_norm_g")}
    for n in ("ln_in_g", "ln_in_b", "b_gate", "conv_dw_b", "conv_ln_g", "conv_ln_b", "w0", "a0", "k_k", "k_a",
              "r_k", "lnx_g", "lnx_b", "ln1_g", "ln1_b", "ln2_g", "ln2_b"):
        cols[n] = col(a[n + "_2"])
    cols["mu"] = col(mu)
    cols["conv_dw"] = a["conv_dw_2"][0].reshape(TAPS, 8, P).transpose(2, 1, 0).reshape(P, -1)
    cols["ffn_dw"] = a["ffn_dw_2"][0].reshape(3, 2 * NF, P).transpose(2, 1, 0).reshape(P, -1)
    r = np.concatenate([a["w_router_group"][0], a["w_router_expert"][0]], 1)
    cols["router"] = r.reshape(8, P, 40).transpose(1, 0, 2).reshape(P, -1)
    cols["w_i"] = part[8].reshape(8, P, 8).transpose(1, 0, 2).reshape(P, -1)
    cols["meta"] = a["meta_tokens_2"].reshape(META, 8, P).transpose(2, 1, 0).reshape(P, -1)
    for name, n in PARAM_COLS:
        assert cols[name].shape == (P, n), (name, cols[name].shape)
    params = np.concatenate([cols[name] for name, _ in PARAM_COLS], 1)
    c0, c1, c2 = shape_constants()
    return {
        "x_t": np.ascontiguousarray(a["x"][0].reshape(T1, 8, P).transpose(2, 1, 0)),
        "slabs": slabs, "params": np.ascontiguousarray(params),
        "router_bias": np.concatenate([a["b_router_group"][0], a["b_router_expert"][0]])[None],
        "const0": c0, "const1": c1, "const2": c2,
    }


def halves(t):
    return [(0, t)] if t <= 512 else [(0, t // 2), (t // 2, t)]


def fold(ap, t):
    return ap.rearrange("p (h w) -> p h w", h=len(halves(t)))


def program(nc, x_t, slabs, params_d, router_bias, const0, const1, const2, out):
    top = ExitStack()
    with top:
        count = [0]

        def sem(name):
            count[0] += 1
            return top.enter_context(nc.semaphore(name))

        def sbt(ctx, name, shape):
            return ctx.enter_context(nc.sbuf_tensor(name, shape, F32))

        def block():
            return nc.Block(no_gpsimd_drain=True)

        comb_d = nc.dram_tensor("combine_rows", [N_EXP, T1], F32, kind="Internal").ap()
        h_d = nc.dram_tensor("h_spill", [P, KD, T2], F32, kind="Internal").ap()
        y_d = nc.dram_tensor("y_spill", [P, KD, T2], F32, kind="Internal").ap()

        acc = [top.enter_context(nc.psum_tensor(f"acc{j}", [P, 2, 512], F32)) for j in range(4)]
        ring = [sbt(top, f"ring{j}", [P, 1024]) for j in range(RING)]
        par = sbt(top, "par", [P, N_PARAMS])
        c0 = sbt(top, "c0", [P, N0])
        slab_in = [sem(f"slab_in{j}") for j in range(RING)]
        slab_used = sem("slab_used")
        chains = {e: [sem(f"{e}_chain"), 0] for e in ("dve", "act", "pool")}

        def link(e, eng, ins):
            c = chains[e]
            c[1] += 1
            ins.then_inc(c[0], 1)
            eng.wait_ge(c[0], c[1])

        def k0(name, n=P, at=0):
            return c0[:, C0[name] + at:C0[name] + at + n]

        def pcol(name, k, rows=P):
            return par[0:rows, PCOL[name] + k:PCOL[name] + k + 1]

        def A(j, t, rows=P, r0=0):
            n = len(halves(t))
            return acc[j][r0:r0 + rows, 0:n, 0:t // n]

        issued, used = [0], [0]
        freed_by = {}

        def slab_done(mm, n):
            used[0] += 1
            freed_by[n] = (slab_used, used[0])
            mm.then_inc(slab_used, 1)


        def load_slabs(sp, name=None):
            if name is None:
                stop = RING
            else:
                i = [n for n, _ in SLAB_COUNTS].index(name)
                stop = min(SLAB0[name] + SLAB_COUNTS[i][1] + RING, N_SLABS)
            for n in range(issued[0], stop):
                if n >= RING:
                    sp.wait_ge(*freed_by[n - RING])
                sp.dma_start(ring[n % RING][:, :], slabs[n]).then_inc(slab_in[n % RING], 16)
            issued[0] = stop

        def slab_wait(pe, n):
            pe.wait_ge(slab_in[n % RING], 16 * (n // RING + 1))

        def pe_tiles(pe, name, kt, nt, rhs, t, ready, freed, rows=P, acc0=0, na=4, first=0, krows=None):
            n_blocks = nt * kt
            for i in range(nt):
                j = acc0 + (first + i) % na
                if first + i >= na:
                    pe.wait_ge(freed, first + i - na + 1)
                for k in range(kt):
                    b = i * kt + k
                    n, at = SLAB0[name] + b // 8, b % 8 * P
                    if b % 8 == 0:
                        slab_wait(pe, n)
                    kr = P if krows is None else krows(k)
                    for s, (lo, hi) in enumerate(halves(t)):
                        mm = nc.tensor.matmul(acc[j][0:rows, s, 0:hi - lo], ring[n % RING][0:kr, at:at + rows],
                                              rhs(k)[0:kr, lo:hi], start=(k == 0), stop=(k == kt - 1))
                    last = b % 8 == 7 or b == n_blocks - 1
                    if k == kt - 1:
                        mm.then_inc(ready, 1)
                        if last:
                            freed_by[n] = (ready, first + i + 1)
                    elif last:
                        slab_done(mm, n)

        norm_sems = [sem("norm_" + n) for n in ("summed", "centred", "squared", "sq_used", "rooted", "scaled")]
        norm_base = [0] * len(norm_sems)

        def normalize(tag, src, dst, kt, t, mean, gain, bias=None, eps=EPS_RMS, func=None):
            centre = bias is not None
            summed, centred, squared, sq_used, rooted, scaled = norm_sems
            b_ = {id(s): norm_base[i] for i, s in enumerate(norm_sems)}
            for i, n in enumerate((1, kt, kt, kt, 1, kt)):
                norm_base[i] += n if centre or norm_sems[i] not in (summed, centred, scaled) else 0
            wait = lambda eng, s, n: eng.wait_ge(s, b_[id(s)] + n)
            with ExitStack() as ctx:
                sq = [sbt(ctx, f"{tag}_sq{i}", [P, t]) for i in range(4)]
                std = sbt(ctx, tag + "_std", [P, t])
                rstd = sbt(ctx, tag + "_rstd", [P, t])
                with block() as b:
                    @b.tensor
                    def _(pe):
                        if centre:
                            for k in range(kt):
                                for s, (lo, hi) in enumerate(halves(t)):
                                    mm = nc.tensor.matmul(acc[0][:, s, 0:hi - lo], mean, src(k)[:, lo:hi],
                                                          start=(k == 0), stop=(k == kt - 1))
                            mm.then_inc(summed, 1)
                        for k in range(kt):
                            wait(pe, squared, k + 1)
                            for s, (lo, hi) in enumerate(halves(t)):
                                mm = nc.tensor.matmul(acc[1][:, s, 0:hi - lo], mean, sq[k % 4][:, lo:hi],
                                                      start=(k == 0), stop=(k == kt - 1))
                            mm.then_inc(sq_used, 1)

                    @b.scalar
                    def _(act):
                        for k in range(kt):
                            if centre:
                                wait(act, centred, k + 1)
                            if k >= 4:
                                wait(act, sq_used, k - 3)
                            nc.scalar.activation(sq[k % 4][:, :], (dst if centre else src)(k),
                                                 ACT.Square).then_inc(squared, 1)
                        wait(act, sq_used, kt)
                        nc.scalar.activation(fold(std[:, :], t), A(1, t), ACT.Sqrt,
                                             bias=k0("eps", 1, eps)).then_inc(rooted, 1)
                        if centre:
                            for k in range(kt):
                                wait(act, scaled, k + 1)
                                nc.scalar.activation(dst(k), dst(k), func or ACT.Identity, scale=gain(k),
                                                     bias=bias(k))

                    @b.vector
                    def _(dve):
                        if centre:
                            wait(dve, summed, 1)
                            for k in range(kt):
                                nc.vector.tensor_tensor(fold(dst(k), t), fold(src(k), t), A(0, t),
                                                        ALU.subtract).then_inc(centred, 1)
                        wait(dve, rooted, 1)
                        link("dve", dve, nc.vector.reciprocal(rstd[:, :], std[:, :]))
                        if centre:
                            wait(dve, centred, kt)
                            wait(dve, squared, kt)
                            for k in range(kt):
                                nc.vector.tensor_tensor(dst(k), dst(k), rstd[:, :], ALU.mult).then_inc(scaled, 1)
                        else:
                            for k in range(kt):
                                nc.vector.scalar_tensor_tensor(out=dst(k), in0=src(k), scalar=gain(k),
                                                               in1=rstd[:, :], op0=ALU.mult, op1=ALU.mult)

        loaded = sem("inputs_loaded")

        def first_block(b1, xt):
            with ExitStack() as c1x:
                c1 = sbt(c1x, "c1", [P, N1])

                def k1(name, n=P, at=0):
                    return c1[:, C1[name] + at:C1[name] + at + n]

                h = sbt(c1x, "h", [P, KD, T1])

                with block() as b:
                    @b.sync
                    def _(sp):
                        sp.dma_start(xt[:, :, :], x_t).then_inc(loaded, 16)
                        sp.dma_start(c0[:, :], const0).then_inc(loaded, 16)
                        sp.dma_start(par[:, :], params_d).then_inc(loaded, 16)
                        sp.dma_start(c1[:, :], const1).then_inc(loaded, 16)
                        load_slabs(sp)
                        sp.wait_ge(loaded, 64)
                normalize("mix", lambda k: xt[:, k, :], lambda k: h[:, k, :], KD, T1, k0("mean1024"),
                          lambda k: pcol("norm_mix_g", k))
                with ExitStack() as att:
                    attention_part(att, xt, h, k1)
                normalize("ffn", lambda k: xt[:, k, :], lambda k: h[:, k, :], KD, T1, k0("mean1024"),
                          lambda k: pcol("norm_ffn_g", k))
                route(h, k1)
                experts(xt, h)
            x2 = sbt(b1, "x2", [P, KD, T2])
            normalize("final", lambda k: xt[:, k, :], lambda k: x2[:, k, META:T2], KD, T1, k0("mean1024"),
                      lambda k: pcol("final_norm_g", k))
            return x2

        def attention_part(att, xt, h, k1):
            qb, kb = sbt(att, "qb", [P, 4, T1]), sbt(att, "kb", [P, 4, T1])
            qi, ki = sbt(att, "qi", [P, 4, T1]), sbt(att, "ki", [P, T1])
            vb, va = sbt(att, "vb", [P, 4, 512]), sbt(att, "va", [P, 4, 512])
            wi = sbt(att, "wi", [P, 4, HEADS])
            ga, gb = sbt(att, "ga", [P, KD, T1]), sbt(att, "gb", [P, KD, T1])
            cc = sbt(att, "cc", [P, 5, T1])
            kr = sbt(att, "kr", [P, T1])
            qa, ka = sbt(att, "qa", [P, HEADS, T1]), sbt(att, "ka", [P, HEADS, T1])
            sel = [None] + [sbt(att, f"sel{i}", [P, (i + 1) * P]) for i in range(1, 4)]
            dests = ([("c_q", cc[:, i, :], None) for i in range(3)] + [("c_kv", cc[:, 3 + i, :], None) for i in range(2)]
                     + [("q_b", qb[:, i, :], None) for i in range(4)] + [("k_b", kb[:, i, :], None) for i in range(4)]
                     + [("q_i", qi[:, i, :], None) for i in range(4)] + [("k_i", ki[:, :], None)]
                     + [("k_r", kr[0:96, :], None)]
                     + [("g_a", ga[:, i, :], ACT.Sigmoid) for i in range(8)]
                     + [("g_b", gb[:, i, :], ACT.Sigmoid) for i in range(8)])
            tile_ready, tile_out = sem("in_ready"), sem("in_out")
            v_ready, v_out = sem("vb_ready"), sem("vb_out")
            with block() as b:
                @b.tensor
                def _(pe):
                    i = 0
                    for name, n in SLAB_COUNTS[:9]:
                        pe_tiles(pe, name, KD, n, lambda k: h[:, k, :], T1, tile_ready, tile_out,
                                 rows=96 if name == "k_r" else P, first=i)
                        i += n
                    pe.wait_ge(tile_out, i)
                    for k in range(KD):
                        n = SLAB0["v_b"] + k // 2
                        if k % 2 == 0:
                            slab_wait(pe, n)
                        for tok in range(4):
                            mm = nc.tensor.matmul(acc[tok][:, 0, :], h[:, k, tok * P:(tok + 1) * P],
                                                  ring[n % RING][:, k % 2 * 512:k % 2 * 512 + 512],
                                                  start=(k == 0), stop=(k == KD - 1))
                        if k % 2:
                            slab_done(mm, n)
                    for tok in range(4):
                        for k in range(KD):
                            o = PCOL["w_i"] + 8 * k
                            mm = nc.tensor.matmul(acc[tok][:, 1, 0:8], h[:, k, tok * P:(tok + 1) * P],
                                                  par[:, o:o + 8], start=(k == 0), stop=(k == KD - 1))
                        mm.then_inc(v_ready, 1)

                @b.scalar
                def _(act):
                    for i, (name, d, f) in enumerate(dests):
                        act.wait_ge(tile_ready, i + 1)
                        rows = 96 if name == "k_r" else P
                        nc.scalar.activation(d, acc[i % 4][0:rows, 0, :], f or ACT.Copy).then_inc(tile_out, 1)
                    for tok in range(4):
                        act.wait_ge(v_ready, tok + 1)
                        nc.scalar.activation(vb[:, tok, :], acc[tok][:, 0, :], ACT.Copy)
                        nc.scalar.activation(wi[:, tok, :], acc[tok][:, 1, 0:8], ACT.Copy, scale=HEADS ** -0.5)

                @b.sync
                def _(sp):
                    load_slabs(sp, "v_b")

            normalize("cq", lambda k: cc[:, k, :], lambda k: cc[:, k, :], 3, T1, k1("mean384"),
                      lambda k: pcol("mla_q_norm_g", k))
            normalize("ckv", lambda k: cc[:, 3 + k, :], lambda k: cc[:, 3 + k, :], 2, T1, k1("mean256"),
                      lambda k: pcol("mla_kv_norm_g", k))
            up_ready, up_out, va_ready = sem("up_ready"), sem("up_out"), sem("va_ready")
            with block() as b:
                @b.tensor
                def _(pe):
                    pe_tiles(pe, "w_uq", 3, HEADS, lambda k: cc[:, k, :], T1, up_ready, up_out, rows=96)
                    pe_tiles(pe, "w_uk", 2, HEADS, lambda k: cc[:, 3 + k, :], T1, up_ready, up_out, rows=64, first=8)
                    pe.wait_ge(up_out, 16)
                    n = SLAB0["w_uv"]
                    slab_wait(pe, n)
                    for tok in range(4):
                        for k in range(2):
                            mm = nc.tensor.matmul(acc[tok][:, 0, :], cc[:, 3 + k, tok * P:(tok + 1) * P],
                                                  ring[n % RING][:, k * 512:k * 512 + 512],
                                                  start=(k == 0), stop=(k == 1))
                        mm.then_inc(va_ready, 1)
                    freed_by[n] = (va_ready, 4)

                @b.scalar
                def _(act):
                    for i in range(16):
                        act.wait_ge(up_ready, i + 1)
                        d, rows = (qa, 96) if i < 8 else (ka, 64)
                        nc.scalar.activation(d[0:rows, i % 8, :], acc[i % 4][0:rows, 0, :], ACT.Copy).then_inc(up_out, 1)
                    for tok in range(4):
                        act.wait_ge(va_ready, tok + 1)
                        nc.scalar.activation(va[:, tok, :], acc[tok][:, 0, :], ACT.Copy)

                @b.sync
                def _(sp):
                    load_slabs(sp, "w_uv")

            rope_tiles = ([(qb[:, i, :], 0) for i in range(4)] + [(kb[:, i, :], 0) for i in range(4)]
                          + [(qi[:, i, :], 0) for i in range(4)] + [(ki[:, :], 0)]
                          + [(kr[0:96, :], 1)] + [(qa[0:96, i, :], 1) for i in range(8)])
            turned, cosed, sined, roped = sem("turned"), sem("cosed"), sem("sined"), sem("roped")
            with ExitStack() as rx, block() as b:
                prod = [sbt(rx, f"rope_prod{i}", [P, T1]) for i in range(2)]

                @b.tensor
                def _(pe):
                    for i, (x, kind) in enumerate(rope_tiles):
                        rows = 96 if kind else P
                        if i >= 4:
                            pe.wait_ge(sined, i - 3)
                        rot = k1("rot96" if kind else "rot64")
                        nc.tensor.matmul(acc[i % 4][0:rows, 0, :], rot[0:rows, 0:rows], x, start=True,
                                         stop=True).then_inc(turned, 1)

                @b.vector
                def _(dve):
                    for i, (x, kind) in enumerate(rope_tiles):
                        rows = 96 if kind else P
                        dve.wait_ge(turned, i + 1)
                        if i >= 2:
                            dve.wait_ge(roped, i - 1)
                        nc.vector.tensor_tensor(prod[i % 2][0:rows, :], acc[i % 4][0:rows, 0, :],
                                                k1("sin96" if kind else "sin64", T1)[0:rows, :],
                                                ALU.mult).then_inc(sined, 1)
                        nc.vector.tensor_tensor(x, x, k1("cos96" if kind else "cos64", T1)[0:rows, :],
                                                ALU.mult).then_inc(cosed, 1)

                @b.gpsimd
                def _(pool):
                    for i, (x, kind) in enumerate(rope_tiles):
                        rows = 96 if kind else P
                        pool.wait_ge(sined, i + 1)
                        pool.wait_ge(cosed, i + 1)
                        nc.gpsimd.tensor_tensor(x, x, prod[i % 2][0:rows, :], ALU.add).then_inc(roped, 1)
                    pool.wait_ge(roped, len(rope_tiles))
                    for hd in range(HEADS):
                        link("pool", pool, nc.gpsimd.tensor_copy(ka[64:96, hd, :], kr[64:96, :]))

            logit_ready, logit_out, rel_used = sem("logit_ready"), sem("logit_out"), sem("rel_used")
            score_seen = sem("score_seen")
            with ExitStack() as ix, block() as b:
                rel = [sbt(ix, f"rel{i}", [P, T1]) for i in range(4)]
                best = sbt(ix, "best", [P, 8])
                units = [(qt, hd) for qt in range(1, 4) for hd in range(HEADS)]

                @b.tensor
                def _(pe):
                    for u, (qt, hd) in enumerate(units):
                        nk, r0 = (qt + 1) * P, 64 * (hd % 2)
                        if u >= 4:
                            pe.wait_ge(logit_out, u - 3)
                        nc.tensor.matmul(acc[u % 4][:, 0, 0:nk], qi[r0:r0 + 64, hd // 2, qt * P:(qt + 1) * P],
                                         ki[r0:r0 + 64, 0:nk], start=True, stop=True).then_inc(logit_ready, 1)

                @b.scalar
                def _(act):
                    for u, (qt, hd) in enumerate(units):
                        nk = (qt + 1) * P
                        act.wait_ge(logit_ready, u + 1)
                        if u >= 4:
                            act.wait_ge(rel_used, u - 3)
                        nc.scalar.activation(rel[u % 4][:, 0:nk], acc[u % 4][:, 0, 0:nk], ACT.Relu,
                                             scale=HD ** -0.5).then_inc(logit_out, 1)

                @b.vector
                def _(dve):
                    for u, (qt, hd) in enumerate(units):
                        nk, s = (qt + 1) * P, sel[qt]
                        dve.wait_ge(logit_out, u + 1)
                        w = wi[:, qt, hd:hd + 1]
                        if hd == 0:
                            ins = nc.vector.tensor_scalar(s[:, :], rel[u % 4][:, 0:nk], w, None, ALU.mult)
                        else:
                            dve.wait_ge(rel_used, u)
                            ins = nc.vector.scalar_tensor_tensor(out=s[:, :], in0=rel[u % 4][:, 0:nk], scalar=w,
                                                                 in1=s[:, :], op0=ALU.mult, op1=ALU.add)
                        ins.then_inc(rel_used, 1)
                        if hd < HEADS - 1:
                            continue
                        dve.wait_ge(rel_used, u + 1)
                        link("dve", dve, nc.vector.memset(s[0:64, nk - 64:nk], NEG))
                        for _r in range(TOPK // 8):
                            link("dve", dve, nc.vector.max(best[:, :], s[:, :]))
                            link("dve", dve, nc.vector.match_replace(s[:, :], best[:, :], s[:, :], TAKEN))
                        link("dve", dve, nc.vector.tensor_scalar(s[:, :], s[:, :], TAKEN / 2, NEG, ALU.is_gt, ALU.mult))

            oa, ob = cc, qi
            causal = lambda qt: k1("causal", (qt + 1) * P, T1 - (qt + 1) * P)
            attend("mla", lambda hd, lo, hi: qa[0:96, hd, lo:hi], lambda hd, n: ka[0:96, hd, 0:n], va,
                   causal, (NOPE + ROPE_D) ** -0.5, oa)
            attend("dsa", lambda hd, lo, hi: qb[64 * (hd % 2):64 * (hd % 2) + 64, hd // 2, lo:hi],
                   lambda hd, n: kb[64 * (hd % 2):64 * (hd % 2) + 64, hd // 2, 0:n], vb,
                   lambda qt: sel[qt][:, :] if qt else causal(0), HD ** -0.5, ob)
            oy_ready, oy_out, y_sum = sem("oy_ready"), sem("oy_out"), sem("y_sum")
            with block() as b:
                @b.tensor
                def _(pe):
                    pe_tiles(pe, "w_o_a", 4, KD, lambda k: oa[:, k, :], T1, oy_ready, oy_out)
                    pe_tiles(pe, "w_o_b", 4, KD, lambda k: ob[:, k, :], T1, oy_ready, oy_out, first=8)

                @b.vector
                def _(dve):
                    for i in range(16):
                        dve.wait_ge(oy_ready, i + 1)
                        d, g = (h, ga) if i < 8 else (gb, gb)
                        nc.vector.tensor_tensor(d[:, i % 8, :], acc[i % 4][:, 0, :], g[:, i % 8, :],
                                                ALU.mult).then_inc(oy_out, 1)

                @b.gpsimd
                def _(pool):
                    for i in range(8):
                        pool.wait_ge(oy_out, 9 + i)
                        link("pool", pool, nc.gpsimd.tensor_tensor(h[:, i, :], h[:, i, :], gb[:, i, :], ALU.add))

                @b.sync
                def _(sp):
                    load_slabs(sp, "w_o_b")
            xo_ready, xo_out = sem("xo_ready"), sem("xo_out")
            with block() as b:
                @b.tensor
                def _(pe):
                    pe_tiles(pe, "w_out", KD, KD, lambda k: h[:, k, :], T1, xo_ready, xo_out)

                @b.vector
                def _(dve):
                    for i in range(8):
                        dve.wait_ge(xo_ready, i + 1)
                        nc.vector.tensor_tensor(xt[:, i, :], xt[:, i, :], acc[i % 4][:, 0, :],
                                                ALU.add).then_inc(xo_out, 1)

                @b.sync
                def _(sp):
                    load_slabs(sp, "w_out")

        attend_sems = [sem("att_" + n) for n in ("s_ready", "s_out", "probs", "scaled", "pt_ready", "pt_out", "o_ready", "o_out")]
        attend_base = [0]

        def attend(tag, q, key, v, bias, scale, o):
            s_ready, s_out, probs, scaled, pt_ready, pt_out, o_ready, o_out = attend_sems
            u0 = attend_base[0]
            attend_base[0] += 4 * HEADS
            units = [(qt, hd) for qt in range(4) for hd in range(HEADS)]
            NU = len(units)
            NS = 4
            with ExitStack() as ax, block() as b:
                sc = [sbt(ax, f"{tag}_sc{i}", [P, T1]) for i in range(NS)]
                pt = [sbt(ax, f"{tag}_pt{i}", [P, T1]) for i in range(2)]
                mx = sbt(ax, f"{tag}_mx", [P, NU])
                nm = sbt(ax, f"{tag}_nm", [P, NU])
                rs = sbt(ax, f"{tag}_rs", [P, NU])
                ri = sbt(ax, f"{tag}_ri", [P, NU])
                sbank = lambda u: acc[u % 4 // 2][:, u % 2, :]

                @b.tensor
                def _(pe):
                    def scores(u):
                        qt, hd = units[u]
                        if u >= 4:
                            pe.wait_ge(s_out, u0 + u - 3)
                        nc.tensor.matmul(sbank(u)[:, 0:(qt + 1) * P], q(hd, qt * P, (qt + 1) * P),
                                         key(hd, (qt + 1) * P), start=True, stop=True).then_inc(s_ready, 1)

                    def turn(u):
                        qt, hd = units[u]
                        pe.wait_ge(scaled, u0 + u + 1)
                        if u >= 2:
                            pe.wait_ge(pt_out, u0 + u - 1)
                        for kt in range(qt + 1):
                            mm = nc.tensor.transpose(acc[2][:, u % 2, kt * P:(kt + 1) * P],
                                                     sc[u % NS][:, kt * P:(kt + 1) * P], k0("ident"))
                        mm.then_inc(pt_ready, 1)

                    def values(u):
                        qt, hd = units[u]
                        r0 = 64 * (hd % 2)
                        pe.wait_ge(pt_out, u0 + u + 1)
                        if u >= 2:
                            pe.wait_ge(o_out, u0 + u - 1)
                        for kt in range(qt + 1):
                            mm = nc.tensor.matmul(acc[3][r0:r0 + 64, u % 2, 0:P], v[:, kt, hd * 64:hd * 64 + 64],
                                                  pt[u % 2][:, kt * P:(kt + 1) * P], start=(kt == 0), stop=(kt == qt))
                        mm.then_inc(o_ready, 1)

                    scores(0)
                    scores(1)
                    for u in range(NU + 1):
                        if u + 2 < NU:
                            scores(u + 2)
                        if u < NU:
                            turn(u)
                        if u >= 1:
                            values(u - 1)

                @b.vector
                def _(dve):
                    def add_bias(u):
                        nk = (units[u][0] + 1) * P
                        dve.wait_ge(s_ready, u0 + u + 1)
                        if u >= NS:
                            dve.wait_ge(pt_ready, u0 + u - NS + 1)
                        nc.vector.tensor_tensor_reduce(sc[u % NS][:, 0:nk], sbank(u)[:, 0:nk], bias(units[u][0]),
                                                       1.0, -3e38, ALU.add, ALU.max, mx[:, u:u + 1]).then_inc(s_out, 1)

                    def normal(u):
                        nk = (units[u][0] + 1) * P
                        dve.wait_ge(probs, u0 + u + 1)
                        link("dve", dve, nc.vector.reciprocal(ri[:, u:u + 1], rs[:, u:u + 1]))
                        nc.vector.tensor_scalar(sc[u % NS][:, 0:nk], sc[u % NS][:, 0:nk], ri[:, u:u + 1], None,
                                                ALU.mult).then_inc(scaled, 1)

                    add_bias(0)
                    for u in range(NU):
                        if u + 1 < NU:
                            add_bias(u + 1)
                        normal(u)

                @b.scalar
                def _(act):
                    def exps(u):
                        nk = (units[u][0] + 1) * P
                        act.wait_ge(s_out, u0 + u + 1)
                        link("act", act, nc.scalar.activation(nm[:, u:u + 1], mx[:, u:u + 1], ACT.Copy, scale=-scale))
                        nc.scalar.activation(sc[u % NS][:, 0:nk], sc[u % NS][:, 0:nk], ACT.Exp, bias=nm[:, u:u + 1],
                                             scale=scale, accum_out=rs[:, u:u + 1]).then_inc(probs, 1)

                    def evacuate(u):
                        nk = (units[u][0] + 1) * P
                        act.wait_ge(pt_ready, u0 + u + 1)
                        if u >= 2:
                            act.wait_ge(o_ready, u0 + u - 1)
                        nc.scalar.activation(pt[u % 2][:, 0:nk], acc[2][:, u % 2, 0:nk], ACT.Copy).then_inc(pt_out, 1)

                    def store(u):
                        qt, hd = units[u]
                        r0 = 64 * (hd % 2)
                        act.wait_ge(o_ready, u0 + u + 1)
                        nc.scalar.activation(o[r0:r0 + 64, hd // 2, qt * P:(qt + 1) * P], acc[3][r0:r0 + 64, u % 2, 0:P],
                                             ACT.Copy).then_inc(o_out, 1)

                    exps(0)
                    for u in range(NU + 1):
                        if u + 1 < NU:
                            exps(u + 1)
                        if u < NU:
                            evacuate(u)
                        if u >= 1:
                            store(u - 1)

        def route(h, k1):
            logits_ready, biased = sem("rt_logits"), sem("rt_biased")
            shifted, exped, paired, exped2 = sem("rt_shifted"), sem("rt_exped"), sem("rt_paired"), sem("rt_exped2")
            combined, turned, copied, stored = sem("rt_combined"), sem("rt_turned"), sem("rt_copied"), sem("rt_stored")
            with ExitStack() as rx, block() as b:
                rb = sbt(rx, "rt_bias", [P, 40])
                lg = sbt(rx, "rt_lg", [P, 4, 40])
                df, e1 = sbt(rx, "rt_df", [P, 4, 8]), sbt(rx, "rt_e1", [P, 4, 8])
                g8, h8 = sbt(rx, "rt_g8", [P, 4, 8]), sbt(rx, "rt_h8", [P, 4, 8])
                m32 = sbt(rx, "rt_m32", [P, 4, 32])
                t32, a32, b32 = (sbt(rx, f"rt_{n}32", [P, 4, 32]) for n in "tab")
                small = sbt(rx, "rt_small", [P, 10, 4])
                ct = sbt(rx, "rt_ct", [32, T1])

                def bc(i, n):
                    return small[:, i, :].unsqueeze(2).to_broadcast([P, 4, n])

                @b.sync
                def _(sp):
                    sp.dma_start(rb[:, :], router_bias.to_broadcast([P, 40])).then_inc(biased, 16)
                    sp.wait_ge(copied, 1)
                    sp.dma_start(comb_d, ct[:, :]).then_inc(stored, 16)
                    sp.wait_ge(stored, 16)

                @b.tensor
                def _(pe):
                    for tok in range(4):
                        for k in range(KD):
                            o = PCOL["router"] + 40 * k
                            mm = nc.tensor.matmul(acc[tok][:, 0, 0:40], h[:, k, tok * P:(tok + 1) * P],
                                                  par[:, o:o + 40], start=(k == 0), stop=(k == KD - 1))
                        mm.then_inc(logits_ready, 1)
                    pe.wait_ge(combined, 1)
                    for tok in range(4):
                        mm = nc.tensor.transpose(acc[0][0:32, 1, tok * P:(tok + 1) * P], m32[:, tok, :], k0("ident"))
                    mm.then_inc(turned, 1)

                @b.vector
                def _(dve):
                    v = nc.vector
                    L = lambda ins: link("dve", dve, ins)
                    dve.wait_ge(biased, 16)
                    for tok in range(4):
                        dve.wait_ge(logits_ready, tok + 1)
                        ins = v.tensor_tensor(lg[:, tok, :], acc[tok][:, 0, 0:40], rb[:, :], ALU.add)
                        if tok < 3:
                            link("dve", dve, ins)
                    L(ins)
                    G, E = lg[:, :, 0:8], lg[:, :, 8:40]
                    row = lambda i: small[:, i, :]

                    def first_best(x, top, n, rev, tmp, hot):
                        L(v.tensor_reduce(row(top), x, AX, ALU.max))
                        L(v.tensor_tensor(tmp, x, bc(top, n), ALU.is_equal))
                        L(v.tensor_tensor(tmp, tmp, rev.unsqueeze(1).to_broadcast([P, 4, n]), ALU.mult))
                        L(v.tensor_reduce(row(9), tmp, AX, ALU.max))
                        L(v.tensor_tensor(hot, tmp, bc(9, n), ALU.is_equal))

                    first_best(G, 0, 8, k1("rev8", 8), g8[:, :, :], h8[:, :, :])
                    v.tensor_tensor(df[:, :, :], G, bc(0, 8), ALU.subtract).then_inc(shifted, 1)
                    L(v.tensor_scalar(g8[:, :, :], h8[:, :, :], -NEG, NEG, ALU.mult, ALU.add))
                    for tok in range(4):
                        L(v.tensor_tensor(m32[:, tok, :].rearrange("p (g e) -> p g e", g=8),
                                          lg[:, tok, 8:40].rearrange("p (g e) -> p g e", g=8),
                                          g8[:, tok, :].unsqueeze(2).to_broadcast([P, 8, 4]), ALU.add))
                    first_best(m32[:, :, :], 1, 32, k1("rev32", 32), t32[:, :, :], a32[:, :, :])
                    L(v.tensor_scalar(t32[:, :, :], a32[:, :, :], 2 * NEG, None, ALU.mult))
                    L(v.tensor_tensor(m32[:, :, :], m32[:, :, :], t32[:, :, :], ALU.add))
                    first_best(m32[:, :, :], 2, 32, k1("rev32", 32), t32[:, :, :], b32[:, :, :])
                    v.tensor_tensor(row(3), row(2), row(1), ALU.subtract).then_inc(paired, 1)
                    dve.wait_ge(exped, 1)
                    L(v.tensor_reduce(row(4), e1[:, :, :], AX, ALU.add))
                    L(v.reciprocal(row(4), row(4)))
                    dve.wait_ge(exped2, 1)
                    L(v.tensor_scalar(row(6), row(5), 1.0, None, ALU.add))
                    L(v.reciprocal(row(6), row(6)))
                    L(v.tensor_tensor(row(6), row(6), row(4), ALU.mult))
                    L(v.tensor_tensor(row(7), row(6), row(5), ALU.mult))
                    L(v.tensor_tensor(a32[:, :, :], a32[:, :, :], bc(6, 32), ALU.mult))
                    L(v.tensor_tensor(b32[:, :, :], b32[:, :, :], bc(7, 32), ALU.mult))
                    v.tensor_tensor(m32[:, :, :], a32[:, :, :], b32[:, :, :], ALU.add).then_inc(combined, 1)

                @b.scalar
                def _(act):
                    act.wait_ge(shifted, 1)
                    nc.scalar.activation(e1[:, :, :], df[:, :, :], ACT.Exp).then_inc(exped, 1)
                    act.wait_ge(paired, 1)
                    nc.scalar.activation(small[:, 5, :], small[:, 3, :], ACT.Exp).then_inc(exped2, 1)
                    act.wait_ge(turned, 1)
                    nc.scalar.activation(ct[:, :], acc[0][0:32, 1, :], ACT.Copy).then_inc(copied, 1)

        def experts(xt, h):
            gu_ready, silued, hid_out = sem("gu_ready"), sem("silued"), sem("hid_out")
            dn_ready, dn_out, comb_used = sem("dn_ready"), sem("dn_out"), sem("comb_used")
            comb_in = [sem(f"comb_in{j}") for j in range(2)]
            s0 = SLAB0["moe"]
            i0 = issued[0]
            assert i0 == s0 + RING
            turns = N_EXP // 2
            with ExitStack() as ex, block() as b:
                cb = [sbt(ex, f"comb{i}", [P, T1]) for i in range(2)]
                sl = [sbt(ex, f"silu{i}", [P, T1]) for i in range(2)]
                hid = [sbt(ex, f"hid{i}", [P, T1]) for i in range(4)]

                @b.sync
                def _(sp):
                    with sp.Fori(0, turns) as i:
                        for s in range(12):
                            n = i0 + s
                            j, r = s // 6, s % 6
                            if r < 4:
                                sp.wait_ge(gu_ready, i * 8 + 4 * j + r + 1)
                            else:
                                sp.wait_ge(dn_ready, i * 16 + 8 * j + 4 * (r - 4) + 4)
                            sp.dma_start(ring[n % RING][:, :], slabs[bass.ds(i * 12 + n, 1)].rearrange("a p n -> (a p) n"))\
                              .then_inc(slab_in[n % RING], 16)
                issued[0] = i0 + 12 * turns
                for s in range(12):
                    j, r = s // 6, s % 6
                    freed_by[s0 + 12 * (turns - 1) + s] = (
                        (gu_ready, 8 * (turns - 1) + 4 * j + r + 1) if r < 4 else
                        (dn_ready, 16 * (turns - 1) + 8 * j + 4 * (r - 4) + 4))

                @b.gpsimd
                def _(pool):
                    def weigh(i, j, e):
                        pool.wait_ge(comb_in[j], i * 16 + 16)
                        for f in range(2):
                            pool.wait_ge(silued, e * 2 + f + 1)
                            nc.gpsimd.tensor_tensor(sl[f][:, :], sl[f][:, :], cb[j][:, :], ALU.mult).then_inc(comb_used, 1)

                    pool.dma_start(cb[0][:, :], comb_d[0:1, :].to_broadcast([P, T1])).then_inc(comb_in[0], 16)
                    pool.dma_start(cb[1][:, :], comb_d[1:2, :].to_broadcast([P, T1])).then_inc(comb_in[1], 16)
                    with pool.Fori(0, turns - 1) as i:
                        for j in range(2):
                            weigh(i, j, i * 2 + j)
                            pool.wait_ge(comb_used, i * 4 + 2 * j + 2)
                            pool.dma_start(cb[j][:, :], comb_d[bass.ds(i * 2 + j + 2, 1), :].to_broadcast([P, T1]))\
                                .then_inc(comb_in[j], 16)
                    for j in range(2):
                        weigh(turns - 1, j, 2 * (turns - 1) + j)

                @b.tensor
                def _(pe):
                    def slab(i, s):
                        n = s0 + s
                        pe.wait_ge(slab_in[n % RING], i * 48 + 16 * (n // RING + 1))
                        return ring[n % RING]

                    def expert(i, j, peeled):
                        s = 6 * j
                        for f in range(2):
                            if not (peeled and j == 0):
                                pe.wait_ge(hid_out, i * 4 + 2 * j - 1 + f)
                            for g in range(2):
                                w = slab(i, s)
                                for k in range(KD):
                                    mm = nc.tensor.matmul(acc[f][:, g, :], w[:, k * P:(k + 1) * P], h[:, k, :],
                                                          start=(k == 0), stop=(k == KD - 1))
                                mm.then_inc(gu_ready, 1)
                                s += 1
                        for q in range(2):
                            w = slab(i, s)
                            if not (peeled and j == 0 and q == 0):
                                pe.wait_ge(dn_out, i * 16 + 8 * j + 4 * q)
                            for f in range(2):
                                if q == 0:
                                    pe.wait_ge(hid_out, i * 4 + 2 * j + f + 1)
                                for t in range(4):
                                    mm = nc.tensor.matmul(acc[2 + t // 2][:, t % 2, :],
                                                          w[:, (2 * t + f) * P:(2 * t + f + 1) * P],
                                                          hid[2 * j + f][:, :], start=(f == 0), stop=(f == 1))
                                    if f == 1:
                                        mm.then_inc(dn_ready, 1)
                            s += 1

                    expert(0, 0, True)
                    expert(0, 1, True)
                    with pe.Fori(1, turns) as i:
                        expert(i, 0, False)
                        expert(i, 1, False)

                @b.scalar
                def _(act):
                    def expert(i, j, peeled):
                        for f in range(2):
                            act.wait_ge(gu_ready, i * 8 + 4 * j + 2 * f + 1)
                            if not (peeled and j == 0):
                                act.wait_ge(hid_out, i * 4 + 2 * j + f - 1)
                            nc.scalar.activation(sl[f][:, :], acc[f][:, 0, :], ACT.Silu).then_inc(silued, 1)

                    expert(0, 0, True)
                    expert(0, 1, True)
                    with act.Fori(1, turns) as i:
                        expert(i, 0, False)
                        expert(i, 1, False)

                @b.vector
                def _(dve):
                    def expert(i, j):
                        for f in range(2):
                            dve.wait_ge(gu_ready, i * 8 + 4 * j + 2 * f + 2)
                            dve.wait_ge(comb_used, i * 4 + 2 * j + f + 1)
                            nc.vector.tensor_tensor(hid[2 * j + f][:, :], sl[f][:, :], acc[f][:, 1, :],
                                                    ALU.mult).then_inc(hid_out, 1)
                        for t in range(8):
                            dve.wait_ge(dn_ready, i * 16 + 8 * j + t + 1)
                            nc.vector.tensor_tensor(xt[:, t, :], xt[:, t, :], acc[2 + t % 4 // 2][:, t % 2, :],
                                                    ALU.add).then_inc(dn_out, 1)

                    with dve.Fori(0, turns) as i:
                        expert(i, 0)
                        expert(i, 1)

        def second_block(b1, xt, h):
            with ExitStack() as sx:
                c2 = sbt(sx, "c2", [P, N2])

                def k2(name, n=P, at=0):
                    return c2[:, C2[name] + at:C2[name] + at + n]

                ht = lambda k: h[:, k, :]
                const2_in, meta_in = sem("const2_in"), sem("meta_in")
                with block() as b:
                    @b.sync
                    def _(sp):
                        sp.dma_start(c2[:, :], const2).then_inc(const2_in, 16)
                        sp.wait_ge(const2_in, 16)

                    @b.vector
                    def _(dve):
                        o = PCOL["meta"]
                        nc.vector.tensor_copy(h[:, :, 0:META], par[:, o:o + 8 * META].rearrange("p (k t) -> p k t", k=8))
                normalize("lnin", ht, ht, KD, T2, k0("mean1024"), lambda k: pcol("ln_in_g", k),
                          lambda k: pcol("ln_in_b", k), EPS_LN)
                with ExitStack() as rx:
                    mixers(rx, xt, h, k2)
                ffn(h)

        def mixers(rx, xt, h, k2):
            spilled = sem("spilled")
            wa, xg = sbt(rx, "wa", [P, T2]), sbt(rx, "xg", [P, 2, T2])
            r, k, v = (sbt(rx, n, [P, KD, T2]) for n in ("rw_r", "rw_k", "rw_v"))
            with ExitStack() as cx:
                cp, cv = sbt(cx, "cp", [P, KD, TAPS - 1 + T2]), sbt(cx, "cv", [P, KD, T2])
                glu_ready, glu_sig, glu_out = sem("glu_ready"), sem("glu_sig"), sem("glu_out")
                with ExitStack() as gx, block() as b:
                    sg = [sbt(gx, f"glu_sg{i}", [P, T2]) for i in range(2)]

                    @b.tensor
                    def _(pe):
                        pe_tiles(pe, "conv_in", KD, 16, lambda q: h[:, q, :], T2, glu_ready, glu_out)

                    @b.scalar
                    def _(act):
                        for i in range(8):
                            act.wait_ge(glu_ready, 2 * i + 2)
                            if i >= 2:
                                act.wait_ge(glu_out, 2 * i - 2)
                            nc.scalar.activation(fold(sg[i % 2][:, :], T2), A(2 * i % 4 + 1, T2),
                                                 ACT.Sigmoid).then_inc(glu_sig, 1)

                    @b.vector
                    def _(dve):
                        nc.vector.memset(cp[:, :, 0:TAPS - 1], 0.0)
                        for i in range(8):
                            dve.wait_ge(glu_sig, i + 1)
                            nc.vector.tensor_tensor(fold(cp[:, i, TAPS - 1:], T2), fold(sg[i % 2][:, :], T2),
                                                    A(2 * i % 4, T2), ALU.mult).then_inc(glu_out, 2)

                    @b.sync
                    def _(sp):
                        load_slabs(sp, "conv_in")
                tap_done = sem("tap_done")
                rw_ready, rw_read, rw_mixed, zeroed = sem("rw_ready"), sem("rw_read"), sem("rw_mixed"), sem("rw_zeroed")
                rw_dest = ([r[:, i, :] for i in range(8)] + [k[:, i, :] for i in range(8)]
                           + [v[:, i, :] for i in range(8)] + [wa[:, :]] + [xg[:, i, :] for i in range(2)])
                with ExitStack() as tx, block() as b:
                    sh = [sbt(tx, f"shift{i}", [P, T2 + 1]) for i in range(3)]
                    keep = sbt(tx, "keep", [P, 27])
                    o_mu = PCOL["mu"]

                    @b.tensor
                    def _(pe):
                        i = 0
                        for name, n in (("rw_r", 8), ("rw_k", 8), ("rw_v", 8), ("rw_wa", 1), ("rw_g", 2)):
                            pe_tiles(pe, name, KD, n, lambda q: h[:, q, :], T2, rw_ready, rw_read, first=i)
                            i += n

                    @b.scalar
                    def _(act):
                        act.wait_ge(zeroed, 4)
                        for i, d in enumerate(rw_dest):
                            act.wait_ge(rw_ready, i + 1)
                            nc.scalar.activation(fold(d, T2), A(i % 4, T2), ACT.Copy, scale=keep[:, i:i + 1])
                            if i >= 3:
                                act.wait_ge(rw_mixed, i - 2)
                            nc.scalar.activation(fold(sh[i % 3][:, 1:T2 + 1], T2), A(i % 4, T2), ACT.Copy,
                                                 scale=par[:, o_mu + i:o_mu + i + 1]).then_inc(rw_read, 1)

                    @b.gpsimd
                    def _(pool):
                        nc.gpsimd.tensor_scalar(keep[:, :], par[:, o_mu:o_mu + 27], -1.0, 1.0, ALU.mult,
                                                ALU.add).then_inc(zeroed, 1)
                        for i in range(3):
                            nc.gpsimd.memset(sh[i][:, 0:1], 0.0).then_inc(zeroed, 1)
                        pool.wait_ge(zeroed, 4)
                        for i, d in enumerate(rw_dest):
                            pool.wait_ge(rw_read, i + 1)
                            nc.gpsimd.tensor_tensor(d, d, sh[i % 3][:, 0:T2], ALU.add).then_inc(rw_mixed, 1)
                        pool.wait_ge(rw_mixed, 27)

                    @b.vector
                    def _(dve):
                        o_w, o_b = PCOL["conv_dw"], PCOL["conv_dw_b"]
                        for q in range(8):
                            nc.vector.tensor_scalar(cv[:, q, :], cp[:, q, 0:T2], par[:, o_w + TAPS * q:o_w + TAPS * q + 1],
                                                    par[:, o_b + q:o_b + q + 1], ALU.mult, ALU.add).then_inc(tap_done, 1)
                        with dve.Fori(1, TAPS) as j:
                            for q in range(8):
                                dve.wait_ge(tap_done, j * 8 + q - 7)
                                nc.vector.scalar_tensor_tensor(
                                    out=cv[:, q, :], in0=cp[:, q, bass.ds(j, T2)],
                                    scalar=par[:, bass.ds(j + (o_w + TAPS * q), 1)], in1=cv[:, q, :],
                                    op0=ALU.mult, op1=ALU.add).then_inc(tap_done, 1)

                    @b.sync
                    def _(sp):
                        load_slabs(sp, "rw_g")
                normalize("lnconv", lambda q: cv[:, q, :], lambda q: cv[:, q, :], KD, T2, k0("mean1024"),
                          lambda q: pcol("conv_ln_g", q), lambda q: pcol("conv_ln_b", q), EPS_LN, ACT.Silu)
                ya_ready, ya_out, ya_sig, ya_done = sem("ya_ready"), sem("ya_out"), sem("ya_sig"), sem("ya_done")
                y1 = lambda q: cp[:, q, 0:T2]
                with block() as b:
                    @b.tensor
                    def _(pe):
                        pe_tiles(pe, "gate_a", KD, 8, lambda q: h[:, q, :], T2, ya_ready, ya_sig)
                        pe.wait_ge(ya_sig, 8)
                        pe_tiles(pe, "conv_out", KD, 8, lambda q: cv[:, q, :], T2, ya_out, ya_done)

                    @b.scalar
                    def _(act):
                        for i in range(8):
                            act.wait_ge(ya_ready, i + 1)
                            nc.scalar.activation(fold(y1(i), T2), A(i % 4, T2), ACT.Sigmoid,
                                                 bias=pcol("b_gate", i)).then_inc(ya_sig, 1)

                    @b.vector
                    def _(dve):
                        for i in range(8):
                            dve.wait_ge(ya_out, i + 1)
                            nc.vector.tensor_tensor(fold(y1(i), T2), fold(y1(i), T2), A(i % 4, T2),
                                                    ALU.mult).then_inc(ya_done, 1)

                    @b.sync
                    def _(sp):
                        load_slabs(sp, "conv_out")
                        sp.dma_start(h_d, h[:, :, :]).then_inc(spilled, 16)
                        sp.wait_ge(ya_done, 8)
                        sp.dma_start(y_d, cp[:, :, 0:T2]).then_inc(spilled, 16)
                        sp.wait_ge(spilled, 32)
            with ExitStack() as wx:
                lw, a = sbt(wx, "rw_lw", [P, KD, T2]), sbt(wx, "rw_a", [P, KD, T2])
                kk = h
                wc = sbt(wx, "rw_wc", [P, KD, 9])
                decay_and_keys(xt, wa, r, k, v, kk, a, lw, wc, k2)
                recurrence(xt, wa, r, k, v, kk, a, lw, wc, k2)
                group_norm_and_gate(xt, r, k, v, lw, xg)
                merge(h, r, k, lw)

        def decay_and_keys(xt, wa, r, k, v, kk, a, lw, wc, k2):
            tanhed, up_ready, up_read = sem("tanhed"), sem("wu_ready"), sem("wu_read")
            with block() as b:
                @b.scalar
                def _(act):
                    nc.scalar.activation(wa[0:64, :], wa[0:64, :], ACT.Tanh).then_inc(tanhed, 1)
                    for i in range(16):
                        act.wait_ge(up_ready, i + 1)
                        d, name = (lw, "w0") if i % 2 == 0 else (a, "a0")
                        nc.scalar.activation(fold(d[:, i // 2, :], T2), A(i % 4, T2), ACT.Sigmoid,
                                             bias=pcol(name, i // 2)).then_inc(up_read, 1)

                @b.tensor
                def _(pe):
                    pe.wait_ge(tanhed, 1)
                    n = SLAB0["wa_up"]
                    slab_wait(pe, n)
                    for i in range(16):
                        r0 = 64 * (i % 2)
                        if i >= 4:
                            pe.wait_ge(up_read, i - 3)
                        for s, (lo, hi) in enumerate(halves(T2)):
                            mm = nc.tensor.matmul(acc[i % 4][:, s, 0:hi - lo], ring[n % RING][r0:r0 + 64, i // 2 * P:i // 2 * P + P],
                                                  wa[r0:r0 + 64, lo:hi], start=True, stop=True)
                        mm.then_inc(up_ready, 1)
                    freed_by[n] = (up_ready, 16)

                @b.sync
                def _(sp):
                    load_slabs(sp, "wa_up")
            kk_made, kk_sq, sq_summed, kk_root, key_done = (sem("kk_made"), sem("kk_sq"), sem("kk_summed"),
                                                          sem("kk_root"), sem("key_done"))
            normed = sem("kk_normed")
            with ExitStack() as nx, block() as b:
                sq = [xt[:, 2 * i:2 * i + 2, :].rearrange("p a t -> p (a t)")[:, 0:T2] for i in range(4)]
                root = [sbt(nx, f"kk_root{i}", [P, T2]) for i in range(2)]
                scr = sbt(nx, "key_scr", [P, T2])
                omk = sbt(nx, "omk", [P, KD])

                @b.vector
                def _(dve):
                    o = PCOL["k_a"]
                    link("dve", dve, nc.vector.tensor_scalar(omk[:, :], par[:, o:o + 8], -1.0, 1.0, ALU.mult, ALU.add))
                    for i in range(8):
                        nc.vector.tensor_scalar(kk[:, i, :], k[:, i, :], pcol("k_k", i), None, ALU.mult).then_inc(kk_made, 1)
                    for i in range(8):
                        link("dve", dve, nc.vector.tensor_scalar(scr[:, :], a[:, i, :], pcol("k_a", i), omk[:, i:i + 1],
                                                                 ALU.mult, ALU.add))
                        link("dve", dve, nc.vector.tensor_tensor(k[:, i, :], k[:, i, :], scr[:, :], ALU.mult))
                        dve.wait_ge(kk_root, i + 1)
                        link("dve", dve, nc.vector.tensor_scalar(root[i % 2][:, :], root[i % 2][:, :], 1e-12, None, ALU.max))
                        link("dve", dve, nc.vector.reciprocal(root[i % 2][:, :], root[i % 2][:, :]))
                        nc.vector.tensor_tensor(kk[:, i, :], kk[:, i, :], root[i % 2][:, :], ALU.mult).then_inc(normed, 1)

                def root_of(act, i):
                    act.wait_ge(sq_summed, i + 1)
                    if i >= 2:
                        act.wait_ge(normed, i - 1)
                    nc.scalar.activation(fold(root[i % 2][:, :], T2), A(i % 4, T2), ACT.Sqrt).then_inc(kk_root, 1)

                @b.scalar
                def _(act):
                    for i in range(8):
                        act.wait_ge(kk_made, i + 1)
                        if i >= 4:
                            act.wait_ge(sq_summed, i - 3)
                        nc.scalar.activation(sq[i % 4], kk[:, i, :], ACT.Square).then_inc(kk_sq, 1)
                        if i >= 1:
                            root_of(act, i - 1)
                    root_of(act, 7)

                @b.tensor
                def _(pe):
                    for i in range(8):
                        pe.wait_ge(kk_sq, i + 1)
                        if i >= 4:
                            pe.wait_ge(kk_root, i - 3)
                        for s, (lo, hi) in enumerate(halves(T2)):
                            mm = nc.tensor.matmul(acc[i % 4][:, s, 0:hi - lo], k0("ones64"), sq[i % 4][:, lo:hi],
                                                  start=True, stop=True)
                        mm.then_inc(sq_summed, 1)
            scanned, e_up, e_dn, up_used, b_made, dn_used = (sem("scanned"), sem("e_up"), sem("e_dn"), sem("up_used"),
                                                            sem("b_made"), sem("dn_used"))
            with ExitStack() as nx, block() as b:
                eu = [sbt(nx, f"eu{i}", [P, T2]) for i in range(2)]
                ed = [sbt(nx, f"ed{i}", [P, T2]) for i in range(2)]
                first = sbt(nx, "first", [P, 9])

                @b.vector
                def _(dve):
                    def scan(i):
                        link("dve", dve, nc.vector.tensor_scalar(lw[:, i, :], lw[:, i, :], -float(np.exp(-0.5)), None, ALU.mult))
                        nc.vector.tensor_tensor_scan(lw[:, i, :], k2("resets", T2), lw[:, i, :], 0.0, ALU.mult,
                                                     ALU.add).then_inc(scanned, 1)

                    scan(0)
                    for i in range(8):
                        if i < 7:
                            scan(i + 1)
                        dve.wait_ge(e_up, i + 1)
                        e = eu[i % 2]
                        nc.vector.tensor_tensor(r[:, i, :], r[:, i, :], e[:, :], ALU.mult)
                        nc.vector.tensor_copy(wc[:, i, 0:8], e[:, CH - 1:T1:CH])
                        nc.vector.tensor_copy(wc[:, i, 8:9], e[:, T2 - 1:T2])
                        dve.wait_ge(b_made, i + 1)
                        link("dve", dve, nc.vector.tensor_scalar(first[:, :], kk[:, i, 0:T2:CH], -1.0, None, ALU.mult))
                        link("dve", dve, nc.vector.scalar_tensor_tensor(out=kk[:, i, 1:T2], in0=kk[:, i, 1:T2], scalar=-1.0,
                                                                        in1=e[:, 0:T2 - 1], op0=ALU.mult, op1=ALU.mult))
                        nc.vector.tensor_copy(kk[:, i, 0:T2:CH], first[:, :]).then_inc(up_used, 1)
                        dve.wait_ge(up_used, i + 1)

                @b.scalar
                def _(act):
                    for i in range(8):
                        act.wait_ge(scanned, i + 1)
                        if i >= 2:
                            act.wait_ge(up_used, i - 1)
                            act.wait_ge(dn_used, i - 1)
                        nc.scalar.activation(eu[i % 2][:, :], lw[:, i, :], ACT.Exp).then_inc(e_up, 1)
                        nc.scalar.activation(ed[i % 2][:, :], lw[:, i, :], ACT.Exp, scale=-1.0).then_inc(e_dn, 1)

                @b.gpsimd
                def _(pool):
                    for i in range(8):
                        nc.gpsimd.tensor_tensor(a[:, i, :], a[:, i, :], kk[:, i, :], ALU.mult).then_inc(b_made, 1)
                    for i in range(8):
                        pool.wait_ge(e_dn, i + 1)
                        nc.gpsimd.tensor_tensor(k[:, i, :], k[:, i, :], ed[i % 2][:, :], ALU.mult)
                        pool.wait_ge(b_made, i + 1)
                        nc.gpsimd.tensor_tensor(a[:, i, :], a[:, i, :], ed[i % 2][:, :], ALU.mult).then_inc(dn_used, 1)
                    pool.wait_ge(dn_used, 8)

        def recurrence(xt, wa, r, k, v, kk, a, o, wc, k2):
            bank = lambda i: acc[i // 2][:, i % 2, :]
            tiles = [(i * P, P, [(0, CH), (CH, CH)], 6) for i in range(T2 // P)] + [(T1, META, [(0, META)], 4)]
            pe_did, act_did, dve_did, pool_did = sem("rec_pe"), sem("rec_act"), sem("rec_dve"), sem("rec_pool")
            arrays = [kk, a, k, v]

            def events(chunks, nl):
                two = range(2)
                pe = [("tm", g) for g in range(8)]
                act = [("tm", g) for g in range(0, 8, 2)]
                dve = [("tm", g) for g in range(1, 8, 2)]
                pool = []
                for bp in two:
                    grams = [("gram", bp, p, m) for p in two for m in range(5)]
                    pe += grams
                    dve += grams
                    for p in two:
                        pool += [("mt", bp, p)]
                    for l in range(1, nl):
                        pe += [("x", bp, l, p) for p in two] + [("m", bp, l, p) for p in two]
                        act += [("x", bp, l, p) for p in two]
                        dve += [("m", bp, l, p) for p in two]
                        pool += [("ot", bp, l, p) for p in two]
                    pe += [("z", bp, p) for p in two] + [("ug", bp, p) for p in two]
                    act += [("z", bp, p) for p in two] + [("gt", bp, p) for p in two]
                    dve += [("uv", bp, p) for p in two]
                for j in range(len(chunks)):
                    pe += [("u", j), ("s", j)]
                    dve += [("u", j), ("s", j)]
                pe += [("y", 0), ("y", 1)]
                act += [("y", 0), ("y", 1)]
                return {"pe": pe, "act": act, "dve": dve, "pool": pool}

            plans, base = [], {"pe": 0, "act": 0, "dve": 0, "pool": 0}
            sems = {"pe": pe_did, "act": act_did, "dve": dve_did, "pool": pool_did}
            for t0, n, chunks, nl in tiles:
                ev = events(chunks, nl)
                plans.append({(e, name): base[e] + i + 1 for e in ev for i, name in enumerate(ev[e])})
                for e in ev:
                    base[e] += len(ev[e])

            def after(eng, ti, who, *name):
                eng.wait_ge(sems[who], plans[ti][(who, name)])

            sent = {e: 0 for e in sems}

            def did(ins, ti, who, *name):
                sent[who] += 1
                assert plans[ti][(who, name)] == sent[who], (ti, who, name)
                ins.then_inc(sems[who], 1)

            with ExitStack() as nx, block() as b:
                tm = [sbt(nx, f"tm{i}", [P, D]) for i in range(4)]
                tm_a, tm_b, tm_k, tm_v = tm
                arb, ark = sbt(nx, "arb", [P, 8, 2, P]), sbt(nx, "ark", [P, 8, 2, P])
                gt, uv = sbt(nx, "gt", [P, 8, P]), sbt(nx, "uv", [P, 8, 2, 64])
                S = [sbt(nx, f"S{i}", [P, 8, 64]) for i in range(3)]
                at = [sbt(nx, f"at{p}", [P, 4, P]) for p in range(2)]
                aak = [sbt(nx, f"aak{p}", [P, 4, P]) for p in range(2)]
                M = [xt[:, 2 * p, :].rearrange("p (q t) -> p q t", q=4) for p in range(2)]
                MT = [xt[:, 2 * p + 1, :].rearrange("p (q t) -> p q t", q=4) for p in range(2)]
                X = [xt[:, 4 + p, :].rearrange("p (q t) -> p q t", q=4) for p in range(2)]
                four = lambda ap: ap.rearrange("p (q t) -> p q t", q=4)
                OT = [[four(xt[:, 7, :]), four(wa[:, 0:512])], [four(k2("resets", 512)), sbt(nx, "ot", [P, 4, P])]]
                z = [four(xt[:, 6, 256 * p:256 * p + 256]) for p in range(2)]
                grid = lambda i, n, w=P: bank(i)[:, 0:4 * w].rearrange("p (q t) -> p q t", q=4)[0:n, :, 0:min(n, w)]
                mask = lambda ap, n: ap[0:n, 0:n].unsqueeze(1).to_broadcast([n, 4, n])

                @b.tensor
                def _(pe):
                    mmul = nc.tensor.matmul
                    chunk0 = 0
                    for ti, (t0, n, chunks, nl) in enumerate(tiles):
                        for g in range(8):
                            if g == 0 and ti:
                                after(pe, ti - 1, "act", "y", 1)
                                after(pe, ti - 1, "dve", "s", len(tiles[ti - 1][2]) - 1)
                            for q in range(4):
                                mm = nc.tensor.transpose(bank(g)[0:n, q * P:(q + 1) * P],
                                                         arrays[g // 2][:, 4 * (g % 2) + q, t0:t0 + n], k0("ident"))
                            did(mm, ti, "pe", "tm", g)
                        for bp in range(2):
                            for p in range(2):
                                rows = slice(64 * p, 64 * p + 64)
                                for m in range(5):
                                    i = 5 * p + m
                                    if i == 0 and bp == 0:
                                        after(pe, ti, "act", "tm", 6)
                                        after(pe, ti, "dve", "tm", 7)
                                    if i == 0 and bp == 1:
                                        after(pe, ti, "act", "gt", 0, 1)
                                        after(pe, ti, "dve", "uv", 0, 1)
                                    if i >= 8:
                                        after(pe, ti, "dve", "gram", bp, (i - 8) // 5, (i - 8) % 5)
                                    left, right = [(a, kk), (kk, a), (k, kk), (a, r), (k, r)][m]
                                    for q in range(4):
                                        mm = mmul(bank(i % 8)[0:n, q * P:q * P + n], left[rows, 4 * bp + q, t0:t0 + n],
                                                  right[rows, 4 * bp + q, t0:t0 + n], start=True, stop=True)
                                    did(mm, ti, "pe", "gram", bp, p, m)
                            after(pe, ti, "dve", "gram", bp, 1, 4)
                            for l in range(1, nl):
                                for p in range(2):
                                    after(pe, ti, "pool", "ot", bp, l, p)
                                    if l > 1:
                                        after(pe, ti, "dve", "m", bp, l - 1, p)
                                    for q in range(4):
                                        mm = mmul(bank(p)[0:n, q * P:q * P + n], OT[l % 2][p][0:n, q, 0:n], M[p][0:n, q, 0:n],
                                                  start=True, stop=True)
                                    did(mm, ti, "pe", "x", bp, l, p)
                                for p in range(2):
                                    after(pe, ti, "act", "x", bp, l, p)
                                    if l == 1:
                                        after(pe, ti, "pool", "mt", bp, p)
                                    if l < nl - 1:
                                        for q in range(4):
                                            mmul(bank(2 + p)[0:n, q * P:q * P + n], MT[p][0:n, q, 0:n], X[p][0:n, q, 0:n],
                                                 start=True, stop=True)
                                    for q in range(4):
                                        mm = mmul(bank(4 + p)[0:n, q * P:q * P + n], X[p][0:n, q, 0:n], MT[p][0:n, q, 0:n],
                                                  start=True, stop=True)
                                    did(mm, ti, "pe", "m", bp, l, p)
                            for p in range(2):
                                for q in range(4):
                                    hd = 64 * (2 * (4 * bp + q) + p)
                                    mm = mmul(bank(6 + p)[0:n, q * 64:q * 64 + 64], aak[p][0:n, q, 0:n],
                                              tm_v[0:n, hd:hd + 64], start=True, stop=True)
                                did(mm, ti, "pe", "z", bp, p)
                            for p in range(2):
                                after(pe, ti, "act", "z", bp, p)
                                after(pe, ti, "dve", "m", bp, nl - 1, p)
                                for q in range(4):
                                    mmul(bank(p)[0:n, q * 64:q * 64 + 64], MT[p][0:n, q, 0:n], z[p][0:n, q, :],
                                         start=True, stop=True)
                                for q in range(4):
                                    hd = 64 * (2 * (4 * bp + q) + p)
                                    mm = mmul(bank(2 + p)[64 * p:64 * p + 64, q * P:q * P + n], tm_a[0:n, hd:hd + 64],
                                              MT[p][0:n, q, 0:n], start=True, stop=True)
                                did(mm, ti, "pe", "ug", bp, p)
                        after(pe, ti, "act", "gt", 1, 1)
                        after(pe, ti, "dve", "uv", 1, 1)
                        for j, (c0_, cn) in enumerate(chunks):
                            s = S[(chunk0 + j) % 3]
                            if j:
                                after(pe, ti, "dve", "s", j - 1)
                            for p in range(2):
                                rows = slice(64 * p, 64 * p + 64)
                                for q in range(8):
                                    mm = mmul(bank(p)[c0_:c0_ + cn, q * 64:q * 64 + 64], gt[rows, q, c0_:c0_ + cn],
                                              s[rows, q, :], start=True, stop=True)
                            did(mm, ti, "pe", "u", j)
                            after(pe, ti, "dve", "u", j)
                            cr = slice(c0_, c0_ + cn)
                            for q in range(8):
                                for p in range(2):
                                    hd = 64 * (2 * q + p)
                                    d = bank(2)[64 * p:64 * p + 64, q * 64:q * 64 + 64]
                                    mmul(d, tm_b[cr, hd:hd + 64], uv[cr, q, p, :], start=True, stop=False)
                                    mm = mmul(d, tm_k[cr, hd:hd + 64], tm_v[cr, hd:hd + 64], start=False, stop=True)
                            did(mm, ti, "pe", "s", j)
                        for half in range(2):
                            for q in range(4 * half, 4 * half + 4):
                                for p in range(2):
                                    hd = 64 * (2 * q + p)
                                    rows = slice(64 * p, 64 * p + 64)
                                    at0 = q % 4 * P
                                    d = bank(4 + half)[rows, at0:at0 + n]
                                    mmul(d, uv[0:n, q, p, :], arb[0:n, q, p, 0:n], start=True, stop=False)
                                    mmul(d, tm_v[0:n, hd:hd + 64], ark[0:n, q, p, 0:n], start=False, stop=False)
                                    for j, (c0_, cn) in enumerate(chunks):
                                        mm = mmul(bank(4 + half)[rows, at0 + c0_:at0 + c0_ + cn], S[(chunk0 + j) % 3][rows, q, :],
                                                  r[rows, q, t0 + c0_:t0 + c0_ + cn], start=False, stop=j == len(chunks) - 1)
                            did(mm, ti, "pe", "y", half)
                        chunk0 += len(chunks)

                @b.scalar
                def _(act):
                    cp_ = lambda d, s_: nc.scalar.activation(d, s_, ACT.Copy)
                    for ti, (t0, n, chunks, nl) in enumerate(tiles):
                        for g in range(0, 8, 2):
                            after(act, ti, "pe", "tm", g)
                            did(cp_(tm[g // 2][0:n, 0:512], bank(g)[0:n, :]), ti, "act", "tm", g)
                        for bp in range(2):
                            for l in range(1, nl):
                                for p in range(2):
                                    after(act, ti, "pe", "x", bp, l, p)
                                    did(cp_(X[p][0:n, :, 0:n], grid(p, n)), ti, "act", "x", bp, l, p)
                            for p in range(2):
                                after(act, ti, "pe", "z", bp, p)
                                did(cp_(z[p][0:n, :, :], bank(6 + p)[0:n, 0:256].rearrange("p (q t) -> p q t", q=4)),
                                    ti, "act", "z", bp, p)
                            for p in range(2):
                                after(act, ti, "pe", "ug", bp, p)
                                rows = slice(64 * p, 64 * p + 64)
                                src = bank(2 + p).rearrange("p (q t) -> p q t", q=4)[rows, :, 0:n]
                                did(cp_(gt[rows, 4 * bp:4 * bp + 4, 0:n], src), ti, "act", "gt", bp, p)
                        for half in range(2):
                            after(act, ti, "pe", "y", half)
                            src = bank(4 + half).rearrange("p (q t) -> p q t", q=4)[:, :, 0:n]
                            did(cp_(o[:, 4 * half:4 * half + 4, t0:t0 + n], src), ti, "act", "y", half)

                @b.vector
                def _(dve):
                    tt = nc.vector.tensor_tensor
                    link("dve", dve, nc.vector.memset(S[0][:, :, :], 0.0))
                    chunk0 = 0
                    for ti, (t0, n, chunks, nl) in enumerate(tiles):
                        for g in range(1, 8, 2):
                            after(dve, ti, "pe", "tm", g)
                            did(nc.vector.tensor_copy(tm[g // 2][0:n, 512:1024], bank(g)[0:n, :]), ti, "dve", "tm", g)
                        for bp in range(2):
                            if bp:
                                after(dve, ti, "pool", "ot", 0, nl - 1, 1)
                            for p in range(2):
                                for m in range(5):
                                    i = 5 * p + m
                                    after(dve, ti, "pe", "gram", bp, p, m)
                                    src = grid(i % 8, n)
                                    d, mk = [(at[p][0:n, :, 0:n], "strict"), (M[p][0:n, :, 0:n], "level0_low"),
                                             (aak[p][0:n, :, 0:n], "strict"), (arb[0:n, 4 * bp:4 * bp + 4, p, 0:n], "incl"),
                                             (ark[0:n, 4 * bp:4 * bp + 4, p, 0:n], "incl")][m]
                                    ins = tt(d, src, mask(k2(mk), n), ALU.mult)
                                    if m == 1:
                                        link("dve", dve, ins)
                                        ins = tt(d, d, mask(k0("ident"), n), ALU.add)
                                    did(ins, ti, "dve", "gram", bp, p, m)
                            for l in range(1, nl):
                                for p in range(2):
                                    after(dve, ti, "pe", "m", bp, l, p)
                                    if l < nl - 1:
                                        tt(M[p][0:n, :, 0:n], M[p][0:n, :, 0:n], grid(2 + p, n), ALU.add)
                                    did(tt(MT[p][0:n, :, 0:n], MT[p][0:n, :, 0:n], grid(4 + p, n), ALU.add),
                                        ti, "dve", "m", bp, l, p)
                            for p in range(2):
                                after(dve, ti, "pe", "ug", bp, p)
                                did(nc.vector.tensor_copy(uv[0:n, 4 * bp:4 * bp + 4, p, :],
                                                          bank(p)[0:n, 0:256].rearrange("p (q t) -> p q t", q=4)),
                                    ti, "dve", "uv", bp, p)
                        for j, (c0_, cn) in enumerate(chunks):
                            after(dve, ti, "pe", "u", j)
                            cr = slice(c0_, c0_ + cn)
                            for p in range(2):
                                ins = tt(uv[cr, :, p, :], uv[cr, :, p, :], bank(p)[cr, :].rearrange("p (q t) -> p q t", q=8), ALU.add)
                            did(ins, ti, "dve", "u", j)
                            after(dve, ti, "pe", "s", j)
                            cg = chunk0 + j
                            s, sn = S[cg % 3], S[(cg + 1) % 3]
                            link("dve", dve, tt(sn[:, :, :], s[:, :, :], bank(2).rearrange("p (q t) -> p q t", q=8), ALU.add))
                            did(tt(sn[:, :, :], sn[:, :, :], wc[:, :, cg:cg + 1].to_broadcast([P, 8, 64]), ALU.mult),
                                ti, "dve", "s", j)
                            after(dve, ti, "dve", "s", j)
                        chunk0 += len(chunks)

                @b.gpsimd
                def _(pool):
                    tt = nc.gpsimd.tensor_tensor
                    for ti, (t0, n, chunks, nl) in enumerate(tiles):
                        for bp in range(2):
                            for p in range(2):
                                after(pool, ti, "dve", "gram", bp, p, 0)
                                if bp or ti:
                                    after(pool, *((ti, "pe", "ug", 0, p) if bp else (ti - 1, "pe", "ug", 1, p)))
                                d = MT[p][0:n, :, 0:n]
                                link("pool", pool, tt(d, at[p][0:n, :, 0:n], mask(k2("levels"), n), ALU.mult))
                                did(tt(d, d, mask(k0("ident"), n), ALU.add), ti, "pool", "mt", bp, p)
                            for l in range(1, nl):
                                for p in range(2):
                                    if l > 2:
                                        after(pool, ti, "pe", "x", bp, l - 2, p)
                                    did(tt(OT[l % 2][p][0:n, :, 0:n], at[p][0:n, :, 0:n], mask(k2("levels", P, l * P), n), ALU.mult),
                                        ti, "pool", "ot", bp, l, p)
                    pool.wait_ge(pool_did, base["pool"])

        def group_norm_and_gate(xt, r, k, v, o, xg):
            meaned, centred, squared, varred, rooted = (sem("gn_" + n) for n in ("meaned", "centred", "squared", "varred", "rooted"))
            scaled, shifted, prod_made, bonus, bonus_read = (sem("gn_" + n) for n in ("scaled", "shifted", "prod", "bonus", "bonus_read"))
            added, g_ready, gated, sig = (sem("gn_" + n) for n in ("added", "g_ready", "gated", "sig"))
            with ExitStack() as nx, block() as b:
                view = lambda i: xt[:, 2 * i:2 * i + 2, :].rearrange("p a t -> p (a t)")[:, 0:T2]
                sq, prod = [view(0), view(1)], [view(2), view(3)]
                root = [sbt(nx, f"gn_root{i}", [P, T2]) for i in range(2)]
                bon = [sbt(nx, f"gn_bon{i}", [P, T2]) for i in range(2)]

                @b.tensor
                def _(pe):
                    def over(j, mat, x):
                        for s, (lo, hi) in enumerate(halves(T2)):
                            mm = nc.tensor.matmul(acc[j][:, s, 0:hi - lo], mat, x[:, lo:hi], start=True, stop=True)
                        return mm

                    n = SLAB0["g_up"]
                    for i in range(8):
                        if i >= 1:
                            pe.wait_ge(centred, i)
                        over(0, k0("mean64"), o[:, i, :]).then_inc(meaned, 1)
                        pe.wait_ge(prod_made, i + 1)
                        if i >= 1:
                            pe.wait_ge(bonus_read, i)
                        over(2, k0("ones64"), prod[i % 2]).then_inc(bonus, 1)
                        pe.wait_ge(squared, i + 1)
                        if i >= 1:
                            pe.wait_ge(rooted, i)
                        over(1, k0("mean64"), sq[i % 2]).then_inc(varred, 1)
                        if i == 0:
                            pe.wait_ge(sig, 1)
                            slab_wait(pe, n)
                            slab_wait(pe, n + 1)
                        else:
                            pe.wait_ge(gated, i)
                        for q in range(2):
                            for s, (lo, hi) in enumerate(halves(T2)):
                                mm = nc.tensor.matmul(acc[3][:, s, 0:hi - lo], ring[(n + q) % RING][:, i * P:(i + 1) * P],
                                                      xg[:, q, lo:hi], start=(q == 0), stop=(q == 1))
                        mm.then_inc(g_ready, 1)
                    freed_by[n] = freed_by[n + 1] = (g_ready, 8)

                @b.scalar
                def _(act):
                    nc.scalar.activation(xg[:, :, :], xg[:, :, :], ACT.Sigmoid).then_inc(sig, 1)
                    for i in range(8):
                        act.wait_ge(centred, i + 1)
                        if i >= 2:
                            act.wait_ge(varred, i - 1)
                        nc.scalar.activation(sq[i % 2], o[:, i, :], ACT.Square).then_inc(squared, 1)
                        act.wait_ge(varred, i + 1)
                        if i >= 2:
                            act.wait_ge(scaled, i - 1)
                        nc.scalar.activation(fold(root[i % 2][:, :], T2), A(1, T2), ACT.Sqrt,
                                             bias=k0("eps", 1, EPS_GN)).then_inc(rooted, 1)
                        act.wait_ge(scaled, i + 1)
                        nc.scalar.activation(o[:, i, :], o[:, i, :], ACT.Identity, scale=pcol("lnx_g", i),
                                             bias=pcol("lnx_b", i)).then_inc(shifted, 1)

                @b.vector
                def _(dve):
                    tt = nc.vector.tensor_tensor
                    for i in range(8):
                        dve.wait_ge(meaned, i + 1)
                        tt(fold(o[:, i, :], T2), fold(o[:, i, :], T2), A(0, T2), ALU.subtract).then_inc(centred, 1)
                        if i >= 2:
                            dve.wait_ge(bonus, i - 1)
                        nc.vector.scalar_tensor_tensor(out=prod[i % 2], in0=r[:, i, :], scalar=pcol("r_k", i), in1=k[:, i, :],
                                                       op0=ALU.mult, op1=ALU.mult).then_inc(prod_made, 1)
                        dve.wait_ge(bonus, i + 1)
                        if i >= 2:
                            dve.wait_ge(added, i - 1)
                        tt(fold(bon[i % 2][:, :], T2), fold(v[:, i, :], T2), A(2, T2), ALU.mult).then_inc(bonus_read, 1)
                        dve.wait_ge(rooted, i + 1)
                        link("dve", dve, nc.vector.reciprocal(root[i % 2][:, :], root[i % 2][:, :]))
                        tt(o[:, i, :], o[:, i, :], root[i % 2][:, :], ALU.mult).then_inc(scaled, 1)
                        dve.wait_ge(added, i + 1)
                        dve.wait_ge(g_ready, i + 1)
                        tt(fold(o[:, i, :], T2), fold(o[:, i, :], T2), A(3, T2), ALU.mult).then_inc(gated, 1)

                @b.gpsimd
                def _(pool):
                    for i in range(8):
                        pool.wait_ge(shifted, i + 1)
                        pool.wait_ge(bonus_read, i + 1)
                        nc.gpsimd.tensor_tensor(o[:, i, :], o[:, i, :], bon[i % 2][:, :], ALU.add).then_inc(added, 1)
                    pool.wait_ge(added, 8)

                @b.sync
                def _(sp):
                    load_slabs(sp, "g_up")

        def merge(h, y, gb, o):
            back = sem("unspilled")
            g_ready, g_out, o_ready, o_out, y_done = (sem("mg_" + n) for n in ("g_ready", "g_out", "o_ready", "o_out", "y_done"))
            with block() as b:
                @b.sync
                def _(sp):
                    sp.dma_start(h[:, :, :], h_d).then_inc(back, 16)
                    sp.dma_start(y[:, :, :], y_d).then_inc(back, 16)

                @b.tensor
                def _(pe):
                    pe.wait_ge(back, 32)
                    pe_tiles(pe, "gate_b", KD, 8, lambda q: h[:, q, :], T2, g_ready, g_out)
                    pe.wait_ge(g_out, 8)
                    pe_tiles(pe, "rw_out", KD, 8, lambda q: o[:, q, :], T2, o_ready, o_out)

                @b.scalar
                def _(act):
                    for i in range(8):
                        act.wait_ge(g_ready, i + 1)
                        nc.scalar.activation(fold(gb[:, i, :], T2), A(i % 4, T2), ACT.Sigmoid,
                                             bias=pcol("b_gate", 8 + i)).then_inc(g_out, 1)

                @b.vector
                def _(dve):
                    for i in range(8):
                        dve.wait_ge(o_ready, i + 1)
                        nc.vector.tensor_tensor(fold(gb[:, i, :], T2), fold(gb[:, i, :], T2), A(i % 4, T2),
                                                ALU.mult).then_inc(o_out, 1)

                @b.gpsimd
                def _(pool):
                    pool.wait_ge(back, 32)
                    for i in range(8):
                        pool.wait_ge(o_out, i + 1)
                        nc.gpsimd.tensor_tensor(y[:, i, :], y[:, i, :], gb[:, i, :], ALU.add).then_inc(y_done, 1)
                    pool.wait_ge(y_done, 8)

                @b.sync
                def _(sp):
                    load_slabs(sp, "rw_out")
            w_ready, w_out = sem("mg_w_ready"), sem("mg_w_out")
            with block() as b:
                @b.tensor
                def _(pe):
                    pe_tiles(pe, "w_o2", KD, 8, lambda q: y[:, q, :], T2, w_ready, w_out)

                @b.vector
                def _(dve):
                    for i in range(8):
                        dve.wait_ge(w_ready, i + 1)
                        nc.vector.scalar_tensor_tensor(out=fold(h[:, i, :], T2), in0=fold(h[:, i, :], T2), scalar=ALPHA,
                                                       in1=A(i % 4, T2), op0=ALU.mult, op1=ALU.add).then_inc(w_out, 1)

                @b.sync
                def _(sp):
                    load_slabs(sp, "w_o2")
            ht = lambda q: h[:, q, :]
            normalize("ln1", ht, ht, KD, T2, k0("mean1024"), lambda q: pcol("ln1_g", q), lambda q: pcol("ln1_b", q), EPS_LN)

        def ffn(h):
            up_ready, up_read, tapped, silued, hid_made = (sem("ff_" + n) for n in ("up_ready", "up_read", "tapped", "silued", "hid"))
            dn_ready, dn_out, stored = sem("ff_dn_ready"), sem("ff_dn_out"), sem("out_stored")
            with ExitStack() as fx:
                hid = sbt(fx, "ff_hid", [P, NF, T2])
                with ExitStack() as ux, block() as b:
                    up = [sbt(ux, f"ff_up{i}", [P, 2 + T2]) for i in range(4)]
                    t = [sbt(ux, f"ff_t{i}", [P, T2]) for i in range(4)]
                    padded = sem("ff_padded")

                    @b.tensor
                    def _(pe):
                        pe_tiles(pe, "ffn_up", KD, 2 * NF, lambda q: h[:, q, :], T2, up_ready, up_read)

                    def silu(act, f):
                        act.wait_ge(tapped, 2 * f + 2)
                        g = t[(2 * f + 1) % 4]
                        nc.scalar.activation(g[:, :], g[:, :], ACT.Silu).then_inc(silued, 1)

                    @b.scalar
                    def _(act):
                        act.wait_ge(padded, 4)
                        for i in range(2 * NF):
                            act.wait_ge(up_ready, i + 1)
                            if i >= 4:
                                act.wait_ge(tapped, i - 3)
                            nc.scalar.activation(fold(up[i % 4][:, 2:2 + T2], T2), A(i % 4, T2), ACT.Copy).then_inc(up_read, 1)
                            if i % 2 and i >= 3:
                                silu(act, i // 2 - 1)
                        silu(act, NF - 1)

                    @b.vector
                    def _(dve):
                        o_w = PCOL["ffn_dw"]
                        for i in range(4):
                            nc.vector.memset(up[i][:, 0:2], 0.0).then_inc(padded, 1)
                        for i in range(2 * NF):
                            f = i // 2 + NF * (i % 2)
                            w = lambda j: par[:, o_w + 3 * f + j:o_w + 3 * f + j + 1]
                            d = t[i % 4][:, :]
                            dve.wait_ge(up_read, i + 1)
                            if i >= 4:
                                dve.wait_ge(hid_made, i // 2 - 1)
                            link("dve", dve, nc.vector.tensor_scalar(d, up[i % 4][:, 0:T2], w(0), None, ALU.mult))
                            link("dve", dve, nc.vector.scalar_tensor_tensor(out=d, in0=up[i % 4][:, 1:1 + T2], scalar=w(1), in1=d,
                                                                            op0=ALU.mult, op1=ALU.add))
                            nc.vector.scalar_tensor_tensor(out=d, in0=up[i % 4][:, 2:2 + T2], scalar=w(2), in1=d,
                                                           op0=ALU.mult, op1=ALU.add).then_inc(tapped, 1)

                    @b.gpsimd
                    def _(pool):
                        for f in range(NF):
                            pool.wait_ge(silued, f + 1)
                            nc.gpsimd.tensor_tensor(hid[:, f, :], t[2 * f % 4][:, :], t[(2 * f + 1) % 4][:, :],
                                                    ALU.mult).then_inc(hid_made, 1)
                        pool.wait_ge(hid_made, NF)

                    @b.sync
                    def _(sp):
                        load_slabs(sp, "ffn_up")
                with block() as b:
                    @b.tensor
                    def _(pe):
                        pe_tiles(pe, "ffn_down", NF, 8, lambda q: hid[:, q, :], T2, dn_ready, dn_out)

                    @b.vector
                    def _(dve):
                        for i in range(8):
                            dve.wait_ge(dn_ready, i + 1)
                            nc.vector.scalar_tensor_tensor(out=fold(h[:, i, :], T2), in0=fold(h[:, i, :], T2), scalar=ALPHA,
                                                           in1=A(i % 4, T2), op0=ALU.mult, op1=ALU.add).then_inc(dn_out, 1)

                    @b.sync
                    def _(sp):
                        load_slabs(sp, "ffn_down")
            ht = lambda q: h[:, q, :]
            normalize("ln2", ht, ht, KD, T2, k0("mean1024"), lambda q: pcol("ln2_g", q), lambda q: pcol("ln2_b", q), EPS_LN)
            with block() as b:
                @b.sync
                def _(sp):
                    sp.dma_start(out, h[:, :, META:T2]).then_inc(stored, 16)
                    sp.wait_ge(stored, 16)

        with ExitStack() as b1:
            xt = sbt(b1, "xt", [P, KD, T1])
            x2 = first_block(b1, xt)
            second_block(b1, xt, x2)


def kernel(**inputs):
    import numpy as _np
    import concourse.bacc as _bacc
    from concourse.bass_utils import run_bass_kernel_spmd as _run

    nc = _bacc.Bacc("TRN2", target_bir_lowering=False, num_devices=1)
    a = {k: _np.asarray(v) for k, v in inputs.items()}
    arrays = lay_out(a)
    args = [nc.dram_tensor(name, v.shape, mybir.dt.from_np(v.dtype), kind="ExternalInput").ap()
            for name, v in arrays.items()]
    args.append(nc.dram_tensor("out_t", (P, KD, T1), F32, kind="ExternalOutput").ap())
    program(nc, *args)
    got = _run(nc, [arrays], core_ids=[0]).results[0]["out_t"]
    return _np.ascontiguousarray(_np.asarray(got).transpose(2, 1, 0).reshape(1, T1, D))
```

```python
from contextlib import ExitStack

import numpy as np

import concourse.bass as bass
from concourse import mybir

F32 = mybir.dt.float32
ALU = mybir.AluOpType
ACT = mybir.ActivationFunctionType
AX = mybir.AxisListType.X

P = 128
D = 1024
KD = D // P
T1 = 512
META = 16
T2 = T1 + META
RING = 4
NEG = -1e30
TAKEN = -3e38
AWAY = 1e6

QL, KVL = 384, 256
HEADS = 8
NOPE, ROPE_D = 64, 32
HD = 64
TOPK = 128
N_EXP, FF = 32, 256
GROUPS = 8
TAPS = 31
D_FF = 2816
NF = D_FF // P
ALPHA = 2.0 ** 0.25
RH = 16
CH = 64

SLAB_COUNTS = [
    ("c_q", 3), ("c_kv", 2), ("q_b", 4), ("k_b", 4), ("q_i", 4), ("k_i", 1), ("k_r", 1),
    ("g_a", 8), ("g_b", 8), ("v_b", 4), ("w_uq", 3), ("w_uk", 2), ("w_uv", 1),
    ("w_o_a", 4), ("w_o_b", 4), ("w_out", 8),
    ("conv_in", 16), ("rw_r", 8), ("rw_k", 8), ("rw_v", 8), ("rw_wa", 1), ("rw_g", 2),
    ("gate_a", 8), ("conv_out", 8), ("wa_up", 1),
    ("g_up", 2), ("gate_b", 8), ("rw_out", 8), ("w_o2", 8), ("ffn_up", 2 * NF), ("ffn_down", NF),
]
SLAB0, _n = {}, 0
for _name, _c in SLAB_COUNTS:
    SLAB0[_name] = _n
    _n += _c
N_SLABS = _n

PARAM_COLS = [
    ("norm_mix_g", 8), ("mla_q_norm_g", 3), ("mla_kv_norm_g", 2), ("norm_ffn_g", 8), ("final_norm_g", 8),
    ("ln_in_g", 8), ("ln_in_b", 8), ("b_gate", 16), ("conv_dw", 8 * TAPS), ("conv_dw_b", 8),
    ("conv_ln_g", 8), ("conv_ln_b", 8), ("mu", 27), ("w0", 8), ("a0", 8), ("k_k", 8), ("k_a", 8),
    ("r_k", 8), ("lnx_g", 8), ("lnx_b", 8), ("ln1_g", 8), ("ln1_b", 8), ("ffn_dw", 3 * 2 * NF),
    ("ln2_g", 8), ("ln2_b", 8), ("router", 8 * 40), ("w_i", 64), ("meta", 8 * META),
]
PCOL, _n = {}, 0
for _name, _c in PARAM_COLS:
    PCOL[_name] = _n
    _n += _c
N_PARAMS = _n

CONST0 = [("ident", P), ("mean1024", P), ("ones64", P), ("mean64", P), ("eps", 4)]
CONST1 = [("mean384", P), ("mean256", P), ("rot64", P), ("rot96", P), ("cos64", T1), ("sin64", T1),
          ("cos96", T1), ("sin96", T1), ("causal", T1), ("rev8", 8), ("rev32", 32),
          ("before", P), ("ones", P), ("iota", P)]
CONST2 = [("levels", 6 * P), ("level0_low", P), ("strict", P), ("incl", P), ("resets", T2)]


def offsets(table):
    out, n = {}, 0
    for name, c in table:
        out[name] = n
        n += c
    return out, n


C0, N0 = offsets(CONST0)
C1, N1 = offsets(CONST1)
C2, N2 = offsets(CONST2)
EPS_RMS, EPS_LN, EPS_GN = 0, 1, 2


def shape_constants():
    f = np.float32
    eye = np.eye(P, dtype=f)
    blk = np.kron(np.eye(2, dtype=f), np.ones((64, 64), f))
    c0 = np.zeros((P, N0), f)
    c0[:, C0["ident"]:][:, :P] = eye
    c0[:, C0["mean1024"]:][:, :P] = 1.0 / D
    c0[:, C0["ones64"]:][:, :P] = blk
    c0[:, C0["mean64"]:][:, :P] = blk / 64
    c0[:, C0["eps"]:][:, :4] = np.array([1e-6, 1e-5, 64e-5, 0], f)
    c1 = np.zeros((P, N1), f)
    c1[:, C1["mean384"]:][:, :P] = f(1.0 / QL)
    c1[:, C1["mean256"]:][:, :P] = f(1.0 / KVL)

    def rotation(starts, rot):
        half = rot // 2
        m, cos, sin = np.zeros((P, P), f), np.ones((P, T1), f), np.zeros((P, T1), f)
        inv = (f(500000.0) ** (-np.arange(half, dtype=f) * f(2.0) / f(rot))).astype(f)
        ang = (np.arange(T1, dtype=f)[:, None] * inv[None, :]).astype(f)
        for s in starts:
            for i in range(half):
                m[s + i + half, s + i] = -1.0
                m[s + i, s + i + half] = 1.0
                for r in (s + i, s + i + half):
                    cos[r], sin[r] = np.cos(ang[:, i]), np.sin(ang[:, i])
        return m, cos, sin

    for name, starts, rot in (("64", (0, 64), 16), ("96", (64,), 32)):
        m, cos, sin = rotation(starts, rot)
        c1[:, C1["rot" + name]:][:, :P] = m
        c1[:, C1["cos" + name]:][:, :T1] = cos
        c1[:, C1["sin" + name]:][:, :T1] = sin
    c1[0:64, C1["causal"] + T1 - 64:C1["causal"] + T1] = NEG
    c1[:, C1["rev8"]:][:, :8] = np.arange(8, 0, -1)
    c1[:, C1["rev32"]:][:, :32] = np.arange(32, 0, -1)
    c1[:, C1["before"]:][:, :P] = np.arange(P)[:, None] < np.arange(P)[None, :]
    c1[:, C1["ones"]:][:, :P] = 1.0
    c1[:, C1["iota"]:][:, :P] = np.arange(P)
    c2 = np.zeros((P, N2), f)
    s, t = np.arange(P)[:, None], np.arange(P)[None, :]
    for l in range(6):
        b = 1 << l
        c2[:, C2["levels"] + l * P:][:, :P] = (s // (2 * b) == t // (2 * b)) & (s // b % 2 == 0) & (t // b % 2 == 1)
    c2[:, C2["level0_low"]:][:, :P] = c2[:, C2["levels"]:][:, :P].T
    c2[:, C2["strict"]:][:, :P] = (s // CH == t // CH) & (s < t)
    c2[:, C2["incl"]:][:, :P] = (s // CH == t // CH) & (s <= t)
    c2[:, C2["resets"]:][:, :T2] = np.arange(T2)[None, :] % CH != 0
    return c0, c1, c2


def blocks(w, width=P, rows=None):
    k, n = w.shape
    kt, nt = -(-k // P), -(-n // width)
    full = np.zeros((kt * P, nt, P), w.dtype)
    padded = np.zeros((kt * P, nt * width), w.dtype)
    padded[:k, :n] = w
    full[:, :, :width] = padded.reshape(kt * P, nt, width)
    b = full.reshape(kt, P, nt, P).transpose(2, 0, 1, 3).reshape(nt * kt, P, P)
    pad = -b.shape[0] % 8
    if pad:
        b = np.concatenate([b, np.zeros((pad, P, P), w.dtype)])
    return b.reshape(-1, 8, P, P).transpose(0, 2, 1, 3).reshape(-1, P, 8 * P)


def rows512(w):
    pad = -w.shape[0] % 256
    w = np.concatenate([w, np.zeros((pad, w.shape[1]), w.dtype)]) if pad else w
    return w.reshape(-1, 2, P, 512).transpose(0, 2, 1, 3).reshape(-1, P, 1024)


def lay_out(a):
    w_in, w2 = a["w_in"][0], a["w_in_2"][0]
    o = np.cumsum([0, QL, KVL, ROPE_D, 512, 512, 512, 512, HD, HEADS, D, D])
    part = [w_in[:, o[i]:o[i + 1]] for i in range(11)]
    c = 2 * D
    s = {"c_q": blocks(part[0]), "c_kv": blocks(part[1]),
         "k_r": blocks(w_in[:, o[2] - 64:o[3]], width=96),
         "q_b": blocks(part[3]), "k_b": blocks(part[4]), "v_b": rows512(part[5]),
         "q_i": blocks(part[6]), "k_i": blocks(np.concatenate([part[7], part[7]], 1)),
         "g_a": blocks(part[9]), "g_b": blocks(part[10]),
         "w_uq": blocks(a["w_uq"][0], width=96), "w_uk": blocks(a["w_uk"][0], width=64),
         "w_uv": rows512(a["w_uv"][0]),
         "w_o_a": blocks(a["w_o_a"][0]), "w_o_b": blocks(a["w_o_b"][0]), "w_out": blocks(a["w_out"][0]),
         "conv_in": blocks(w2[:, :c]).reshape(2, 8, P, 1024).transpose(1, 0, 2, 3).reshape(16, P, 1024),
         "rw_r": blocks(w2[:, c:c + D]), "rw_k": blocks(w2[:, c + D:c + 2 * D]),
         "rw_v": blocks(w2[:, c + 2 * D:c + 3 * D]),
         "rw_wa": blocks(w2[:, c + 3 * D:c + 3 * D + P]),
         "rw_g": blocks(w2[:, c + 3 * D + P:c + 3 * D + P + 160]),
         "gate_a": blocks(w2[:, 5408:5408 + D]), "gate_b": blocks(w2[:, 5408 + D:5408 + 2 * D]),
         "conv_out": blocks(a["w_conv_out_2"][0]),
         "wa_up": np.concatenate([a["w_decay_up_2"][0], a["a_up_2"][0]])[None],
         "g_up": np.concatenate([a["g_up_2"][0], np.zeros((96, D), w2.dtype)]).reshape(2, P, D),
         "rw_out": blocks(a["w_rwkv_out_2"][0]), "w_o2": blocks(a["w_o_2"][0]),
         "ffn_down": blocks(a["ffn_down_2"][0])}
    up = blocks(a["ffn_up_2"][0])
    s["ffn_up"] = up.reshape(2, NF, P, 1024).transpose(1, 0, 2, 3).reshape(2 * NF, P, 1024)
    gate_up = np.concatenate([a["w_gate"][0], a["w_up"][0]], 2).reshape(N_EXP, 4, 2, P, 2 * FF)
    gate_up = gate_up.transpose(0, 1, 3, 2, 4).reshape(N_EXP, 4, P, 1024)
    moe = np.concatenate([gate_up, a["w_down"][0].reshape(N_EXP, 2, P, D)], 1).reshape(-1, P, 1024)
    for name, n in SLAB_COUNTS:
        assert s[name].shape == (n, P, 1024), (name, s[name].shape)
    slabs = np.concatenate([s[name] for name, _ in SLAB_COUNTS])

    def col(v):
        v = np.asarray(v).reshape(-1)
        pad = -v.size % P
        v = np.concatenate([v, np.zeros(pad, v.dtype)]) if pad else v
        return v.reshape(-1, P).T

    mu = a["rwkv_mu_2"][0]
    cols = {n: col(a[n]) for n in ("norm_mix_g", "mla_q_norm_g", "mla_kv_norm_g", "norm_ffn_g", "final_norm_g")}
    for n in ("ln_in_g", "ln_in_b", "b_gate", "conv_dw_b", "conv_ln_g", "conv_ln_b", "w0", "a0", "k_k", "k_a",
              "r_k", "lnx_g", "lnx_b", "ln1_g", "ln1_b", "ln2_g", "ln2_b"):
        cols[n] = col(a[n + "_2"])
    cols["mu"] = col(mu)
    cols["conv_dw"] = a["conv_dw_2"][0].reshape(TAPS, 8, P).transpose(2, 1, 0).reshape(P, -1)
    cols["ffn_dw"] = a["ffn_dw_2"][0].reshape(3, 2 * NF, P).transpose(2, 1, 0).reshape(P, -1)
    r = np.concatenate([a["w_router_group"][0], a["w_router_expert"][0]], 1)
    cols["router"] = r.reshape(8, P, 40).transpose(1, 0, 2).reshape(P, -1)
    cols["w_i"] = part[8].reshape(8, P, 8).transpose(1, 0, 2).reshape(P, -1)
    cols["meta"] = a["meta_tokens_2"].reshape(META, 8, P).transpose(2, 1, 0).reshape(P, -1)
    for name, n in PARAM_COLS:
        assert cols[name].shape == (P, n), (name, cols[name].shape)
    params = np.concatenate([cols[name] for name, _ in PARAM_COLS], 1)
    c0, c1, c2 = shape_constants()
    return {
        "x_t": np.ascontiguousarray(a["x"][0].reshape(T1, 8, P).transpose(2, 1, 0)),
        "slabs": slabs, "moe_slabs": moe, "params": np.ascontiguousarray(params),
        "router_bias": np.concatenate([a["b_router_group"][0], a["b_router_expert"][0]])[None],
        "const0": c0, "const1": c1, "const2": c2,
    }


def halves(t):
    return [(0, t)] if t <= 512 else [(0, t // 2), (t // 2, t)]


def fold(ap, t):
    return ap.rearrange("p (h w) -> p h w", h=len(halves(t)))


def program(nc, x_t, slabs, moe_slabs, params_d, router_bias, const0, const1, const2, out):
    top = ExitStack()
    with top:
        count = [0]

        def sem(name):
            count[0] += 1
            return top.enter_context(nc.semaphore(name))

        def sbt(ctx, name, shape):
            return ctx.enter_context(nc.sbuf_tensor(name, shape, F32))

        def block():
            return nc.Block(no_gpsimd_drain=True)

        h_d = nc.dram_tensor("h_spill", [P, KD, T2], F32, kind="Internal").ap()
        y_d = nc.dram_tensor("y_spill", [P, KD, T2], F32, kind="Internal").ap()

        acc = [top.enter_context(nc.psum_tensor(f"acc{j}", [P, 2, 512], F32)) for j in range(4)]
        ring = [sbt(top, f"ring{j}", [P, 1024]) for j in range(RING)]
        par = sbt(top, "par", [P, N_PARAMS])
        c0 = sbt(top, "c0", [P, N0])
        slab_in = [sem(f"slab_in{j}") for j in range(RING)]
        slab_used = sem("slab_used")
        chains = {e: [sem(f"{e}_chain"), 0] for e in ("dve", "act", "pool")}

        def link(e, eng, ins):
            c = chains[e]
            c[1] += 1
            ins.then_inc(c[0], 1)
            eng.wait_ge(c[0], c[1])

        def k0(name, n=P, at=0):
            return c0[:, C0[name] + at:C0[name] + at + n]

        def pcol(name, k, rows=P):
            return par[0:rows, PCOL[name] + k:PCOL[name] + k + 1]

        def A(j, t, rows=P, r0=0):
            n = len(halves(t))
            return acc[j][r0:r0 + rows, 0:n, 0:t // n]

        issued, used = [0], [0]
        freed_by = {}

        def slab_done(mm, n):
            used[0] += 1
            freed_by[n] = (slab_used, used[0])
            mm.then_inc(slab_used, 1)


        def load_slabs(sp, name=None):
            if name is None:
                stop = RING
            else:
                i = [n for n, _ in SLAB_COUNTS].index(name)
                stop = min(SLAB0[name] + SLAB_COUNTS[i][1] + RING, N_SLABS)
            for n in range(issued[0], stop):
                if n >= RING:
                    sp.wait_ge(*freed_by[n - RING])
                sp.dma_start(ring[n % RING][:, :], slabs[n]).then_inc(slab_in[n % RING], 16)
            issued[0] = stop

        def slab_wait(pe, n):
            pe.wait_ge(slab_in[n % RING], 16 * (n // RING + 1))

        def pe_tiles(pe, name, kt, nt, rhs, t, ready, freed, rows=P, acc0=0, na=4, first=0, krows=None):
            n_blocks = nt * kt
            for i in range(nt):
                j = acc0 + (first + i) % na
                if first + i >= na:
                    pe.wait_ge(freed, first + i - na + 1)
                for k in range(kt):
                    b = i * kt + k
                    n, at = SLAB0[name] + b // 8, b % 8 * P
                    if b % 8 == 0:
                        slab_wait(pe, n)
                    kr = P if krows is None else krows(k)
                    for s, (lo, hi) in enumerate(halves(t)):
                        mm = nc.tensor.matmul(acc[j][0:rows, s, 0:hi - lo], ring[n % RING][0:kr, at:at + rows],
                                              rhs(k)[0:kr, lo:hi], start=(k == 0), stop=(k == kt - 1))
                    last = b % 8 == 7 or b == n_blocks - 1
                    if k == kt - 1:
                        mm.then_inc(ready, 1)
                        if last:
                            freed_by[n] = (ready, first + i + 1)
                    elif last:
                        slab_done(mm, n)

        norm_sems = [sem("norm_" + n) for n in ("summed", "centred", "squared", "sq_used", "rooted", "scaled")]
        norm_base = [0] * len(norm_sems)

        def normalize(tag, src, dst, kt, t, mean, gain, bias=None, eps=EPS_RMS, func=None):
            centre = bias is not None
            summed, centred, squared, sq_used, rooted, scaled = norm_sems
            b_ = {id(s): norm_base[i] for i, s in enumerate(norm_sems)}
            for i, n in enumerate((1, kt, kt, kt, 1, kt)):
                norm_base[i] += n if centre or norm_sems[i] not in (summed, centred, scaled) else 0
            wait = lambda eng, s, n: eng.wait_ge(s, b_[id(s)] + n)
            with ExitStack() as ctx:
                sq = [sbt(ctx, f"{tag}_sq{i}", [P, t]) for i in range(4)]
                std = sbt(ctx, tag + "_std", [P, t])
                rstd = sbt(ctx, tag + "_rstd", [P, t])
                with block() as b:
                    @b.tensor
                    def _(pe):
                        if centre:
                            for k in range(kt):
                                for s, (lo, hi) in enumerate(halves(t)):
                                    mm = nc.tensor.matmul(acc[0][:, s, 0:hi - lo], mean, src(k)[:, lo:hi],
                                                          start=(k == 0), stop=(k == kt - 1))
                            mm.then_inc(summed, 1)
                        for k in range(kt):
                            wait(pe, squared, k + 1)
                            for s, (lo, hi) in enumerate(halves(t)):
                                mm = nc.tensor.matmul(acc[1][:, s, 0:hi - lo], mean, sq[k % 4][:, lo:hi],
                                                      start=(k == 0), stop=(k == kt - 1))
                            mm.then_inc(sq_used, 1)

                    @b.scalar
                    def _(act):
                        for k in range(kt):
                            if centre:
                                wait(act, centred, k + 1)
                            if k >= 4:
                                wait(act, sq_used, k - 3)
                            nc.scalar.activation(sq[k % 4][:, :], (dst if centre else src)(k),
                                                 ACT.Square).then_inc(squared, 1)
                        wait(act, sq_used, kt)
                        nc.scalar.activation(fold(std[:, :], t), A(1, t), ACT.Sqrt,
                                             bias=k0("eps", 1, eps)).then_inc(rooted, 1)
                        if centre:
                            for k in range(kt):
                                wait(act, scaled, k + 1)
                                nc.scalar.activation(dst(k), dst(k), func or ACT.Identity, scale=gain(k),
                                                     bias=bias(k))

                    @b.vector
                    def _(dve):
                        if centre:
                            wait(dve, summed, 1)
                            for k in range(kt):
                                nc.vector.tensor_tensor(fold(dst(k), t), fold(src(k), t), A(0, t),
                                                        ALU.subtract).then_inc(centred, 1)
                        wait(dve, rooted, 1)
                        link("dve", dve, nc.vector.reciprocal(rstd[:, :], std[:, :]))
                        if centre:
                            wait(dve, centred, kt)
                            wait(dve, squared, kt)
                            for k in range(kt):
                                nc.vector.tensor_tensor(dst(k), dst(k), rstd[:, :], ALU.mult).then_inc(scaled, 1)
                        else:
                            for k in range(kt):
                                nc.vector.scalar_tensor_tensor(out=dst(k), in0=src(k), scalar=gain(k),
                                                               in1=rstd[:, :], op0=ALU.mult, op1=ALU.mult)

        loaded = sem("inputs_loaded")

        def first_block(b1, xt):
            with ExitStack() as c1x:
                c1 = sbt(c1x, "c1", [P, N1])

                def k1(name, n=P, at=0):
                    return c1[:, C1[name] + at:C1[name] + at + n]

                h = sbt(c1x, "h", [P, KD, T1])

                with block() as b:
                    @b.sync
                    def _(sp):
                        sp.dma_start(xt[:, :, :], x_t).then_inc(loaded, 16)
                        sp.dma_start(c0[:, :], const0).then_inc(loaded, 16)
                        sp.dma_start(par[:, :], params_d).then_inc(loaded, 16)
                        sp.dma_start(c1[:, :], const1).then_inc(loaded, 16)
                        load_slabs(sp)
                        sp.wait_ge(loaded, 64)
                normalize("mix", lambda k: xt[:, k, :], lambda k: h[:, k, :], KD, T1, k0("mean1024"),
                          lambda k: pcol("norm_mix_g", k))
                with ExitStack() as att:
                    attention_part(att, xt, h, k1)
                normalize("ffn", lambda k: xt[:, k, :], lambda k: h[:, k, :], KD, T1, k0("mean1024"),
                          lambda k: pcol("norm_ffn_g", k))
                with ExitStack() as mx:
                    experts(mx, xt, h, k1)
            x2 = sbt(b1, "x2", [P, KD, T2])
            normalize("final", lambda k: xt[:, k, :], lambda k: x2[:, k, META:T2], KD, T1, k0("mean1024"),
                      lambda k: pcol("final_norm_g", k))
            return x2

        def attention_part(att, xt, h, k1):
            qb, kb = sbt(att, "qb", [P, 4, T1]), sbt(att, "kb", [P, 4, T1])
            qi, ki = sbt(att, "qi", [P, 4, T1]), sbt(att, "ki", [P, T1])
            vb, va = sbt(att, "vb", [P, 4, 512]), sbt(att, "va", [P, 4, 512])
            wi = sbt(att, "wi", [P, 4, HEADS])
            ga, gb = sbt(att, "ga", [P, KD, T1]), sbt(att, "gb", [P, KD, T1])
            cc = sbt(att, "cc", [P, 5, T1])
            kr = sbt(att, "kr", [P, T1])
            qa, ka = sbt(att, "qa", [P, HEADS, T1]), sbt(att, "ka", [P, HEADS, T1])
            sel = [None] + [sbt(att, f"sel{i}", [P, (i + 1) * P]) for i in range(1, 4)]
            dests = ([("c_q", cc[:, i, :], None) for i in range(3)] + [("c_kv", cc[:, 3 + i, :], None) for i in range(2)]
                     + [("q_b", qb[:, i, :], None) for i in range(4)] + [("k_b", kb[:, i, :], None) for i in range(4)]
                     + [("q_i", qi[:, i, :], None) for i in range(4)] + [("k_i", ki[:, :], None)]
                     + [("k_r", kr[0:96, :], None)]
                     + [("g_a", ga[:, i, :], ACT.Sigmoid) for i in range(8)]
                     + [("g_b", gb[:, i, :], ACT.Sigmoid) for i in range(8)])
            tile_ready, tile_out = sem("in_ready"), sem("in_out")
            v_ready, v_out = sem("vb_ready"), sem("vb_out")
            with block() as b:
                @b.tensor
                def _(pe):
                    i = 0
                    for name, n in SLAB_COUNTS[:9]:
                        pe_tiles(pe, name, KD, n, lambda k: h[:, k, :], T1, tile_ready, tile_out,
                                 rows=96 if name == "k_r" else P, first=i)
                        i += n
                    pe.wait_ge(tile_out, i)
                    for k in range(KD):
                        n = SLAB0["v_b"] + k // 2
                        if k % 2 == 0:
                            slab_wait(pe, n)
                        for tok in range(4):
                            mm = nc.tensor.matmul(acc[tok][:, 0, :], h[:, k, tok * P:(tok + 1) * P],
                                                  ring[n % RING][:, k % 2 * 512:k % 2 * 512 + 512],
                                                  start=(k == 0), stop=(k == KD - 1))
                        if k % 2:
                            slab_done(mm, n)
                    for tok in range(4):
                        for k in range(KD):
                            o = PCOL["w_i"] + 8 * k
                            mm = nc.tensor.matmul(acc[tok][:, 1, 0:8], h[:, k, tok * P:(tok + 1) * P],
                                                  par[:, o:o + 8], start=(k == 0), stop=(k == KD - 1))
                        mm.then_inc(v_ready, 1)

                @b.scalar
                def _(act):
                    for i, (name, d, f) in enumerate(dests):
                        act.wait_ge(tile_ready, i + 1)
                        rows = 96 if name == "k_r" else P
                        nc.scalar.activation(d, acc[i % 4][0:rows, 0, :], f or ACT.Copy).then_inc(tile_out, 1)
                    for tok in range(4):
                        act.wait_ge(v_ready, tok + 1)
                        nc.scalar.activation(vb[:, tok, :], acc[tok][:, 0, :], ACT.Copy)
                        nc.scalar.activation(wi[:, tok, :], acc[tok][:, 1, 0:8], ACT.Copy, scale=HEADS ** -0.5)

                @b.sync
                def _(sp):
                    load_slabs(sp, "v_b")

            normalize("cq", lambda k: cc[:, k, :], lambda k: cc[:, k, :], 3, T1, k1("mean384"),
                      lambda k: pcol("mla_q_norm_g", k))
            normalize("ckv", lambda k: cc[:, 3 + k, :], lambda k: cc[:, 3 + k, :], 2, T1, k1("mean256"),
                      lambda k: pcol("mla_kv_norm_g", k))
            up_ready, up_out, va_ready = sem("up_ready"), sem("up_out"), sem("va_ready")
            with block() as b:
                @b.tensor
                def _(pe):
                    pe_tiles(pe, "w_uq", 3, HEADS, lambda k: cc[:, k, :], T1, up_ready, up_out, rows=96)
                    pe_tiles(pe, "w_uk", 2, HEADS, lambda k: cc[:, 3 + k, :], T1, up_ready, up_out, rows=64, first=8)
                    pe.wait_ge(up_out, 16)
                    n = SLAB0["w_uv"]
                    slab_wait(pe, n)
                    for tok in range(4):
                        for k in range(2):
                            mm = nc.tensor.matmul(acc[tok][:, 0, :], cc[:, 3 + k, tok * P:(tok + 1) * P],
                                                  ring[n % RING][:, k * 512:k * 512 + 512],
                                                  start=(k == 0), stop=(k == 1))
                        mm.then_inc(va_ready, 1)
                    freed_by[n] = (va_ready, 4)

                @b.scalar
                def _(act):
                    for i in range(16):
                        act.wait_ge(up_ready, i + 1)
                        d, rows = (qa, 96) if i < 8 else (ka, 64)
                        nc.scalar.activation(d[0:rows, i % 8, :], acc[i % 4][0:rows, 0, :], ACT.Copy).then_inc(up_out, 1)
                    for tok in range(4):
                        act.wait_ge(va_ready, tok + 1)
                        nc.scalar.activation(va[:, tok, :], acc[tok][:, 0, :], ACT.Copy)

                @b.sync
                def _(sp):
                    load_slabs(sp, "w_uv")

            rope_tiles = ([(qb[:, i, :], 0) for i in range(4)] + [(kb[:, i, :], 0) for i in range(4)]
                          + [(qi[:, i, :], 0) for i in range(4)] + [(ki[:, :], 0)]
                          + [(kr[0:96, :], 1)] + [(qa[0:96, i, :], 1) for i in range(8)])
            turned, cosed, sined, roped = sem("turned"), sem("cosed"), sem("sined"), sem("roped")
            with ExitStack() as rx, block() as b:
                prod = [sbt(rx, f"rope_prod{i}", [P, T1]) for i in range(2)]

                @b.tensor
                def _(pe):
                    for i, (x, kind) in enumerate(rope_tiles):
                        rows = 96 if kind else P
                        if i >= 4:
                            pe.wait_ge(sined, i - 3)
                        rot = k1("rot96" if kind else "rot64")
                        nc.tensor.matmul(acc[i % 4][0:rows, 0, :], rot[0:rows, 0:rows], x, start=True,
                                         stop=True).then_inc(turned, 1)

                @b.vector
                def _(dve):
                    for i, (x, kind) in enumerate(rope_tiles):
                        rows = 96 if kind else P
                        dve.wait_ge(turned, i + 1)
                        if i >= 2:
                            dve.wait_ge(roped, i - 1)
                        nc.vector.tensor_tensor(prod[i % 2][0:rows, :], acc[i % 4][0:rows, 0, :],
                                                k1("sin96" if kind else "sin64", T1)[0:rows, :],
                                                ALU.mult).then_inc(sined, 1)
                        nc.vector.tensor_tensor(x, x, k1("cos96" if kind else "cos64", T1)[0:rows, :],
                                                ALU.mult).then_inc(cosed, 1)

                @b.gpsimd
                def _(pool):
                    for i, (x, kind) in enumerate(rope_tiles):
                        rows = 96 if kind else P
                        pool.wait_ge(sined, i + 1)
                        pool.wait_ge(cosed, i + 1)
                        nc.gpsimd.tensor_tensor(x, x, prod[i % 2][0:rows, :], ALU.add).then_inc(roped, 1)
                    pool.wait_ge(roped, len(rope_tiles))
                    for hd in range(HEADS):
                        link("pool", pool, nc.gpsimd.tensor_copy(ka[64:96, hd, :], kr[64:96, :]))

            logit_ready, logit_out, rel_used = sem("logit_ready"), sem("logit_out"), sem("rel_used")
            score_seen = sem("score_seen")
            with ExitStack() as ix, block() as b:
                rel = [sbt(ix, f"rel{i}", [P, T1]) for i in range(4)]
                best = sbt(ix, "best", [P, 8])
                units = [(qt, hd) for qt in range(1, 4) for hd in range(HEADS)]

                @b.tensor
                def _(pe):
                    for u, (qt, hd) in enumerate(units):
                        nk, r0 = (qt + 1) * P, 64 * (hd % 2)
                        if u >= 4:
                            pe.wait_ge(logit_out, u - 3)
                        nc.tensor.matmul(acc[u % 4][:, 0, 0:nk], qi[r0:r0 + 64, hd // 2, qt * P:(qt + 1) * P],
                                         ki[r0:r0 + 64, 0:nk], start=True, stop=True).then_inc(logit_ready, 1)

                @b.scalar
                def _(act):
                    for u, (qt, hd) in enumerate(units):
                        nk = (qt + 1) * P
                        act.wait_ge(logit_ready, u + 1)
                        if u >= 4:
                            act.wait_ge(rel_used, u - 3)
                        nc.scalar.activation(rel[u % 4][:, 0:nk], acc[u % 4][:, 0, 0:nk], ACT.Relu,
                                             scale=HD ** -0.5).then_inc(logit_out, 1)

                @b.vector
                def _(dve):
                    for u, (qt, hd) in enumerate(units):
                        nk, s = (qt + 1) * P, sel[qt]
                        dve.wait_ge(logit_out, u + 1)
                        w = wi[:, qt, hd:hd + 1]
                        if hd == 0:
                            ins = nc.vector.tensor_scalar(s[:, :], rel[u % 4][:, 0:nk], w, None, ALU.mult)
                        else:
                            dve.wait_ge(rel_used, u)
                            ins = nc.vector.scalar_tensor_tensor(out=s[:, :], in0=rel[u % 4][:, 0:nk], scalar=w,
                                                                 in1=s[:, :], op0=ALU.mult, op1=ALU.add)
                        ins.then_inc(rel_used, 1)
                        if hd < HEADS - 1:
                            continue
                        dve.wait_ge(rel_used, u + 1)
                        link("dve", dve, nc.vector.memset(s[0:64, nk - 64:nk], NEG))
                        for _r in range(TOPK // 8):
                            link("dve", dve, nc.vector.max(best[:, :], s[:, :]))
                            link("dve", dve, nc.vector.match_replace(s[:, :], best[:, :], s[:, :], TAKEN))
                        link("dve", dve, nc.vector.tensor_scalar(s[:, :], s[:, :], TAKEN / 2, NEG, ALU.is_gt, ALU.mult))

            oa, ob = cc, qi
            causal = lambda qt: k1("causal", (qt + 1) * P, T1 - (qt + 1) * P)
            attend("mla", lambda hd, lo, hi: qa[0:96, hd, lo:hi], lambda hd, n: ka[0:96, hd, 0:n], va,
                   causal, (NOPE + ROPE_D) ** -0.5, oa)
            attend("dsa", lambda hd, lo, hi: qb[64 * (hd % 2):64 * (hd % 2) + 64, hd // 2, lo:hi],
                   lambda hd, n: kb[64 * (hd % 2):64 * (hd % 2) + 64, hd // 2, 0:n], vb,
                   lambda qt: sel[qt][:, :] if qt else causal(0), HD ** -0.5, ob)
            oy_ready, oy_out, y_sum = sem("oy_ready"), sem("oy_out"), sem("y_sum")
            with block() as b:
                @b.tensor
                def _(pe):
                    pe_tiles(pe, "w_o_a", 4, KD, lambda k: oa[:, k, :], T1, oy_ready, oy_out)
                    pe_tiles(pe, "w_o_b", 4, KD, lambda k: ob[:, k, :], T1, oy_ready, oy_out, first=8)

                @b.vector
                def _(dve):
                    for i in range(16):
                        dve.wait_ge(oy_ready, i + 1)
                        d, g = (h, ga) if i < 8 else (gb, gb)
                        nc.vector.tensor_tensor(d[:, i % 8, :], acc[i % 4][:, 0, :], g[:, i % 8, :],
                                                ALU.mult).then_inc(oy_out, 1)

                @b.gpsimd
                def _(pool):
                    for i in range(8):
                        pool.wait_ge(oy_out, 9 + i)
                        link("pool", pool, nc.gpsimd.tensor_tensor(h[:, i, :], h[:, i, :], gb[:, i, :], ALU.add))

                @b.sync
                def _(sp):
                    load_slabs(sp, "w_o_b")
            xo_ready, xo_out = sem("xo_ready"), sem("xo_out")
            with block() as b:
                @b.tensor
                def _(pe):
                    pe_tiles(pe, "w_out", KD, KD, lambda k: h[:, k, :], T1, xo_ready, xo_out)

                @b.vector
                def _(dve):
                    for i in range(8):
                        dve.wait_ge(xo_ready, i + 1)
                        nc.vector.tensor_tensor(xt[:, i, :], xt[:, i, :], acc[i % 4][:, 0, :],
                                                ALU.add).then_inc(xo_out, 1)

                @b.sync
                def _(sp):
                    load_slabs(sp, "w_out")

        attend_sems = [sem("att_" + n) for n in ("s_ready", "s_out", "probs", "scaled", "pt_ready", "pt_out", "o_ready", "o_out")]
        attend_base = [0]

        def attend(tag, q, key, v, bias, scale, o):
            s_ready, s_out, probs, scaled, pt_ready, pt_out, o_ready, o_out = attend_sems
            u0 = attend_base[0]
            attend_base[0] += 4 * HEADS
            units = [(qt, hd) for qt in range(4) for hd in range(HEADS)]
            NU = len(units)
            NS = 4
            with ExitStack() as ax, block() as b:
                sc = [sbt(ax, f"{tag}_sc{i}", [P, T1]) for i in range(NS)]
                pt = [sbt(ax, f"{tag}_pt{i}", [P, T1]) for i in range(2)]
                mx = sbt(ax, f"{tag}_mx", [P, NU])
                nm = sbt(ax, f"{tag}_nm", [P, NU])
                rs = sbt(ax, f"{tag}_rs", [P, NU])
                ri = sbt(ax, f"{tag}_ri", [P, NU])
                sbank = lambda u: acc[u % 4 // 2][:, u % 2, :]

                @b.tensor
                def _(pe):
                    def scores(u):
                        qt, hd = units[u]
                        if u >= 4:
                            pe.wait_ge(s_out, u0 + u - 3)
                        nc.tensor.matmul(sbank(u)[:, 0:(qt + 1) * P], q(hd, qt * P, (qt + 1) * P),
                                         key(hd, (qt + 1) * P), start=True, stop=True).then_inc(s_ready, 1)

                    def turn(u):
                        qt, hd = units[u]
                        pe.wait_ge(scaled, u0 + u + 1)
                        if u >= 2:
                            pe.wait_ge(pt_out, u0 + u - 1)
                        for kt in range(qt + 1):
                            mm = nc.tensor.transpose(acc[2][:, u % 2, kt * P:(kt + 1) * P],
                                                     sc[u % NS][:, kt * P:(kt + 1) * P], k0("ident"))
                        mm.then_inc(pt_ready, 1)

                    def values(u):
                        qt, hd = units[u]
                        r0 = 64 * (hd % 2)
                        pe.wait_ge(pt_out, u0 + u + 1)
                        if u >= 2:
                            pe.wait_ge(o_out, u0 + u - 1)
                        for kt in range(qt + 1):
                            mm = nc.tensor.matmul(acc[3][r0:r0 + 64, u % 2, 0:P], v[:, kt, hd * 64:hd * 64 + 64],
                                                  pt[u % 2][:, kt * P:(kt + 1) * P], start=(kt == 0), stop=(kt == qt))
                        mm.then_inc(o_ready, 1)

                    scores(0)
                    scores(1)
                    for u in range(NU + 1):
                        if u + 2 < NU:
                            scores(u + 2)
                        if u < NU:
                            turn(u)
                        if u >= 1:
                            values(u - 1)

                @b.vector
                def _(dve):
                    def add_bias(u):
                        nk = (units[u][0] + 1) * P
                        dve.wait_ge(s_ready, u0 + u + 1)
                        if u >= NS:
                            dve.wait_ge(pt_ready, u0 + u - NS + 1)
                        nc.vector.tensor_tensor_reduce(sc[u % NS][:, 0:nk], sbank(u)[:, 0:nk], bias(units[u][0]),
                                                       1.0, -3e38, ALU.add, ALU.max, mx[:, u:u + 1]).then_inc(s_out, 1)

                    def normal(u):
                        nk = (units[u][0] + 1) * P
                        dve.wait_ge(probs, u0 + u + 1)
                        link("dve", dve, nc.vector.reciprocal(ri[:, u:u + 1], rs[:, u:u + 1]))
                        nc.vector.tensor_scalar(sc[u % NS][:, 0:nk], sc[u % NS][:, 0:nk], ri[:, u:u + 1], None,
                                                ALU.mult).then_inc(scaled, 1)

                    add_bias(0)
                    for u in range(NU):
                        if u + 1 < NU:
                            add_bias(u + 1)
                        normal(u)

                @b.scalar
                def _(act):
                    def exps(u):
                        nk = (units[u][0] + 1) * P
                        act.wait_ge(s_out, u0 + u + 1)
                        link("act", act, nc.scalar.activation(nm[:, u:u + 1], mx[:, u:u + 1], ACT.Copy, scale=-scale))
                        nc.scalar.activation(sc[u % NS][:, 0:nk], sc[u % NS][:, 0:nk], ACT.Exp, bias=nm[:, u:u + 1],
                                             scale=scale, accum_out=rs[:, u:u + 1]).then_inc(probs, 1)

                    def evacuate(u):
                        nk = (units[u][0] + 1) * P
                        act.wait_ge(pt_ready, u0 + u + 1)
                        if u >= 2:
                            act.wait_ge(o_ready, u0 + u - 1)
                        nc.scalar.activation(pt[u % 2][:, 0:nk], acc[2][:, u % 2, 0:nk], ACT.Copy).then_inc(pt_out, 1)

                    def store(u):
                        qt, hd = units[u]
                        r0 = 64 * (hd % 2)
                        act.wait_ge(o_ready, u0 + u + 1)
                        nc.scalar.activation(o[r0:r0 + 64, hd // 2, qt * P:(qt + 1) * P], acc[3][r0:r0 + 64, u % 2, 0:P],
                                             ACT.Copy).then_inc(o_out, 1)

                    exps(0)
                    for u in range(NU + 1):
                        if u + 1 < NU:
                            exps(u + 1)
                        if u < NU:
                            evacuate(u)
                        if u >= 1:
                            store(u - 1)

        def route(h, k1, h_tok, comb, rank, passes):
            logits_ready, biased, hot_made, ranked = sem("rt_logits"), sem("rt_biased"), sem("rt_hot"), sem("rt_ranked")
            shifted, exped, paired, exped2 = sem("rt_shifted"), sem("rt_exped"), sem("rt_paired"), sem("rt_exped2")
            turned, copied = sem("rt_turned"), sem("rt_copied")
            with ExitStack() as rx, block() as b:
                rb = sbt(rx, "rt_bias", [P, 40])
                lg = sbt(rx, "rt_lg", [P, 4, 40])
                df, e1 = sbt(rx, "rt_df", [P, 4, 8]), sbt(rx, "rt_e1", [P, 4, 8])
                g8, hot = sbt(rx, "rt_g8", [P, 4, 8]), sbt(rx, "rt_hot8", [P, 4, 8])
                t32, a32, b32 = (sbt(rx, f"rt_{n}32", [P, 4, 32]) for n in "tab")
                small = sbt(rx, "rt_small", [P, 10, 4])
                cnt = sbt(rx, "rt_cnt", [P, 4])

                def bc(i, n):
                    return small[:, i, :].unsqueeze(2).to_broadcast([P, 4, n])

                @b.sync
                def _(sp):
                    sp.dma_start(rb[:, :], router_bias.to_broadcast([P, 40])).then_inc(biased, 16)
                    sp.wait_ge(biased, 16)

                @b.tensor
                def _(pe):
                    for tok in range(4):
                        for k in range(KD):
                            o = PCOL["router"] + 40 * k
                            mm = nc.tensor.matmul(acc[tok][:, 0, 0:40], h[:, k, tok * P:(tok + 1) * P],
                                                  par[:, o:o + 40], start=(k == 0), stop=(k == KD - 1))
                        mm.then_inc(logits_ready, 1)
                    for i in range(8):
                        if i >= 4:
                            pe.wait_ge(copied, i - 3)
                        tok, half = i // 2, i % 2
                        for q in range(4):
                            mm = nc.tensor.transpose(acc[i % 4][:, 1, q * P:(q + 1) * P],
                                                     h[:, 4 * half + q, tok * P:(tok + 1) * P], k0("ident"))
                        mm.then_inc(turned, 1)
                    pe.wait_ge(hot_made, 1)
                    for tok in range(4):
                        for t in range(tok + 1):
                            nc.tensor.matmul(acc[0][:, 0, 8 * tok:8 * tok + 8], k1("before" if t == tok else "ones"),
                                             hot[:, t, :], start=(t == 0), stop=(t == tok))
                    for t in range(4):
                        mm = nc.tensor.matmul(acc[0][:, 0, 32:40], k1("ones"), hot[:, t, :], start=(t == 0), stop=(t == 3))
                    mm.then_inc(ranked, 1)

                @b.vector
                def _(dve):
                    v = nc.vector
                    L = lambda ins: link("dve", dve, ins)
                    dve.wait_ge(biased, 16)
                    for tok in range(4):
                        dve.wait_ge(logits_ready, tok + 1)
                        L(v.tensor_tensor(lg[:, tok, :], acc[tok][:, 0, 0:40], rb[:, :], ALU.add))
                    G = lg[:, :, 0:8]
                    row = lambda i: small[:, i, :]

                    def first_best(x, top, n, rev, tmp, best, signal=None):
                        L(v.tensor_reduce(row(top), x, AX, ALU.max))
                        L(v.tensor_tensor(tmp, x, bc(top, n), ALU.is_equal))
                        L(v.tensor_tensor(tmp, tmp, rev.unsqueeze(1).to_broadcast([P, 4, n]), ALU.mult))
                        L(v.tensor_reduce(row(9), tmp, AX, ALU.max))
                        ins = v.tensor_tensor(best, tmp, bc(9, n), ALU.is_equal)
                        if signal is None:
                            L(ins)
                        else:
                            ins.then_inc(signal, 1)
                            dve.wait_ge(signal, 1)

                    first_best(G, 0, 8, k1("rev8", 8), g8[:, :, :], hot[:, :, :], hot_made)
                    v.tensor_tensor(df[:, :, :], G, bc(0, 8), ALU.subtract).then_inc(shifted, 1)
                    L(v.tensor_scalar(g8[:, :, :], hot[:, :, :], -NEG, NEG, ALU.mult, ALU.add))
                    for tok in range(4):
                        L(v.tensor_tensor(comb[:, tok, :].rearrange("p (g e) -> p g e", g=8),
                                          lg[:, tok, 8:40].rearrange("p (g e) -> p g e", g=8),
                                          g8[:, tok, :].unsqueeze(2).to_broadcast([P, 8, 4]), ALU.add))
                    first_best(comb[:, :, :], 1, 32, k1("rev32", 32), t32[:, :, :], a32[:, :, :])
                    L(v.tensor_scalar(t32[:, :, :], a32[:, :, :], 2 * NEG, None, ALU.mult))
                    L(v.tensor_tensor(comb[:, :, :], comb[:, :, :], t32[:, :, :], ALU.add))
                    first_best(comb[:, :, :], 2, 32, k1("rev32", 32), t32[:, :, :], b32[:, :, :])
                    v.tensor_tensor(row(3), row(2), row(1), ALU.subtract).then_inc(paired, 1)
                    dve.wait_ge(exped, 1)
                    L(v.tensor_reduce(row(4), e1[:, :, :], AX, ALU.add))
                    L(v.reciprocal(row(4), row(4)))
                    dve.wait_ge(exped2, 1)
                    L(v.tensor_scalar(row(6), row(5), 1.0, None, ALU.add))
                    L(v.reciprocal(row(6), row(6)))
                    L(v.tensor_tensor(row(6), row(6), row(4), ALU.mult))
                    L(v.tensor_tensor(row(7), row(6), row(5), ALU.mult))
                    L(v.tensor_tensor(a32[:, :, :], a32[:, :, :], bc(6, 32), ALU.mult))
                    L(v.tensor_tensor(b32[:, :, :], b32[:, :, :], bc(7, 32), ALU.mult))
                    L(v.tensor_tensor(comb[:, :, :], a32[:, :, :], b32[:, :, :], ALU.add))
                    dve.wait_ge(ranked, 1)
                    L(v.tensor_scalar(rank[:, :, 0:8], acc[0][:, 0, 0:32].rearrange("p (t g) -> p t g", t=4), AWAY, None, ALU.add))
                    L(v.tensor_tensor(rank[:, :, 0:8], rank[:, :, 0:8], hot[:, :, :], ALU.mult))
                    L(v.tensor_scalar(rank[:, :, 0:8], rank[:, :, 0:8], -AWAY, None, ALU.add))
                    L(v.tensor_scalar(rank[:, :, 8:9], rank[:, :, 0:1], -float(P), None, ALU.add))
                    L(v.tensor_reduce(cnt[:, 0:1], acc[0][:, 0, 32:40], AX, ALU.max))
                    for i in range(1, 4):
                        L(v.tensor_scalar(cnt[:, i:i + 1], cnt[:, 0:1], i * P + 0.5, None, ALU.is_gt))
                    L(v.tensor_reduce(cnt[:, 0:1], cnt[:, 1:4], AX, ALU.add))
                    L(v.tensor_scalar(passes[:, :], cnt[:, 0:1], 1.0, None, ALU.add))

                @b.scalar
                def _(act):
                    for i in range(8):
                        act.wait_ge(turned, i + 1)
                        nc.scalar.activation(h_tok[:, i // 2, i % 2 * 512:i % 2 * 512 + 512], acc[i % 4][:, 1, :],
                                             ACT.Copy).then_inc(copied, 1)
                    act.wait_ge(shifted, 1)
                    nc.scalar.activation(e1[:, :, :], df[:, :, :], ACT.Exp).then_inc(exped, 1)
                    act.wait_ge(paired, 1)
                    nc.scalar.activation(small[:, 5, :], small[:, 3, :], ACT.Exp).then_inc(exped2, 1)

        def experts(mx, xt, h, k1):
            h_tok = sbt(mx, "h_tok", [P, 4, D])
            comb, rank = sbt(mx, "comb", [P, 4, N_EXP]), sbt(mx, "rank", [P, 4, GROUPS + 1])
            passes = mx.enter_context(nc.sbuf_tensor("passes", [P, 1], mybir.dt.int32))
            route(h, k1, h_tok, comb, rank, passes)
            NR, PER = 12, 6
            per_group = 4 * PER
            slab_here = [sem(f"moe_in{j}") for j in range(NR)]
            gu_used, gu_done, dn_half, dn_done = sem("gu_used"), sem("gu_done"), sem("dn_half"), sem("dn_done")
            onehot, onehot_t, onehot_tc = sem("onehot_made"), sem("onehot_turned"), sem("onehot_copied")
            gathered, g_copied, c_ready, c_copied = sem("gathered"), sem("g_copied"), sem("c_ready"), sem("c_copied")
            silued, hid_made, hid_turned, hid_copied = sem("silued"), sem("hid_made"), sem("hid_turned"), sem("hid_copied")
            y_copied, scattered, added, moved_on = sem("y_copied"), sem("scattered"), sem("moe_added"), sem("moved_on")
            bank = lambda i: acc[i // 2][:, i % 2, :]
            SCAT = [5, 6, 7, 0]
            with ExitStack() as ex, block() as b:
                ringm = [sbt(ex, f"moe_ring{j}", [P, 1024]) for j in range(NR)]
                gm, gmt = sbt(ex, "onehot", [P, 4, P]), sbt(ex, "onehot_t", [P, T1])
                hg, ys = sbt(ex, "h_slots", [P, KD, P]), sbt(ex, "y_slots", [P, D])
                cs = sbt(ex, "comb_slots", [P, 4])
                sl, hid = [[sbt(ex, f"{n}{i}", [P, FF]) for i in range(2)] for n in ("silu", "hid")]
                hidt = [sbt(ex, f"hid_t{i}", [P, FF]) for i in range(2)]

                def groups(eng, body, end=None):
                    count = eng.value_load(passes[0:1, 0:1], min_val=1, max_val=T1 // P)
                    with eng.Fori(0, count) as ps:
                        with eng.Fori(0, GROUPS) as g:
                            body(ps * GROUPS + g, g)
                        if end:
                            end(ps)

                @b.sync
                def _(sp):
                    sp.sem_inc(gu_used, 6)
                    for s in (gu_done, dn_half, dn_done):
                        sp.sem_inc(s, 2)

                    def body(n, g):
                        for s in range(per_group):
                            e, i = s // PER, s % PER
                            if i < 3:
                                sp.wait_ge(gu_used, n * 12 + 3 * e + i + 1)
                            else:
                                sp.wait_ge((gu_done, dn_half, dn_done)[i - 3], n * 4 + e + 1)
                            sp.dma_start(ringm[s % NR][:, :], moe_slabs[bass.ds(g * per_group + s, 1)]
                                         .rearrange("a p n -> (a p) n")).then_inc(slab_here[s % NR], 16)

                    groups(sp, body)

                @b.tensor
                def _(pe):
                    mmul = nc.tensor.matmul

                    def body(n, g):
                        def slab(s):
                            pe.wait_ge(slab_here[s % NR], n * 32 + 16 * (s // NR + 1))
                            return ringm[s % NR]

                        def gate_up(e):
                            if e >= 2:
                                pe.wait_ge(hid_made, n * 4 + e - 1)
                            for i in range(4):
                                w = slab(e * PER + i)
                                for q in range(2):
                                    k = 2 * i + q
                                    mm = mmul(bank(e % 2), hg[:, k, :], w[:, q * 512:q * 512 + 512],
                                              start=(k == 0), stop=(k == KD - 1))
                                mm.then_inc(gu_done if i == 3 else gu_used, 1)

                        def turn(e):
                            pe.wait_ge(hid_made, n * 4 + e + 1)
                            if e == 0:
                                pe.wait_ge(c_copied, n + 1)
                            else:
                                pe.wait_ge(hid_copied, n * 4 + e)
                            for f in range(2):
                                mm = nc.tensor.transpose(bank(4)[:, f * P:(f + 1) * P], hid[e % 2][:, f * P:(f + 1) * P], k0("ident"))
                            mm.then_inc(hid_turned, 1)

                        def down(e):
                            pe.wait_ge(hid_copied, n * 4 + e + 1)
                            for f in range(2):
                                w = slab(e * PER + 4 + f)
                                for half in range(2):
                                    mm = mmul(bank(2 + half), hidt[e % 2][:, f * P:(f + 1) * P],
                                              w[:, half * 512:half * 512 + 512],
                                              start=(e == 0 and f == 0), stop=(e == 3 and f == 1))
                                mm.then_inc(dn_done if f == 1 else dn_half, 1)

                        pe.wait_ge(onehot, n + 1)
                        pe.wait_ge(added, n * KD + 1)
                        for k in range(KD):
                            for t in range(4):
                                mm = mmul(bank(5 + k // 4)[:, k % 4 * P:k % 4 * P + P], h_tok[:, t, k * P:(k + 1) * P],
                                          gm[:, t, :], start=(t == 0), stop=(t == 3))
                            if k % 4 == 3:
                                mm.then_inc(gathered, 1)
                        for t in range(4):
                            mm = mmul(bank(4)[:, 0:4], gm[:, t, :], comb[:, t, bass.ds(g * 4, 4)], start=(t == 0), stop=(t == 3))
                        mm.then_inc(c_ready, 1)
                        for t in range(4):
                            mm = nc.tensor.transpose(bank(7)[:, t * P:(t + 1) * P], gm[:, t, :], k0("ident"))
                        mm.then_inc(onehot_t, 1)
                        pe.wait_ge(g_copied, n * 2 + 2)
                        gate_up(0)
                        gate_up(1)
                        for e in range(4):
                            turn(e)
                            if e < 2:
                                gate_up(e + 2)
                            down(e)
                        pe.wait_ge(y_copied, n * 2 + 2)
                        pe.wait_ge(onehot_tc, n + 1)
                        for k in range(KD):
                            if k >= 4:
                                pe.wait_ge(added, n * KD + k - 2)
                            mmul(bank(SCAT[k % 4]), ys[:, k * P:(k + 1) * P], gmt[:, :], start=True, stop=True).then_inc(scattered, 1)

                    groups(pe, body)

                @b.scalar
                def _(act):
                    cp_ = lambda d, s_: nc.scalar.activation(d, s_, ACT.Copy)

                    def body(n, g):
                        for i in range(2):
                            act.wait_ge(gathered, n * 2 + i + 1)
                            cp_(hg[:, 4 * i:4 * i + 4, :].rearrange("p k s -> p (k s)"), bank(5 + i)).then_inc(g_copied, 1)
                        act.wait_ge(c_ready, n + 1)
                        cp_(cs[:, :], bank(4)[:, 0:4]).then_inc(c_copied, 1)
                        act.wait_ge(onehot_t, n + 1)
                        cp_(gmt[:, :], bank(7)).then_inc(onehot_tc, 1)

                        def silu(e):
                            act.wait_ge(gu_done, n * 4 + e + 3)
                            if e >= 2:
                                act.wait_ge(hid_made, n * 4 + e - 1)
                            nc.scalar.activation(sl[e % 2][:, :], bank(e % 2)[:, 0:FF], ACT.Silu).then_inc(silued, 1)

                        def turn(e):
                            act.wait_ge(hid_turned, n * 4 + e + 1)
                            cp_(hidt[e % 2][:, :], bank(4)[:, 0:FF]).then_inc(hid_copied, 1)

                        silu(0)
                        silu(1)
                        turn(0)
                        silu(2)
                        turn(1)
                        silu(3)
                        turn(2)
                        turn(3)
                        act.wait_ge(dn_done, n * 4 + 6)
                        for i in range(2):
                            cp_(ys[:, i * 512:i * 512 + 512], bank(2 + i)).then_inc(y_copied, 1)

                    groups(act, body)

                @b.vector
                def _(dve):
                    def make_onehot(col):
                        for t in range(4):
                            ins = nc.vector.tensor_scalar(gm[:, t, :], k1("iota"), rank[:, t, col], None, ALU.is_equal)
                        ins.then_inc(onehot, 1)

                    def body(n, g):
                        for e in range(4):
                            dve.wait_ge(silued, n * 4 + e + 1)
                            if e == 0:
                                dve.wait_ge(c_copied, n + 1)
                            if e >= 2:
                                dve.wait_ge(hid_turned, n * 4 + e - 1)
                            nc.vector.scalar_tensor_tensor(out=hid[e % 2][:, :], in0=sl[e % 2][:, :], scalar=cs[:, e:e + 1],
                                                           in1=bank(e % 2)[:, FF:2 * FF], op0=ALU.mult,
                                                           op1=ALU.mult).then_inc(hid_made, 1)
                        dve.wait_ge(onehot_t, n + 1)
                        make_onehot(bass.ds(g + 1, 1))
                        for k in range(KD):
                            dve.wait_ge(scattered, n * KD + k + 1)
                            nc.vector.tensor_tensor(xt[:, k, :], xt[:, k, :], bank(SCAT[k % 4]), ALU.add).then_inc(added, 1)

                    def next_pass(ps):
                        dve.wait_ge(onehot, ps * GROUPS + GROUPS + 1)
                        nc.vector.tensor_scalar(rank[:, :, :], rank[:, :, :], -float(P), None, ALU.add).then_inc(moved_on, 1)
                        dve.wait_ge(moved_on, ps + 1)

                    make_onehot(slice(0, 1))
                    nc.vector.tensor_copy(cs[:, :], rank[:, 0, 0:4]).then_inc(added, 1)
                    groups(dve, body, next_pass)

        def second_block(b1, xt, h):
            with ExitStack() as sx:
                c2 = sbt(sx, "c2", [P, N2])

                def k2(name, n=P, at=0):
                    return c2[:, C2[name] + at:C2[name] + at + n]

                ht = lambda k: h[:, k, :]
                const2_in, meta_in = sem("const2_in"), sem("meta_in")
                with block() as b:
                    @b.sync
                    def _(sp):
                        sp.dma_start(c2[:, :], const2).then_inc(const2_in, 16)
                        sp.wait_ge(const2_in, 16)

                    @b.vector
                    def _(dve):
                        o = PCOL["meta"]
                        nc.vector.tensor_copy(h[:, :, 0:META], par[:, o:o + 8 * META].rearrange("p (k t) -> p k t", k=8))
                normalize("lnin", ht, ht, KD, T2, k0("mean1024"), lambda k: pcol("ln_in_g", k),
                          lambda k: pcol("ln_in_b", k), EPS_LN)
                with ExitStack() as rx:
                    mixers(rx, xt, h, k2)
                ffn(h)

        def mixers(rx, xt, h, k2):
            spilled = sem("spilled")
            wa, xg = sbt(rx, "wa", [P, T2]), sbt(rx, "xg", [P, 2, T2])
            r, k, v = (sbt(rx, n, [P, KD, T2]) for n in ("rw_r", "rw_k", "rw_v"))
            with ExitStack() as cx:
                cp, cv = sbt(cx, "cp", [P, KD, TAPS - 1 + T2]), sbt(cx, "cv", [P, KD, T2])
                glu_ready, glu_sig, glu_out = sem("glu_ready"), sem("glu_sig"), sem("glu_out")
                with ExitStack() as gx, block() as b:
                    sg = [sbt(gx, f"glu_sg{i}", [P, T2]) for i in range(2)]

                    @b.tensor
                    def _(pe):
                        pe_tiles(pe, "conv_in", KD, 16, lambda q: h[:, q, :], T2, glu_ready, glu_out)

                    @b.scalar
                    def _(act):
                        for i in range(8):
                            act.wait_ge(glu_ready, 2 * i + 2)
                            if i >= 2:
                                act.wait_ge(glu_out, 2 * i - 2)
                            nc.scalar.activation(fold(sg[i % 2][:, :], T2), A(2 * i % 4 + 1, T2),
                                                 ACT.Sigmoid).then_inc(glu_sig, 1)

                    @b.vector
                    def _(dve):
                        nc.vector.memset(cp[:, :, 0:TAPS - 1], 0.0)
                        for i in range(8):
                            dve.wait_ge(glu_sig, i + 1)
                            nc.vector.tensor_tensor(fold(cp[:, i, TAPS - 1:], T2), fold(sg[i % 2][:, :], T2),
                                                    A(2 * i % 4, T2), ALU.mult).then_inc(glu_out, 2)

                    @b.sync
                    def _(sp):
                        load_slabs(sp, "conv_in")
                tap_done = sem("tap_done")
                rw_ready, rw_read, rw_mixed, zeroed = sem("rw_ready"), sem("rw_read"), sem("rw_mixed"), sem("rw_zeroed")
                rw_dest = ([r[:, i, :] for i in range(8)] + [k[:, i, :] for i in range(8)]
                           + [v[:, i, :] for i in range(8)] + [wa[:, :]] + [xg[:, i, :] for i in range(2)])
                with ExitStack() as tx, block() as b:
                    sh = [sbt(tx, f"shift{i}", [P, T2 + 1]) for i in range(3)]
                    keep = sbt(tx, "keep", [P, 27])
                    o_mu = PCOL["mu"]

                    @b.tensor
                    def _(pe):
                        i = 0
                        for name, n in (("rw_r", 8), ("rw_k", 8), ("rw_v", 8), ("rw_wa", 1), ("rw_g", 2)):
                            pe_tiles(pe, name, KD, n, lambda q: h[:, q, :], T2, rw_ready, rw_read, first=i)
                            i += n

                    @b.scalar
                    def _(act):
                        act.wait_ge(zeroed, 4)
                        for i, d in enumerate(rw_dest):
                            act.wait_ge(rw_ready, i + 1)
                            nc.scalar.activation(fold(d, T2), A(i % 4, T2), ACT.Copy, scale=keep[:, i:i + 1])
                            if i >= 3:
                                act.wait_ge(rw_mixed, i - 2)
                            nc.scalar.activation(fold(sh[i % 3][:, 1:T2 + 1], T2), A(i % 4, T2), ACT.Copy,
                                                 scale=par[:, o_mu + i:o_mu + i + 1]).then_inc(rw_read, 1)

                    @b.gpsimd
                    def _(pool):
                        nc.gpsimd.tensor_scalar(keep[:, :], par[:, o_mu:o_mu + 27], -1.0, 1.0, ALU.mult,
                                                ALU.add).then_inc(zeroed, 1)
                        for i in range(3):
                            nc.gpsimd.memset(sh[i][:, 0:1], 0.0).then_inc(zeroed, 1)
                        pool.wait_ge(zeroed, 4)
                        for i, d in enumerate(rw_dest):
                            pool.wait_ge(rw_read, i + 1)
                            nc.gpsimd.tensor_tensor(d, d, sh[i % 3][:, 0:T2], ALU.add).then_inc(rw_mixed, 1)
                        pool.wait_ge(rw_mixed, 27)

                    @b.vector
                    def _(dve):
                        o_w, o_b = PCOL["conv_dw"], PCOL["conv_dw_b"]
                        for q in range(8):
                            nc.vector.tensor_scalar(cv[:, q, :], cp[:, q, 0:T2], par[:, o_w + TAPS * q:o_w + TAPS * q + 1],
                                                    par[:, o_b + q:o_b + q + 1], ALU.mult, ALU.add).then_inc(tap_done, 1)
                        with dve.Fori(1, TAPS) as j:
                            for q in range(8):
                                dve.wait_ge(tap_done, j * 8 + q - 7)
                                nc.vector.scalar_tensor_tensor(
                                    out=cv[:, q, :], in0=cp[:, q, bass.ds(j, T2)],
                                    scalar=par[:, bass.ds(j + (o_w + TAPS * q), 1)], in1=cv[:, q, :],
                                    op0=ALU.mult, op1=ALU.add).then_inc(tap_done, 1)

                    @b.sync
                    def _(sp):
                        load_slabs(sp, "rw_g")
                normalize("lnconv", lambda q: cv[:, q, :], lambda q: cv[:, q, :], KD, T2, k0("mean1024"),
                          lambda q: pcol("conv_ln_g", q), lambda q: pcol("conv_ln_b", q), EPS_LN, ACT.Silu)
                ya_ready, ya_out, ya_sig, ya_done = sem("ya_ready"), sem("ya_out"), sem("ya_sig"), sem("ya_done")
                y1 = lambda q: cp[:, q, 0:T2]
                with block() as b:
                    @b.tensor
                    def _(pe):
                        pe_tiles(pe, "gate_a", KD, 8, lambda q: h[:, q, :], T2, ya_ready, ya_sig)
                        pe.wait_ge(ya_sig, 8)
                        pe_tiles(pe, "conv_out", KD, 8, lambda q: cv[:, q, :], T2, ya_out, ya_done)

                    @b.scalar
                    def _(act):
                        for i in range(8):
                            act.wait_ge(ya_ready, i + 1)
                            nc.scalar.activation(fold(y1(i), T2), A(i % 4, T2), ACT.Sigmoid,
                                                 bias=pcol("b_gate", i)).then_inc(ya_sig, 1)

                    @b.vector
                    def _(dve):
                        for i in range(8):
                            dve.wait_ge(ya_out, i + 1)
                            nc.vector.tensor_tensor(fold(y1(i), T2), fold(y1(i), T2), A(i % 4, T2),
                                                    ALU.mult).then_inc(ya_done, 1)

                    @b.sync
                    def _(sp):
                        load_slabs(sp, "conv_out")
                        sp.dma_start(h_d, h[:, :, :]).then_inc(spilled, 16)
                        sp.wait_ge(ya_done, 8)
                        sp.dma_start(y_d, cp[:, :, 0:T2]).then_inc(spilled, 16)
                        sp.wait_ge(spilled, 32)
            with ExitStack() as wx:
                lw, a = sbt(wx, "rw_lw", [P, KD, T2]), sbt(wx, "rw_a", [P, KD, T2])
                kk = h
                wc = sbt(wx, "rw_wc", [P, KD, 9])
                decay_and_keys(xt, wa, r, k, v, kk, a, lw, wc, k2)
                recurrence(xt, wa, r, k, v, kk, a, lw, wc, k2)
                group_norm_and_gate(xt, r, k, v, lw, xg)
                merge(h, r, k, lw)

        def decay_and_keys(xt, wa, r, k, v, kk, a, lw, wc, k2):
            tanhed, up_ready, up_read = sem("tanhed"), sem("wu_ready"), sem("wu_read")
            with block() as b:
                @b.scalar
                def _(act):
                    nc.scalar.activation(wa[0:64, :], wa[0:64, :], ACT.Tanh).then_inc(tanhed, 1)
                    for i in range(16):
                        act.wait_ge(up_ready, i + 1)
                        d, name = (lw, "w0") if i % 2 == 0 else (a, "a0")
                        nc.scalar.activation(fold(d[:, i // 2, :], T2), A(i % 4, T2), ACT.Sigmoid,
                                             bias=pcol(name, i // 2)).then_inc(up_read, 1)

                @b.tensor
                def _(pe):
                    pe.wait_ge(tanhed, 1)
                    n = SLAB0["wa_up"]
                    slab_wait(pe, n)
                    for i in range(16):
                        r0 = 64 * (i % 2)
                        if i >= 4:
                            pe.wait_ge(up_read, i - 3)
                        for s, (lo, hi) in enumerate(halves(T2)):
                            mm = nc.tensor.matmul(acc[i % 4][:, s, 0:hi - lo], ring[n % RING][r0:r0 + 64, i // 2 * P:i // 2 * P + P],
                                                  wa[r0:r0 + 64, lo:hi], start=True, stop=True)
                        mm.then_inc(up_ready, 1)
                    freed_by[n] = (up_ready, 16)

                @b.sync
                def _(sp):
                    load_slabs(sp, "wa_up")
            kk_made, kk_sq, sq_summed, kk_root, key_done = (sem("kk_made"), sem("kk_sq"), sem("kk_summed"),
                                                          sem("kk_root"), sem("key_done"))
            normed = sem("kk_normed")
            with ExitStack() as nx, block() as b:
                sq = [xt[:, 2 * i:2 * i + 2, :].rearrange("p a t -> p (a t)")[:, 0:T2] for i in range(4)]
                root = [sbt(nx, f"kk_root{i}", [P, T2]) for i in range(2)]
                scr = sbt(nx, "key_scr", [P, T2])
                omk = sbt(nx, "omk", [P, KD])

                @b.vector
                def _(dve):
                    o = PCOL["k_a"]
                    link("dve", dve, nc.vector.tensor_scalar(omk[:, :], par[:, o:o + 8], -1.0, 1.0, ALU.mult, ALU.add))
                    for i in range(8):
                        nc.vector.tensor_scalar(kk[:, i, :], k[:, i, :], pcol("k_k", i), None, ALU.mult).then_inc(kk_made, 1)
                    for i in range(8):
                        link("dve", dve, nc.vector.tensor_scalar(scr[:, :], a[:, i, :], pcol("k_a", i), omk[:, i:i + 1],
                                                                 ALU.mult, ALU.add))
                        link("dve", dve, nc.vector.tensor_tensor(k[:, i, :], k[:, i, :], scr[:, :], ALU.mult))
                        dve.wait_ge(kk_root, i + 1)
                        link("dve", dve, nc.vector.tensor_scalar(root[i % 2][:, :], root[i % 2][:, :], 1e-12, None, ALU.max))
                        link("dve", dve, nc.vector.reciprocal(root[i % 2][:, :], root[i % 2][:, :]))
                        nc.vector.tensor_tensor(kk[:, i, :], kk[:, i, :], root[i % 2][:, :], ALU.mult).then_inc(normed, 1)

                def root_of(act, i):
                    act.wait_ge(sq_summed, i + 1)
                    if i >= 2:
                        act.wait_ge(normed, i - 1)
                    nc.scalar.activation(fold(root[i % 2][:, :], T2), A(i % 4, T2), ACT.Sqrt).then_inc(kk_root, 1)

                @b.scalar
                def _(act):
                    for i in range(8):
                        act.wait_ge(kk_made, i + 1)
                        if i >= 4:
                            act.wait_ge(sq_summed, i - 3)
                        nc.scalar.activation(sq[i % 4], kk[:, i, :], ACT.Square).then_inc(kk_sq, 1)
                        if i >= 1:
                            root_of(act, i - 1)
                    root_of(act, 7)

                @b.tensor
                def _(pe):
                    for i in range(8):
                        pe.wait_ge(kk_sq, i + 1)
                        if i >= 4:
                            pe.wait_ge(kk_root, i - 3)
                        for s, (lo, hi) in enumerate(halves(T2)):
                            mm = nc.tensor.matmul(acc[i % 4][:, s, 0:hi - lo], k0("ones64"), sq[i % 4][:, lo:hi],
                                                  start=True, stop=True)
                        mm.then_inc(sq_summed, 1)
            scanned, e_up, e_dn, up_used, b_made, dn_used = (sem("scanned"), sem("e_up"), sem("e_dn"), sem("up_used"),
                                                            sem("b_made"), sem("dn_used"))
            with ExitStack() as nx, block() as b:
                eu = [sbt(nx, f"eu{i}", [P, T2]) for i in range(2)]
                ed = [sbt(nx, f"ed{i}", [P, T2]) for i in range(2)]
                first = sbt(nx, "first", [P, 9])

                @b.vector
                def _(dve):
                    def scan(i):
                        link("dve", dve, nc.vector.tensor_scalar(lw[:, i, :], lw[:, i, :], -float(np.exp(-0.5)), None, ALU.mult))
                        nc.vector.tensor_tensor_scan(lw[:, i, :], k2("resets", T2), lw[:, i, :], 0.0, ALU.mult,
                                                     ALU.add).then_inc(scanned, 1)

                    scan(0)
                    for i in range(8):
                        if i < 7:
                            scan(i + 1)
                        dve.wait_ge(e_up, i + 1)
                        e = eu[i % 2]
                        nc.vector.tensor_tensor(r[:, i, :], r[:, i, :], e[:, :], ALU.mult)
                        nc.vector.tensor_copy(wc[:, i, 0:8], e[:, CH - 1:T1:CH])
                        nc.vector.tensor_copy(wc[:, i, 8:9], e[:, T2 - 1:T2])
                        dve.wait_ge(b_made, i + 1)
                        link("dve", dve, nc.vector.tensor_scalar(first[:, :], kk[:, i, 0:T2:CH], -1.0, None, ALU.mult))
                        link("dve", dve, nc.vector.scalar_tensor_tensor(out=kk[:, i, 1:T2], in0=kk[:, i, 1:T2], scalar=-1.0,
                                                                        in1=e[:, 0:T2 - 1], op0=ALU.mult, op1=ALU.mult))
                        nc.vector.tensor_copy(kk[:, i, 0:T2:CH], first[:, :]).then_inc(up_used, 1)
                        dve.wait_ge(up_used, i + 1)

                @b.scalar
                def _(act):
                    for i in range(8):
                        act.wait_ge(scanned, i + 1)
                        if i >= 2:
                            act.wait_ge(up_used, i - 1)
                            act.wait_ge(dn_used, i - 1)
                        nc.scalar.activation(eu[i % 2][:, :], lw[:, i, :], ACT.Exp).then_inc(e_up, 1)
                        nc.scalar.activation(ed[i % 2][:, :], lw[:, i, :], ACT.Exp, scale=-1.0).then_inc(e_dn, 1)

                @b.gpsimd
                def _(pool):
                    for i in range(8):
                        nc.gpsimd.tensor_tensor(a[:, i, :], a[:, i, :], kk[:, i, :], ALU.mult).then_inc(b_made, 1)
                    for i in range(8):
                        pool.wait_ge(e_dn, i + 1)
                        nc.gpsimd.tensor_tensor(k[:, i, :], k[:, i, :], ed[i % 2][:, :], ALU.mult)
                        pool.wait_ge(b_made, i + 1)
                        nc.gpsimd.tensor_tensor(a[:, i, :], a[:, i, :], ed[i % 2][:, :], ALU.mult).then_inc(dn_used, 1)
                    pool.wait_ge(dn_used, 8)

        def recurrence(xt, wa, r, k, v, kk, a, o, wc, k2):
            bank = lambda i: acc[i // 2][:, i % 2, :]
            tiles = [(i * P, P, [(0, CH), (CH, CH)], 6) for i in range(T2 // P)] + [(T1, META, [(0, META)], 4)]
            pe_did, act_did, dve_did, pool_did = sem("rec_pe"), sem("rec_act"), sem("rec_dve"), sem("rec_pool")
            arrays = [kk, a, k, v]

            def events(chunks, nl):
                two = range(2)
                pe = [("tm", g) for g in range(8)]
                act = [("tm", g) for g in range(0, 8, 2)]
                dve = [("tm", g) for g in range(1, 8, 2)]
                pool = []
                for bp in two:
                    grams = [("gram", bp, p, m) for p in two for m in range(5)]
                    pe += grams
                    dve += grams
                    for p in two:
                        pool += [("mt", bp, p)]
                    for l in range(1, nl):
                        pe += [("x", bp, l, p) for p in two] + [("m", bp, l, p) for p in two]
                        act += [("x", bp, l, p) for p in two]
                        dve += [("m", bp, l, p) for p in two]
                        pool += [("ot", bp, l, p) for p in two]
                    pe += [("z", bp, p) for p in two] + [("ug", bp, p) for p in two]
                    act += [("z", bp, p) for p in two] + [("gt", bp, p) for p in two]
                    dve += [("uv", bp, p) for p in two]
                for j in range(len(chunks)):
                    pe += [("u", j), ("s", j)]
                    dve += [("u", j), ("s", j)]
                pe += [("y", 0), ("y", 1)]
                act += [("y", 0), ("y", 1)]
                return {"pe": pe, "act": act, "dve": dve, "pool": pool}

            plans, base = [], {"pe": 0, "act": 0, "dve": 0, "pool": 0}
            sems = {"pe": pe_did, "act": act_did, "dve": dve_did, "pool": pool_did}
            for t0, n, chunks, nl in tiles:
                ev = events(chunks, nl)
                plans.append({(e, name): base[e] + i + 1 for e in ev for i, name in enumerate(ev[e])})
                for e in ev:
                    base[e] += len(ev[e])

            def after(eng, ti, who, *name):
                eng.wait_ge(sems[who], plans[ti][(who, name)])

            sent = {e: 0 for e in sems}

            def did(ins, ti, who, *name):
                sent[who] += 1
                assert plans[ti][(who, name)] == sent[who], (ti, who, name)
                ins.then_inc(sems[who], 1)

            with ExitStack() as nx, block() as b:
                tm = [sbt(nx, f"tm{i}", [P, D]) for i in range(4)]
                tm_a, tm_b, tm_k, tm_v = tm
                arb, ark = sbt(nx, "arb", [P, 8, 2, P]), sbt(nx, "ark", [P, 8, 2, P])
                gt, uv = sbt(nx, "gt", [P, 8, P]), sbt(nx, "uv", [P, 8, 2, 64])
                S = [sbt(nx, f"S{i}", [P, 8, 64]) for i in range(3)]
                at = [sbt(nx, f"at{p}", [P, 4, P]) for p in range(2)]
                aak = [sbt(nx, f"aak{p}", [P, 4, P]) for p in range(2)]
                M = [xt[:, 2 * p, :].rearrange("p (q t) -> p q t", q=4) for p in range(2)]
                MT = [xt[:, 2 * p + 1, :].rearrange("p (q t) -> p q t", q=4) for p in range(2)]
                X = [xt[:, 4 + p, :].rearrange("p (q t) -> p q t", q=4) for p in range(2)]
                four = lambda ap: ap.rearrange("p (q t) -> p q t", q=4)
                OT = [[four(xt[:, 7, :]), four(wa[:, 0:512])], [four(k2("resets", 512)), sbt(nx, "ot", [P, 4, P])]]
                z = [four(xt[:, 6, 256 * p:256 * p + 256]) for p in range(2)]
                grid = lambda i, n, w=P: bank(i)[:, 0:4 * w].rearrange("p (q t) -> p q t", q=4)[0:n, :, 0:min(n, w)]
                mask = lambda ap, n: ap[0:n, 0:n].unsqueeze(1).to_broadcast([n, 4, n])

                @b.tensor
                def _(pe):
                    mmul = nc.tensor.matmul
                    chunk0 = 0
                    for ti, (t0, n, chunks, nl) in enumerate(tiles):
                        for g in range(8):
                            if g == 0 and ti:
                                after(pe, ti - 1, "act", "y", 1)
                                after(pe, ti - 1, "dve", "s", len(tiles[ti - 1][2]) - 1)
                            for q in range(4):
                                mm = nc.tensor.transpose(bank(g)[0:n, q * P:(q + 1) * P],
                                                         arrays[g // 2][:, 4 * (g % 2) + q, t0:t0 + n], k0("ident"))
                            did(mm, ti, "pe", "tm", g)
                        for bp in range(2):
                            for p in range(2):
                                rows = slice(64 * p, 64 * p + 64)
                                for m in range(5):
                                    i = 5 * p + m
                                    if i == 0 and bp == 0:
                                        after(pe, ti, "act", "tm", 6)
                                        after(pe, ti, "dve", "tm", 7)
                                    if i == 0 and bp == 1:
                                        after(pe, ti, "act", "gt", 0, 1)
                                        after(pe, ti, "dve", "uv", 0, 1)
                                    if i >= 8:
                                        after(pe, ti, "dve", "gram", bp, (i - 8) // 5, (i - 8) % 5)
                                    left, right = [(a, kk), (kk, a), (k, kk), (a, r), (k, r)][m]
                                    for q in range(4):
                                        mm = mmul(bank(i % 8)[0:n, q * P:q * P + n], left[rows, 4 * bp + q, t0:t0 + n],
                                                  right[rows, 4 * bp + q, t0:t0 + n], start=True, stop=True)
                                    did(mm, ti, "pe", "gram", bp, p, m)
                            after(pe, ti, "dve", "gram", bp, 1, 4)
                            for l in range(1, nl):
                                for p in range(2):
                                    after(pe, ti, "pool", "ot", bp, l, p)
                                    if l > 1:
                                        after(pe, ti, "dve", "m", bp, l - 1, p)
                                    for q in range(4):
                                        mm = mmul(bank(p)[0:n, q * P:q * P + n], OT[l % 2][p][0:n, q, 0:n], M[p][0:n, q, 0:n],
                                                  start=True, stop=True)
                                    did(mm, ti, "pe", "x", bp, l, p)
                                for p in range(2):
                                    after(pe, ti, "act", "x", bp, l, p)
                                    if l == 1:
                                        after(pe, ti, "pool", "mt", bp, p)
                                    if l < nl - 1:
                                        for q in range(4):
                                            mmul(bank(2 + p)[0:n, q * P:q * P + n], MT[p][0:n, q, 0:n], X[p][0:n, q, 0:n],
                                                 start=True, stop=True)
                                    for q in range(4):
                                        mm = mmul(bank(4 + p)[0:n, q * P:q * P + n], X[p][0:n, q, 0:n], MT[p][0:n, q, 0:n],
                                                  start=True, stop=True)
                                    did(mm, ti, "pe", "m", bp, l, p)
                            for p in range(2):
                                for q in range(4):
                                    hd = 64 * (2 * (4 * bp + q) + p)
                                    mm = mmul(bank(6 + p)[0:n, q * 64:q * 64 + 64], aak[p][0:n, q, 0:n],
                                              tm_v[0:n, hd:hd + 64], start=True, stop=True)
                                did(mm, ti, "pe", "z", bp, p)
                            for p in range(2):
                                after(pe, ti, "act", "z", bp, p)
                                after(pe, ti, "dve", "m", bp, nl - 1, p)
                                for q in range(4):
                                    mmul(bank(p)[0:n, q * 64:q * 64 + 64], MT[p][0:n, q, 0:n], z[p][0:n, q, :],
                                         start=True, stop=True)
                                for q in range(4):
                                    hd = 64 * (2 * (4 * bp + q) + p)
                                    mm = mmul(bank(2 + p)[64 * p:64 * p + 64, q * P:q * P + n], tm_a[0:n, hd:hd + 64],
                                              MT[p][0:n, q, 0:n], start=True, stop=True)
                                did(mm, ti, "pe", "ug", bp, p)
                        after(pe, ti, "act", "gt", 1, 1)
                        after(pe, ti, "dve", "uv", 1, 1)
                        for j, (c0_, cn) in enumerate(chunks):
                            s = S[(chunk0 + j) % 3]
                            if j:
                                after(pe, ti, "dve", "s", j - 1)
                            for p in range(2):
                                rows = slice(64 * p, 64 * p + 64)
                                for q in range(8):
                                    mm = mmul(bank(p)[c0_:c0_ + cn, q * 64:q * 64 + 64], gt[rows, q, c0_:c0_ + cn],
                                              s[rows, q, :], start=True, stop=True)
                            did(mm, ti, "pe", "u", j)
                            after(pe, ti, "dve", "u", j)
                            cr = slice(c0_, c0_ + cn)
                            for q in range(8):
                                for p in range(2):
                                    hd = 64 * (2 * q + p)
                                    d = bank(2)[64 * p:64 * p + 64, q * 64:q * 64 + 64]
                                    mmul(d, tm_b[cr, hd:hd + 64], uv[cr, q, p, :], start=True, stop=False)
                                    mm = mmul(d, tm_k[cr, hd:hd + 64], tm_v[cr, hd:hd + 64], start=False, stop=True)
                            did(mm, ti, "pe", "s", j)
                        for half in range(2):
                            for q in range(4 * half, 4 * half + 4):
                                for p in range(2):
                                    hd = 64 * (2 * q + p)
                                    rows = slice(64 * p, 64 * p + 64)
                                    at0 = q % 4 * P
                                    d = bank(4 + half)[rows, at0:at0 + n]
                                    mmul(d, uv[0:n, q, p, :], arb[0:n, q, p, 0:n], start=True, stop=False)
                                    mmul(d, tm_v[0:n, hd:hd + 64], ark[0:n, q, p, 0:n], start=False, stop=False)
                                    for j, (c0_, cn) in enumerate(chunks):
                                        mm = mmul(bank(4 + half)[rows, at0 + c0_:at0 + c0_ + cn], S[(chunk0 + j) % 3][rows, q, :],
                                                  r[rows, q, t0 + c0_:t0 + c0_ + cn], start=False, stop=j == len(chunks) - 1)
                            did(mm, ti, "pe", "y", half)
                        chunk0 += len(chunks)

                @b.scalar
                def _(act):
                    cp_ = lambda d, s_: nc.scalar.activation(d, s_, ACT.Copy)
                    for ti, (t0, n, chunks, nl) in enumerate(tiles):
                        for g in range(0, 8, 2):
                            after(act, ti, "pe", "tm", g)
                            did(cp_(tm[g // 2][0:n, 0:512], bank(g)[0:n, :]), ti, "act", "tm", g)
                        for bp in range(2):
                            for l in range(1, nl):
                                for p in range(2):
                                    after(act, ti, "pe", "x", bp, l, p)
                                    did(cp_(X[p][0:n, :, 0:n], grid(p, n)), ti, "act", "x", bp, l, p)
                            for p in range(2):
                                after(act, ti, "pe", "z", bp, p)
                                did(cp_(z[p][0:n, :, :], bank(6 + p)[0:n, 0:256].rearrange("p (q t) -> p q t", q=4)),
                                    ti, "act", "z", bp, p)
                            for p in range(2):
                                after(act, ti, "pe", "ug", bp, p)
                                rows = slice(64 * p, 64 * p + 64)
                                src = bank(2 + p).rearrange("p (q t) -> p q t", q=4)[rows, :, 0:n]
                                did(cp_(gt[rows, 4 * bp:4 * bp + 4, 0:n], src), ti, "act", "gt", bp, p)
                        for half in range(2):
                            after(act, ti, "pe", "y", half)
                            src = bank(4 + half).rearrange("p (q t) -> p q t", q=4)[:, :, 0:n]
                            did(cp_(o[:, 4 * half:4 * half + 4, t0:t0 + n], src), ti, "act", "y", half)

                @b.vector
                def _(dve):
                    tt = nc.vector.tensor_tensor
                    link("dve", dve, nc.vector.memset(S[0][:, :, :], 0.0))
                    chunk0 = 0
                    for ti, (t0, n, chunks, nl) in enumerate(tiles):
                        for g in range(1, 8, 2):
                            after(dve, ti, "pe", "tm", g)
                            did(nc.vector.tensor_copy(tm[g // 2][0:n, 512:1024], bank(g)[0:n, :]), ti, "dve", "tm", g)
                        for bp in range(2):
                            if bp:
                                after(dve, ti, "pool", "ot", 0, nl - 1, 1)
                            for p in range(2):
                                for m in range(5):
                                    i = 5 * p + m
                                    after(dve, ti, "pe", "gram", bp, p, m)
                                    src = grid(i % 8, n)
                                    d, mk = [(at[p][0:n, :, 0:n], "strict"), (M[p][0:n, :, 0:n], "level0_low"),
                                             (aak[p][0:n, :, 0:n], "strict"), (arb[0:n, 4 * bp:4 * bp + 4, p, 0:n], "incl"),
                                             (ark[0:n, 4 * bp:4 * bp + 4, p, 0:n], "incl")][m]
                                    ins = tt(d, src, mask(k2(mk), n), ALU.mult)
                                    if m == 1:
                                        link("dve", dve, ins)
                                        ins = tt(d, d, mask(k0("ident"), n), ALU.add)
                                    did(ins, ti, "dve", "gram", bp, p, m)
                            for l in range(1, nl):
                                for p in range(2):
                                    after(dve, ti, "pe", "m", bp, l, p)
                                    if l < nl - 1:
                                        tt(M[p][0:n, :, 0:n], M[p][0:n, :, 0:n], grid(2 + p, n), ALU.add)
                                    did(tt(MT[p][0:n, :, 0:n], MT[p][0:n, :, 0:n], grid(4 + p, n), ALU.add),
                                        ti, "dve", "m", bp, l, p)
                            for p in range(2):
                                after(dve, ti, "pe", "ug", bp, p)
                                did(nc.vector.tensor_copy(uv[0:n, 4 * bp:4 * bp + 4, p, :],
                                                          bank(p)[0:n, 0:256].rearrange("p (q t) -> p q t", q=4)),
                                    ti, "dve", "uv", bp, p)
                        for j, (c0_, cn) in enumerate(chunks):
                            after(dve, ti, "pe", "u", j)
                            cr = slice(c0_, c0_ + cn)
                            for p in range(2):
                                ins = tt(uv[cr, :, p, :], uv[cr, :, p, :], bank(p)[cr, :].rearrange("p (q t) -> p q t", q=8), ALU.add)
                            did(ins, ti, "dve", "u", j)
                            after(dve, ti, "pe", "s", j)
                            cg = chunk0 + j
                            s, sn = S[cg % 3], S[(cg + 1) % 3]
                            link("dve", dve, tt(sn[:, :, :], s[:, :, :], bank(2).rearrange("p (q t) -> p q t", q=8), ALU.add))
                            did(tt(sn[:, :, :], sn[:, :, :], wc[:, :, cg:cg + 1].to_broadcast([P, 8, 64]), ALU.mult),
                                ti, "dve", "s", j)
                            after(dve, ti, "dve", "s", j)
                        chunk0 += len(chunks)

                @b.gpsimd
                def _(pool):
                    tt = nc.gpsimd.tensor_tensor
                    for ti, (t0, n, chunks, nl) in enumerate(tiles):
                        for bp in range(2):
                            for p in range(2):
                                after(pool, ti, "dve", "gram", bp, p, 0)
                                if bp or ti:
                                    after(pool, *((ti, "pe", "ug", 0, p) if bp else (ti - 1, "pe", "ug", 1, p)))
                                d = MT[p][0:n, :, 0:n]
                                link("pool", pool, tt(d, at[p][0:n, :, 0:n], mask(k2("levels"), n), ALU.mult))
                                did(tt(d, d, mask(k0("ident"), n), ALU.add), ti, "pool", "mt", bp, p)
                            for l in range(1, nl):
                                for p in range(2):
                                    if l > 2:
                                        after(pool, ti, "pe", "x", bp, l - 2, p)
                                    did(tt(OT[l % 2][p][0:n, :, 0:n], at[p][0:n, :, 0:n], mask(k2("levels", P, l * P), n), ALU.mult),
                                        ti, "pool", "ot", bp, l, p)
                    pool.wait_ge(pool_did, base["pool"])

        def group_norm_and_gate(xt, r, k, v, o, xg):
            meaned, centred, squared, varred, rooted = (sem("gn_" + n) for n in ("meaned", "centred", "squared", "varred", "rooted"))
            scaled, shifted, prod_made, bonus, bonus_read = (sem("gn_" + n) for n in ("scaled", "shifted", "prod", "bonus", "bonus_read"))
            added, g_ready, gated, sig = (sem("gn_" + n) for n in ("added", "g_ready", "gated", "sig"))
            with ExitStack() as nx, block() as b:
                view = lambda i: xt[:, 2 * i:2 * i + 2, :].rearrange("p a t -> p (a t)")[:, 0:T2]
                sq, prod = [view(0), view(1)], [view(2), view(3)]
                root = [sbt(nx, f"gn_root{i}", [P, T2]) for i in range(2)]
                bon = [sbt(nx, f"gn_bon{i}", [P, T2]) for i in range(2)]

                @b.tensor
                def _(pe):
                    def over(j, mat, x):
                        for s, (lo, hi) in enumerate(halves(T2)):
                            mm = nc.tensor.matmul(acc[j][:, s, 0:hi - lo], mat, x[:, lo:hi], start=True, stop=True)
                        return mm

                    n = SLAB0["g_up"]
                    for i in range(8):
                        if i >= 1:
                            pe.wait_ge(centred, i)
                        over(0, k0("mean64"), o[:, i, :]).then_inc(meaned, 1)
                        pe.wait_ge(prod_made, i + 1)
                        if i >= 1:
                            pe.wait_ge(bonus_read, i)
                        over(2, k0("ones64"), prod[i % 2]).then_inc(bonus, 1)
                        pe.wait_ge(squared, i + 1)
                        if i >= 1:
                            pe.wait_ge(rooted, i)
                        over(1, k0("mean64"), sq[i % 2]).then_inc(varred, 1)
                        if i == 0:
                            pe.wait_ge(sig, 1)
                            slab_wait(pe, n)
                            slab_wait(pe, n + 1)
                        else:
                            pe.wait_ge(gated, i)
                        for q in range(2):
                            for s, (lo, hi) in enumerate(halves(T2)):
                                mm = nc.tensor.matmul(acc[3][:, s, 0:hi - lo], ring[(n + q) % RING][:, i * P:(i + 1) * P],
                                                      xg[:, q, lo:hi], start=(q == 0), stop=(q == 1))
                        mm.then_inc(g_ready, 1)
                    freed_by[n] = freed_by[n + 1] = (g_ready, 8)

                @b.scalar
                def _(act):
                    nc.scalar.activation(xg[:, :, :], xg[:, :, :], ACT.Sigmoid).then_inc(sig, 1)
                    for i in range(8):
                        act.wait_ge(centred, i + 1)
                        if i >= 2:
                            act.wait_ge(varred, i - 1)
                        nc.scalar.activation(sq[i % 2], o[:, i, :], ACT.Square).then_inc(squared, 1)
                        act.wait_ge(varred, i + 1)
                        if i >= 2:
                            act.wait_ge(scaled, i - 1)
                        nc.scalar.activation(fold(root[i % 2][:, :], T2), A(1, T2), ACT.Sqrt,
                                             bias=k0("eps", 1, EPS_GN)).then_inc(rooted, 1)
                        act.wait_ge(scaled, i + 1)
                        nc.scalar.activation(o[:, i, :], o[:, i, :], ACT.Identity, scale=pcol("lnx_g", i),
                                             bias=pcol("lnx_b", i)).then_inc(shifted, 1)

                @b.vector
                def _(dve):
                    tt = nc.vector.tensor_tensor
                    for i in range(8):
                        dve.wait_ge(meaned, i + 1)
                        tt(fold(o[:, i, :], T2), fold(o[:, i, :], T2), A(0, T2), ALU.subtract).then_inc(centred, 1)
                        if i >= 2:
                            dve.wait_ge(bonus, i - 1)
                        nc.vector.scalar_tensor_tensor(out=prod[i % 2], in0=r[:, i, :], scalar=pcol("r_k", i), in1=k[:, i, :],
                                                       op0=ALU.mult, op1=ALU.mult).then_inc(prod_made, 1)
                        dve.wait_ge(bonus, i + 1)
                        if i >= 2:
                            dve.wait_ge(added, i - 1)
                        tt(fold(bon[i % 2][:, :], T2), fold(v[:, i, :], T2), A(2, T2), ALU.mult).then_inc(bonus_read, 1)
                        dve.wait_ge(rooted, i + 1)
                        link("dve", dve, nc.vector.reciprocal(root[i % 2][:, :], root[i % 2][:, :]))
                        tt(o[:, i, :], o[:, i, :], root[i % 2][:, :], ALU.mult).then_inc(scaled, 1)
                        dve.wait_ge(added, i + 1)
                        dve.wait_ge(g_ready, i + 1)
                        tt(fold(o[:, i, :], T2), fold(o[:, i, :], T2), A(3, T2), ALU.mult).then_inc(gated, 1)

                @b.gpsimd
                def _(pool):
                    for i in range(8):
                        pool.wait_ge(shifted, i + 1)
                        pool.wait_ge(bonus_read, i + 1)
                        nc.gpsimd.tensor_tensor(o[:, i, :], o[:, i, :], bon[i % 2][:, :], ALU.add).then_inc(added, 1)
                    pool.wait_ge(added, 8)

                @b.sync
                def _(sp):
                    load_slabs(sp, "g_up")

        def merge(h, y, gb, o):
            back = sem("unspilled")
            g_ready, g_out, o_ready, o_out, y_done = (sem("mg_" + n) for n in ("g_ready", "g_out", "o_ready", "o_out", "y_done"))
            with block() as b:
                @b.sync
                def _(sp):
                    sp.dma_start(h[:, :, :], h_d).then_inc(back, 16)
                    sp.dma_start(y[:, :, :], y_d).then_inc(back, 16)

                @b.tensor
                def _(pe):
                    pe.wait_ge(back, 32)
                    pe_tiles(pe, "gate_b", KD, 8, lambda q: h[:, q, :], T2, g_ready, g_out)
                    pe.wait_ge(g_out, 8)
                    pe_tiles(pe, "rw_out", KD, 8, lambda q: o[:, q, :], T2, o_ready, o_out)

                @b.scalar
                def _(act):
                    for i in range(8):
                        act.wait_ge(g_ready, i + 1)
                        nc.scalar.activation(fold(gb[:, i, :], T2), A(i % 4, T2), ACT.Sigmoid,
                                             bias=pcol("b_gate", 8 + i)).then_inc(g_out, 1)

                @b.vector
                def _(dve):
                    for i in range(8):
                        dve.wait_ge(o_ready, i + 1)
                        nc.vector.tensor_tensor(fold(gb[:, i, :], T2), fold(gb[:, i, :], T2), A(i % 4, T2),
                                                ALU.mult).then_inc(o_out, 1)

                @b.gpsimd
                def _(pool):
                    pool.wait_ge(back, 32)
                    for i in range(8):
                        pool.wait_ge(o_out, i + 1)
                        nc.gpsimd.tensor_tensor(y[:, i, :], y[:, i, :], gb[:, i, :], ALU.add).then_inc(y_done, 1)
                    pool.wait_ge(y_done, 8)

                @b.sync
                def _(sp):
                    load_slabs(sp, "rw_out")
            w_ready, w_out = sem("mg_w_ready"), sem("mg_w_out")
            with block() as b:
                @b.tensor
                def _(pe):
                    pe_tiles(pe, "w_o2", KD, 8, lambda q: y[:, q, :], T2, w_ready, w_out)

                @b.vector
                def _(dve):
                    for i in range(8):
                        dve.wait_ge(w_ready, i + 1)
                        nc.vector.scalar_tensor_tensor(out=fold(h[:, i, :], T2), in0=fold(h[:, i, :], T2), scalar=ALPHA,
                                                       in1=A(i % 4, T2), op0=ALU.mult, op1=ALU.add).then_inc(w_out, 1)

                @b.sync
                def _(sp):
                    load_slabs(sp, "w_o2")
            ht = lambda q: h[:, q, :]
            normalize("ln1", ht, ht, KD, T2, k0("mean1024"), lambda q: pcol("ln1_g", q), lambda q: pcol("ln1_b", q), EPS_LN)

        def ffn(h):
            up_ready, up_read, tapped, silued, hid_made = (sem("ff_" + n) for n in ("up_ready", "up_read", "tapped", "silued", "hid"))
            dn_ready, dn_out, stored = sem("ff_dn_ready"), sem("ff_dn_out"), sem("out_stored")
            with ExitStack() as fx:
                hid = sbt(fx, "ff_hid", [P, NF, T2])
                with ExitStack() as ux, block() as b:
                    up = [sbt(ux, f"ff_up{i}", [P, 2 + T2]) for i in range(4)]
                    t = [sbt(ux, f"ff_t{i}", [P, T2]) for i in range(4)]
                    padded = sem("ff_padded")

                    @b.tensor
                    def _(pe):
                        pe_tiles(pe, "ffn_up", KD, 2 * NF, lambda q: h[:, q, :], T2, up_ready, up_read)

                    def silu(act, f):
                        act.wait_ge(tapped, 2 * f + 2)
                        g = t[(2 * f + 1) % 4]
                        nc.scalar.activation(g[:, :], g[:, :], ACT.Silu).then_inc(silued, 1)

                    @b.scalar
                    def _(act):
                        act.wait_ge(padded, 4)
                        for i in range(2 * NF):
                            act.wait_ge(up_ready, i + 1)
                            if i >= 4:
                                act.wait_ge(tapped, i - 3)
                            nc.scalar.activation(fold(up[i % 4][:, 2:2 + T2], T2), A(i % 4, T2), ACT.Copy).then_inc(up_read, 1)
                            if i % 2 and i >= 3:
                                silu(act, i // 2 - 1)
                        silu(act, NF - 1)

                    @b.vector
                    def _(dve):
                        o_w = PCOL["ffn_dw"]
                        for i in range(4):
                            nc.vector.memset(up[i][:, 0:2], 0.0).then_inc(padded, 1)
                        for i in range(2 * NF):
                            f = i // 2 + NF * (i % 2)
                            w = lambda j: par[:, o_w + 3 * f + j:o_w + 3 * f + j + 1]
                            d = t[i % 4][:, :]
                            dve.wait_ge(up_read, i + 1)
                            if i >= 4:
                                dve.wait_ge(hid_made, i // 2 - 1)
                            link("dve", dve, nc.vector.tensor_scalar(d, up[i % 4][:, 0:T2], w(0), None, ALU.mult))
                            link("dve", dve, nc.vector.scalar_tensor_tensor(out=d, in0=up[i % 4][:, 1:1 + T2], scalar=w(1), in1=d,
                                                                            op0=ALU.mult, op1=ALU.add))
                            nc.vector.scalar_tensor_tensor(out=d, in0=up[i % 4][:, 2:2 + T2], scalar=w(2), in1=d,
                                                           op0=ALU.mult, op1=ALU.add).then_inc(tapped, 1)

                    @b.gpsimd
                    def _(pool):
                        for f in range(NF):
                            pool.wait_ge(silued, f + 1)
                            nc.gpsimd.tensor_tensor(hid[:, f, :], t[2 * f % 4][:, :], t[(2 * f + 1) % 4][:, :],
                                                    ALU.mult).then_inc(hid_made, 1)
                        pool.wait_ge(hid_made, NF)

                    @b.sync
                    def _(sp):
                        load_slabs(sp, "ffn_up")
                with block() as b:
                    @b.tensor
                    def _(pe):
                        pe_tiles(pe, "ffn_down", NF, 8, lambda q: hid[:, q, :], T2, dn_ready, dn_out)

                    @b.vector
                    def _(dve):
                        for i in range(8):
                            dve.wait_ge(dn_ready, i + 1)
                            nc.vector.scalar_tensor_tensor(out=fold(h[:, i, :], T2), in0=fold(h[:, i, :], T2), scalar=ALPHA,
                                                           in1=A(i % 4, T2), op0=ALU.mult, op1=ALU.add).then_inc(dn_out, 1)

                    @b.sync
                    def _(sp):
                        load_slabs(sp, "ffn_down")
            ht = lambda q: h[:, q, :]
            normalize("ln2", ht, ht, KD, T2, k0("mean1024"), lambda q: pcol("ln2_g", q), lambda q: pcol("ln2_b", q), EPS_LN)
            with block() as b:
                @b.sync
                def _(sp):
                    sp.dma_start(out, h[:, :, META:T2]).then_inc(stored, 16)
                    sp.wait_ge(stored, 16)

        with ExitStack() as b1:
            xt = sbt(b1, "xt", [P, KD, T1])
            x2 = first_block(b1, xt)
            second_block(b1, xt, x2)


def kernel(**inputs):
    import numpy as _np
    import concourse.bacc as _bacc
    from concourse.bass_utils import run_bass_kernel_spmd as _run

    nc = _bacc.Bacc("TRN2", target_bir_lowering=False, num_devices=1)
    a = {k: _np.asarray(v) for k, v in inputs.items()}
    arrays = lay_out(a)
    args = [nc.dram_tensor(name, v.shape, mybir.dt.from_np(v.dtype), kind="ExternalInput").ap()
            for name, v in arrays.items()]
    args.append(nc.dram_tensor("out_t", (P, KD, T1), F32, kind="ExternalOutput").ap())
    program(nc, *args)
    got = _run(nc, [arrays], core_ids=[0]).results[0]["out_t"]
    return _np.ascontiguousarray(_np.asarray(got).transpose(2, 1, 0).reshape(1, T1, D))
```

```python
from contextlib import ExitStack

import numpy as np

import concourse.bass as bass
from concourse import mybir

F32 = mybir.dt.float32
F32R = mybir.dt.float32r
ALU = mybir.AluOpType
ACT = mybir.ActivationFunctionType
AX = mybir.AxisListType.X

P = 128
D = 1024
KD = D // P
T1 = 512
META = 16
T2 = T1 + META
RING = 4
NEG = -1e30
TAKEN = -3e38
AWAY = 1e6

QL, KVL = 384, 256
HEADS = 8
NOPE, ROPE_D = 64, 32
HD = 64
TOPK = 128
N_EXP, FF = 32, 256
GROUPS = 8
TAPS = 31
D_FF = 2816
NF = D_FF // P
ALPHA = 2.0 ** 0.25
RH = 16
CH = 64

SLAB_COUNTS = [
    ("c_q", 3), ("c_kv", 2), ("q_b", 4), ("k_b", 4), ("q_i", 4), ("k_i", 1), ("k_r", 1),
    ("g_a", 8), ("g_b", 8), ("v_b", 4), ("w_uq", 3), ("w_uk", 2), ("w_uv", 1),
    ("w_o_a", 4), ("w_o_b", 4), ("w_out", 8),
    ("conv_in", 16), ("rw_r", 8), ("rw_k", 8), ("rw_v", 8), ("rw_wa", 1), ("rw_g", 2),
    ("gate_a", 8), ("conv_out", 8), ("wa_up", 1),
    ("g_up", 2), ("gate_b", 8), ("rw_out", 8), ("w_o2", 8), ("ffn_up", 2 * NF), ("ffn_down", NF),
]
SLAB0, _n = {}, 0
for _name, _c in SLAB_COUNTS:
    SLAB0[_name] = _n
    _n += _c
N_SLABS = _n

MOE_STEPS = [("gate_up", 0), ("gate_up", 1), ("gate_up", 2), ("down", 0), ("gate_up", 3), ("down", 1), ("down", 2), ("down", 3)]
MOE_ORDER = [(kind, e, i) for kind, e in MOE_STEPS for i in range(4 if kind == "gate_up" else 2)]
MOE_AHEAD = 6

PARAM_COLS = [
    ("norm_mix_g", 8), ("mla_q_norm_g", 3), ("mla_kv_norm_g", 2), ("norm_ffn_g", 8), ("final_norm_g", 8),
    ("ln_in_g", 8), ("ln_in_b", 8), ("b_gate", 16), ("conv_dw", 8 * TAPS), ("conv_dw_b", 8),
    ("conv_ln_g", 8), ("conv_ln_b", 8), ("mu", 27), ("w0", 8), ("a0", 8), ("k_k", 8), ("k_a", 8),
    ("r_k", 8), ("lnx_g", 8), ("lnx_b", 8), ("ln1_g", 8), ("ln1_b", 8), ("ffn_dw", 3 * 2 * NF),
    ("ln2_g", 8), ("ln2_b", 8), ("router", 8 * 40), ("w_i", 64), ("meta", 8 * META),
]
PCOL, _n = {}, 0
for _name, _c in PARAM_COLS:
    PCOL[_name] = _n
    _n += _c
N_PARAMS = _n

CONST0 = [("ident", P), ("mean1024", P), ("ones64", P), ("mean64", P), ("eps", 4)]
CONST1 = [("mean384", P), ("mean256", P), ("rot64", P), ("rot96", P), ("cos64", T1), ("sin64", T1),
          ("cos96", T1), ("sin96", T1), ("causal", T1), ("rev8", 8), ("rev32", 32),
          ("before", P), ("ones", P), ("iota", P)]
CONST2 = [("levels", 6 * P), ("level0_low", P), ("strict", P), ("incl", P), ("resets", T2)]


def offsets(table):
    out, n = {}, 0
    for name, c in table:
        out[name] = n
        n += c
    return out, n


C0, N0 = offsets(CONST0)
C1, N1 = offsets(CONST1)
C2, N2 = offsets(CONST2)
EPS_RMS, EPS_LN, EPS_GN = 0, 1, 2


def shape_constants():
    f = np.float32
    eye = np.eye(P, dtype=f)
    blk = np.kron(np.eye(2, dtype=f), np.ones((64, 64), f))
    c0 = np.zeros((P, N0), f)
    c0[:, C0["ident"]:][:, :P] = eye
    c0[:, C0["mean1024"]:][:, :P] = 1.0 / D
    c0[:, C0["ones64"]:][:, :P] = blk
    c0[:, C0["mean64"]:][:, :P] = blk / 64
    c0[:, C0["eps"]:][:, :4] = np.array([1e-6, 1e-5, 64e-5, 0], f)
    c1 = np.zeros((P, N1), f)
    c1[:, C1["mean384"]:][:, :P] = f(1.0 / QL)
    c1[:, C1["mean256"]:][:, :P] = f(1.0 / KVL)

    def rotation(starts, rot):
        half = rot // 2
        m, cos, sin = np.zeros((P, P), f), np.ones((P, T1), f), np.zeros((P, T1), f)
        inv = (f(500000.0) ** (-np.arange(half, dtype=f) * f(2.0) / f(rot))).astype(f)
        ang = (np.arange(T1, dtype=f)[:, None] * inv[None, :]).astype(f)
        for s in starts:
            for i in range(half):
                m[s + i + half, s + i] = -1.0
                m[s + i, s + i + half] = 1.0
                for r in (s + i, s + i + half):
                    cos[r], sin[r] = np.cos(ang[:, i]), np.sin(ang[:, i])
        return m, cos, sin

    for name, starts, rot in (("64", (0, 64), 16), ("96", (64,), 32)):
        m, cos, sin = rotation(starts, rot)
        c1[:, C1["rot" + name]:][:, :P] = m
        c1[:, C1["cos" + name]:][:, :T1] = cos
        c1[:, C1["sin" + name]:][:, :T1] = sin
    c1[0:64, C1["causal"] + T1 - 64:C1["causal"] + T1] = NEG
    c1[:, C1["rev8"]:][:, :8] = np.arange(8, 0, -1)
    c1[:, C1["rev32"]:][:, :32] = np.arange(32, 0, -1)
    c1[:, C1["before"]:][:, :P] = np.arange(P)[:, None] < np.arange(P)[None, :]
    c1[:, C1["ones"]:][:, :P] = 1.0
    c1[:, C1["iota"]:][:, :P] = np.arange(P)
    c2 = np.zeros((P, N2), f)
    s, t = np.arange(P)[:, None], np.arange(P)[None, :]
    for l in range(6):
        b = 1 << l
        c2[:, C2["levels"] + l * P:][:, :P] = (s // (2 * b) == t // (2 * b)) & (s // b % 2 == 0) & (t // b % 2 == 1)
    c2[:, C2["level0_low"]:][:, :P] = c2[:, C2["levels"]:][:, :P].T
    c2[:, C2["strict"]:][:, :P] = (s // CH == t // CH) & (s < t)
    c2[:, C2["incl"]:][:, :P] = (s // CH == t // CH) & (s <= t)
    c2[:, C2["resets"]:][:, :T2] = np.arange(T2)[None, :] % CH != 0
    return c0, c1, c2


def blocks(w, width=P, rows=None):
    k, n = w.shape
    kt, nt = -(-k // P), -(-n // width)
    full = np.zeros((kt * P, nt, P), w.dtype)
    padded = np.zeros((kt * P, nt * width), w.dtype)
    padded[:k, :n] = w
    full[:, :, :width] = padded.reshape(kt * P, nt, width)
    b = full.reshape(kt, P, nt, P).transpose(2, 0, 1, 3).reshape(nt * kt, P, P)
    pad = -b.shape[0] % 8
    if pad:
        b = np.concatenate([b, np.zeros((pad, P, P), w.dtype)])
    return b.reshape(-1, 8, P, P).transpose(0, 2, 1, 3).reshape(-1, P, 8 * P)


def rows512(w):
    pad = -w.shape[0] % 256
    w = np.concatenate([w, np.zeros((pad, w.shape[1]), w.dtype)]) if pad else w
    return w.reshape(-1, 2, P, 512).transpose(0, 2, 1, 3).reshape(-1, P, 1024)


def lay_out(a):
    w_in, w2 = a["w_in"][0], a["w_in_2"][0]
    o = np.cumsum([0, QL, KVL, ROPE_D, 512, 512, 512, 512, HD, HEADS, D, D])
    part = [w_in[:, o[i]:o[i + 1]] for i in range(11)]
    c = 2 * D
    s = {"c_q": blocks(part[0]), "c_kv": blocks(part[1]),
         "k_r": blocks(w_in[:, o[2] - 64:o[3]], width=96),
         "q_b": blocks(part[3]), "k_b": blocks(part[4]), "v_b": rows512(part[5]),
         "q_i": blocks(part[6]), "k_i": blocks(np.concatenate([part[7], part[7]], 1)),
         "g_a": blocks(part[9]), "g_b": blocks(part[10]),
         "w_uq": blocks(a["w_uq"][0], width=96), "w_uk": blocks(a["w_uk"][0], width=64),
         "w_uv": rows512(a["w_uv"][0]),
         "w_o_a": blocks(a["w_o_a"][0]), "w_o_b": blocks(a["w_o_b"][0]), "w_out": blocks(a["w_out"][0]),
         "conv_in": blocks(w2[:, :c]).reshape(2, 8, P, 1024).transpose(1, 0, 2, 3).reshape(16, P, 1024),
         "rw_r": blocks(w2[:, c:c + D]), "rw_k": blocks(w2[:, c + D:c + 2 * D]),
         "rw_v": blocks(w2[:, c + 2 * D:c + 3 * D]),
         "rw_wa": blocks(w2[:, c + 3 * D:c + 3 * D + P]),
         "rw_g": blocks(w2[:, c + 3 * D + P:c + 3 * D + P + 160]),
         "gate_a": blocks(w2[:, 5408:5408 + D]), "gate_b": blocks(w2[:, 5408 + D:5408 + 2 * D]),
         "conv_out": blocks(a["w_conv_out_2"][0]),
         "wa_up": np.concatenate([a["w_decay_up_2"][0], a["a_up_2"][0]])[None],
         "g_up": np.concatenate([a["g_up_2"][0], np.zeros((96, D), w2.dtype)]).reshape(2, P, D),
         "rw_out": blocks(a["w_rwkv_out_2"][0]), "w_o2": blocks(a["w_o_2"][0]),
         "ffn_down": blocks(a["ffn_down_2"][0])}
    up = blocks(a["ffn_up_2"][0])
    s["ffn_up"] = up.reshape(2, NF, P, 1024).transpose(1, 0, 2, 3).reshape(2 * NF, P, 1024)
    gate_up = np.concatenate([a["w_gate"][0], a["w_up"][0]], 2).reshape(GROUPS, 4, 4, 2, P, 2 * FF)
    gate_up = gate_up.transpose(0, 1, 2, 4, 3, 5).reshape(GROUPS, 4, 4, P, 1024)
    down = a["w_down"][0].reshape(GROUPS, 4, 2, P, D)
    moe = np.stack([(gate_up if kind == "gate_up" else down)[:, e, i] for kind, e, i in MOE_ORDER], 1)
    moe = moe.reshape(-1, P, 1024)
    moe = np.concatenate([moe, moe[:MOE_AHEAD]])
    for name, n in SLAB_COUNTS:
        assert s[name].shape == (n, P, 1024), (name, s[name].shape)
    slabs = np.concatenate([s[name] for name, _ in SLAB_COUNTS])

    def col(v):
        v = np.asarray(v).reshape(-1)
        pad = -v.size % P
        v = np.concatenate([v, np.zeros(pad, v.dtype)]) if pad else v
        return v.reshape(-1, P).T

    mu = a["rwkv_mu_2"][0]
    cols = {n: col(a[n]) for n in ("norm_mix_g", "mla_q_norm_g", "mla_kv_norm_g", "norm_ffn_g", "final_norm_g")}
    for n in ("ln_in_g", "ln_in_b", "b_gate", "conv_dw_b", "conv_ln_g", "conv_ln_b", "w0", "a0", "k_k", "k_a",
              "r_k", "lnx_g", "lnx_b", "ln1_g", "ln1_b", "ln2_g", "ln2_b"):
        cols[n] = col(a[n + "_2"])
    cols["mu"] = col(mu)
    cols["conv_dw"] = a["conv_dw_2"][0].reshape(TAPS, 8, P).transpose(2, 1, 0).reshape(P, -1)
    cols["ffn_dw"] = a["ffn_dw_2"][0].reshape(3, 2 * NF, P).transpose(2, 1, 0).reshape(P, -1)
    r = np.concatenate([a["w_router_group"][0], a["w_router_expert"][0]], 1)
    cols["router"] = r.reshape(8, P, 40).transpose(1, 0, 2).reshape(P, -1)
    cols["w_i"] = part[8].reshape(8, P, 8).transpose(1, 0, 2).reshape(P, -1)
    cols["meta"] = a["meta_tokens_2"].reshape(META, 8, P).transpose(2, 1, 0).reshape(P, -1)
    for name, n in PARAM_COLS:
        assert cols[name].shape == (P, n), (name, cols[name].shape)
    params = np.concatenate([cols[name] for name, _ in PARAM_COLS], 1)
    c0, c1, c2 = shape_constants()
    return {
        "x_t": np.ascontiguousarray(a["x"][0].reshape(T1, 8, P).transpose(2, 1, 0)),
        "slabs": slabs, "moe_slabs": moe, "params": np.ascontiguousarray(params),
        "router_bias": np.concatenate([a["b_router_group"][0], a["b_router_expert"][0]])[None],
        "const0": c0, "const1": c1, "const2": c2,
    }


def halves(t):
    return [(0, t)] if t <= 512 else [(0, t // 2), (t // 2, t)]


def fold(ap, t):
    return ap.rearrange("p (h w) -> p h w", h=len(halves(t)))


def program(nc, x_t, slabs, moe_slabs, params_d, router_bias, const0, const1, const2, out):
    top = ExitStack()
    with top:
        count = [0]

        def sem(name):
            count[0] += 1
            return top.enter_context(nc.semaphore(name))

        def sbt(ctx, name, shape, dt=F32):
            return ctx.enter_context(nc.sbuf_tensor(name, shape, dt))

        def block():
            return nc.Block(no_gpsimd_drain=True)

        h_d = nc.dram_tensor("h_spill", [P, KD, T2], F32, kind="Internal").ap()
        y_d = nc.dram_tensor("y_spill", [P, KD, T2], F32, kind="Internal").ap()

        acc = [top.enter_context(nc.psum_tensor(f"acc{j}", [P, 2, 512], F32)) for j in range(4)]
        ring = [sbt(top, f"ring{j}", [P, 1024]) for j in range(RING)]
        par = sbt(top, "par", [P, N_PARAMS])
        c0 = sbt(top, "c0", [P, N0])
        slab_in = [sem(f"slab_in{j}") for j in range(RING)]
        slab_used = sem("slab_used")
        chains = {e: [sem(f"{e}_chain"), 0] for e in ("dve", "act", "pool")}

        def link(e, eng, ins):
            c = chains[e]
            c[1] += 1
            ins.then_inc(c[0], 1)
            eng.wait_ge(c[0], c[1])

        def k0(name, n=P, at=0):
            return c0[:, C0[name] + at:C0[name] + at + n]

        def pcol(name, k, rows=P):
            return par[0:rows, PCOL[name] + k:PCOL[name] + k + 1]

        def A(j, t, rows=P, r0=0):
            n = len(halves(t))
            return acc[j][r0:r0 + rows, 0:n, 0:t // n]

        issued, used = [0], [0]
        freed_by = {}

        def slab_done(mm, n):
            used[0] += 1
            freed_by[n] = (slab_used, used[0])
            mm.then_inc(slab_used, 1)


        def load_slabs(sp, name=None):
            if name is None:
                stop = RING
            else:
                i = [n for n, _ in SLAB_COUNTS].index(name)
                stop = min(SLAB0[name] + SLAB_COUNTS[i][1] + RING, N_SLABS)
            for n in range(issued[0], stop):
                if n - RING in split_rank:
                    sp.wait_ge(lo_made, split_rank[n - RING] + 1)
                elif n >= RING:
                    sp.wait_ge(*freed_by[n - RING])
                sp.dma_start(ring[n % RING][:, :], slabs[n]).then_inc(slab_in[n % RING], 16)
            issued[0] = stop

        def slab_wait(pe, n):
            pe.wait_ge(slab_in[n % RING], 16 * (n // RING + 1))

        hi_made, lo_made = sem("slab_hi_made"), sem("slab_lo_made")
        x_hi, x_lo, x_count = sem("x_hi_made"), sem("x_lo_made"), [0]
        split_rank = {}
        for name, cnt in SLAB_COUNTS:
            if name not in ("w_uq", "w_uk", "w_uv", "wa_up", "g_up"):
                for i in range(cnt):
                    split_rank[SLAB0[name] + i] = len(split_rank)

        def slab_range(*names):
            table = dict(SLAB_COUNTS)
            return [SLAB0[m] + i for m in names for i in range(table[m])]

        class Weights:

            def __init__(self, ctx, tag, depth=3):
                self.depth = depth
                self.hi = [sbt(ctx, f"{tag}_whi{i}", [P, 1024], F32R) for i in range(depth)]
                self.lo = [sbt(ctx, f"{tag}_wlo{i}", [P, 1024], F32R) for i in range(depth)]
                self.first = None

            def act(self, act, n):
                if self.first is None:
                    self.first = self.next = n
                if n < self.next:
                    return
                self.next = n + 1
                slab_wait(act, n)
                if n - self.depth >= self.first:
                    act.wait_ge(*freed_by[n - self.depth])
                nc.scalar.activation(self.hi[n % self.depth][:, :], ring[n % RING][:, :], ACT.Copy).then_inc(hi_made, 1)

            def pool(self, pool, n):
                pool.wait_ge(hi_made, split_rank[n] + 1)
                nc.gpsimd.tensor_tensor(self.lo[n % self.depth][:, :], ring[n % RING][:, :],
                                        self.hi[n % self.depth][:, :].bitcast(F32), ALU.subtract).then_inc(lo_made, 1)

            def begin(self, act, names, *operands):
                n = slab_range(*names)[0]
                self.act(act, n)
                x = operands[0]
                x.act(act, 0, x.kt // 2)
                self.act(act, n + 1)
                x.act(act, x.kt // 2, x.kt)
                for x in operands[1:]:
                    x.act(act)

            def all_act(self, act, names):
                for n in slab_range(*names):
                    self.act(act, n)

            def all_pool(self, pool, names):
                for n in slab_range(*names):
                    self.pool(pool, n)
                pool.wait_ge(lo_made, split_rank[n] + 1)

            def wait(self, pe, n):
                pe.wait_ge(lo_made, split_rank[n] + 1)
                return self.hi[n % self.depth], self.lo[n % self.depth]

        class Operand:

            def __init__(self, ctx, tag, kt, t):
                self.kt = kt
                self.hi, self.lo = (sbt(ctx, f"{tag}_x{n}", [P, kt, t], F32R) for n in ("hi", "lo"))

            def start(self, x):
                self.x, self.base = x, x_count[0]
                x_count[0] += self.kt

            def act(self, act, first=0, end=None):
                for k in range(first, end or self.kt):
                    nc.scalar.activation(self.hi[:, k, :], self.x(k), ACT.Copy).then_inc(x_hi, 1)

            def dve(self, dve):
                for k in range(self.kt):
                    dve.wait_ge(x_hi, self.base + k + 1)
                    nc.vector.tensor_tensor(self.lo[:, k, :], self.x(k), self.hi[:, k, :].bitcast(F32),
                                            ALU.subtract).then_inc(x_lo, 1)

            def wait(self, pe, k):
                pe.wait_ge(x_lo, self.base + k + 1)

        def schedule(name, kt, nt):
            return [[SLAB0[name] + b // 8 for b in range(i * kt, (i + 1) * kt) if b % 8 == 0] for i in range(nt)]

        def tile_loop(act, w, stages, each, ahead=2):
            need = [t for name, kt, nt in stages for t in schedule(name, kt, nt)]
            done = 0
            for i in range(len(need)):
                while done < min(i + ahead + 1, len(need)):
                    for n in need[done]:
                        w.act(act, n)
                    done += 1
                if each:
                    each(i)

        def pe_tiles(pe, w, name, kt, nt, x, t, ready, freed, rows=P, first=0):
            n_blocks = nt * kt
            for i in range(nt):
                j = (first + i) % 4
                if first + i >= 4:
                    pe.wait_ge(freed, first + i - 3)
                for k in range(kt):
                    b = i * kt + k
                    n, at = SLAB0[name] + b // 8, b % 8 * P
                    if w is None:
                        if b % 8 == 0:
                            slab_wait(pe, n)
                        pairs = [(ring[n % RING], x(k))]
                    else:
                        if b % 8 == 0:
                            hi, lo = w.wait(pe, n)
                        if i == 0:
                            x.wait(pe, k)
                        pairs = [(hi, x.hi[:, k, :]), (hi, x.lo[:, k, :]), (lo, x.hi[:, k, :])]
                    for s, (t0, t1) in enumerate(halves(t)):
                        for m, (wp, xp) in enumerate(pairs):
                            mm = nc.tensor.matmul(acc[j][0:rows, s, 0:t1 - t0], wp[:, at:at + rows], xp[:, t0:t1],
                                                  start=(k == 0 and m == 0),
                                                  stop=(k == kt - 1 and m == len(pairs) - 1))
                    last = b % 8 == 7 or b == n_blocks - 1
                    if k == kt - 1:
                        mm.then_inc(ready, 1)
                        if last:
                            freed_by[n] = (ready, first + i + 1)
                    elif last:
                        slab_done(mm, n)

        norm_sems = [sem("norm_" + n) for n in ("summed", "centred", "squared", "sq_used", "rooted", "scaled")]
        norm_base = [0] * len(norm_sems)

        def normalize(tag, src, dst, kt, t, mean, gain, bias=None, eps=EPS_RMS, func=None):
            centre = bias is not None
            summed, centred, squared, sq_used, rooted, scaled = norm_sems
            b_ = {id(s): norm_base[i] for i, s in enumerate(norm_sems)}
            for i, n in enumerate((1, kt, kt, kt, 1, kt)):
                norm_base[i] += n if centre or norm_sems[i] not in (summed, centred, scaled) else 0
            wait = lambda eng, s, n: eng.wait_ge(s, b_[id(s)] + n)
            with ExitStack() as ctx:
                sq = [sbt(ctx, f"{tag}_sq{i}", [P, t]) for i in range(4)]
                std = sbt(ctx, tag + "_std", [P, t])
                rstd = sbt(ctx, tag + "_rstd", [P, t])
                with block() as b:
                    @b.tensor
                    def _(pe):
                        if centre:
                            for k in range(kt):
                                for s, (lo, hi) in enumerate(halves(t)):
                                    mm = nc.tensor.matmul(acc[0][:, s, 0:hi - lo], mean, src(k)[:, lo:hi],
                                                          start=(k == 0), stop=(k == kt - 1))
                            mm.then_inc(summed, 1)
                        for k in range(kt):
                            wait(pe, squared, k + 1)
                            for s, (lo, hi) in enumerate(halves(t)):
                                mm = nc.tensor.matmul(acc[1][:, s, 0:hi - lo], mean, sq[k % 4][:, lo:hi],
                                                      start=(k == 0), stop=(k == kt - 1))
                            mm.then_inc(sq_used, 1)

                    @b.scalar
                    def _(act):
                        for k in range(kt):
                            if centre:
                                wait(act, centred, k + 1)
                            if k >= 4:
                                wait(act, sq_used, k - 3)
                            nc.scalar.activation(sq[k % 4][:, :], (dst if centre else src)(k),
                                                 ACT.Square).then_inc(squared, 1)
                        wait(act, sq_used, kt)
                        nc.scalar.activation(fold(std[:, :], t), A(1, t), ACT.Sqrt,
                                             bias=k0("eps", 1, eps)).then_inc(rooted, 1)
                        if centre:
                            for k in range(kt):
                                wait(act, scaled, k + 1)
                                nc.scalar.activation(dst(k), dst(k), func or ACT.Identity, scale=gain(k),
                                                     bias=bias(k))

                    @b.vector
                    def _(dve):
                        if centre:
                            wait(dve, summed, 1)
                            for k in range(kt):
                                nc.vector.tensor_tensor(fold(dst(k), t), fold(src(k), t), A(0, t),
                                                        ALU.subtract).then_inc(centred, 1)
                        wait(dve, rooted, 1)
                        link("dve", dve, nc.vector.reciprocal(rstd[:, :], std[:, :]))
                        if centre:
                            wait(dve, centred, kt)
                            wait(dve, squared, kt)
                            for k in range(kt):
                                nc.vector.tensor_tensor(dst(k), dst(k), rstd[:, :], ALU.mult).then_inc(scaled, 1)
                        else:
                            for k in range(kt):
                                nc.vector.scalar_tensor_tensor(out=dst(k), in0=src(k), scalar=gain(k),
                                                               in1=rstd[:, :], op0=ALU.mult, op1=ALU.mult)

        loaded = sem("inputs_loaded")

        def first_block(xt, x2_of):
            with ExitStack() as c1x:
                c1 = sbt(c1x, "c1", [P, N1])

                def k1(name, n=P, at=0):
                    return c1[:, C1[name] + at:C1[name] + at + n]

                h = sbt(c1x, "h", [P, KD, T1])

                with block() as b:
                    @b.sync
                    def _(sp):
                        sp.dma_start(xt[:, :, :], x_t).then_inc(loaded, 16)
                        sp.dma_start(c0[:, :], const0).then_inc(loaded, 16)
                        sp.dma_start(par[:, :], params_d).then_inc(loaded, 16)
                        sp.dma_start(c1[:, :], const1).then_inc(loaded, 16)
                        load_slabs(sp)
                        sp.wait_ge(loaded, 64)
                normalize("mix", lambda k: xt[:, k, :], lambda k: h[:, k, :], KD, T1, k0("mean1024"),
                          lambda k: pcol("norm_mix_g", k))
                with ExitStack() as att:
                    attention_part(att, xt, h, k1)
                out_projection(xt, h)
                normalize("ffn", lambda k: xt[:, k, :], lambda k: h[:, k, :], KD, T1, k0("mean1024"),
                          lambda k: pcol("norm_ffn_g", k))
                with ExitStack() as mx:
                    experts(mx, xt, h, k1)
            x2 = x2_of()
            normalize("final", lambda k: xt[:, k, :], lambda k: x2[:, k, META:T2], KD, T1, k0("mean1024"),
                      lambda k: pcol("final_norm_g", k))
            return x2

        def attention_part(att, xt, h, k1):
            qb, kb = sbt(att, "qb", [P, 4, T1]), sbt(att, "kb", [P, 4, T1])
            qi, ki = sbt(att, "qi", [P, 4, T1]), sbt(att, "ki", [P, T1])
            vb = sbt(att, "vb", [P, 4, 512])
            wi = sbt(att, "wi", [P, 4, HEADS])
            ga, gb = sbt(att, "ga", [P, KD, T1]), sbt(att, "gb", [P, KD, T1])
            cc = sbt(att, "cc", [P, 5, T1])
            kr = sbt(att, "kr", [P, T1])
            dests = ([("c_q", cc[:, i, :], None) for i in range(3)] + [("c_kv", cc[:, 3 + i, :], None) for i in range(2)]
                     + [("q_b", qb[:, i, :], None) for i in range(4)] + [("k_b", kb[:, i, :], None) for i in range(4)]
                     + [("q_i", qi[:, i, :], None) for i in range(4)] + [("k_i", ki[:, :], None)]
                     + [("k_r", kr[0:96, :], None)]
                     + [("g_a", ga[:, i, :], ACT.Sigmoid) for i in range(8)]
                     + [("g_b", gb[:, i, :], ACT.Sigmoid) for i in range(8)])
            tile_ready, tile_out = sem("in_ready"), sem("in_out")
            v_ready, v_out = sem("vb_ready"), sem("vb_out")
            in_names = [name for name, _ in SLAB_COUNTS[:9]]
            with ExitStack() as px, block() as b:
                hx = Operand(px, "in", KD, T1)
                w = Weights(px, "in")
                hx.start(lambda k: h[:, k, :])

                @b.tensor
                def _(pe):
                    i = 0
                    for name, n in SLAB_COUNTS[:9]:
                        pe_tiles(pe, w, name, KD, n, hx, T1, tile_ready, tile_out,
                                 rows=96 if name == "k_r" else P, first=i)
                        i += n
                    pe.wait_ge(tile_out, i)
                    for k in range(KD):
                        n = SLAB0["v_b"] + k // 2
                        if k % 2 == 0:
                            hi, lo = w.wait(pe, n)
                        for tok in range(4):
                            for m, (xp, wp) in enumerate(((hx.hi, hi), (hx.lo, hi), (hx.hi, lo))):
                                mm = nc.tensor.matmul(acc[tok][:, 0, :], xp[:, k, tok * P:(tok + 1) * P],
                                                      wp[:, k % 2 * 512:k % 2 * 512 + 512],
                                                      start=(k == 0 and m == 0), stop=(k == KD - 1 and m == 2))
                        if k % 2:
                            slab_done(mm, n)
                    for tok in range(4):
                        for k in range(KD):
                            o = PCOL["w_i"] + 8 * k
                            mm = nc.tensor.matmul(acc[tok][:, 1, 0:8], h[:, k, tok * P:(tok + 1) * P],
                                                  par[:, o:o + 8], start=(k == 0), stop=(k == KD - 1))
                        mm.then_inc(v_ready, 1)

                @b.scalar
                def _(act):
                    w.begin(act, ["c_q"], hx)

                    def take(i):
                        name, d, f = dests[i]
                        act.wait_ge(tile_ready, i + 1)
                        rows = 96 if name == "k_r" else P
                        nc.scalar.activation(d, acc[i % 4][0:rows, 0, :], f or ACT.Copy).then_inc(tile_out, 1)

                    tile_loop(act, w, [(name, KD, n) for name, n in SLAB_COUNTS[:9]], take)
                    w.all_act(act, ["v_b"])
                    for tok in range(4):
                        act.wait_ge(v_ready, tok + 1)
                        nc.scalar.activation(vb[:, tok, :], acc[tok][:, 0, :], ACT.Copy)
                        nc.scalar.activation(wi[:, tok, :], acc[tok][:, 1, 0:8], ACT.Copy, scale=HEADS ** -0.5)

                @b.vector
                def _(dve):
                    hx.dve(dve)

                @b.gpsimd
                def _(pool):
                    w.all_pool(pool, in_names + ["v_b"])

                @b.sync
                def _(sp):
                    load_slabs(sp, "v_b")

            normalize("cq", lambda k: cc[:, k, :], lambda k: cc[:, k, :], 3, T1, k1("mean384"),
                      lambda k: pcol("mla_q_norm_g", k))
            normalize("ckv", lambda k: cc[:, 3 + k, :], lambda k: cc[:, 3 + k, :], 2, T1, k1("mean256"),
                      lambda k: pcol("mla_kv_norm_g", k))
            late = att.enter_context(ExitStack())
            qa, ka = sbt(late, "qa", [P, HEADS, T1]), sbt(late, "ka", [P, HEADS, T1])
            va = sbt(late, "va", [P, 4, 512])
            up_ready, up_out, va_ready = sem("up_ready"), sem("up_out"), sem("va_ready")
            with block() as b:
                @b.tensor
                def _(pe):
                    pe_tiles(pe, None, "w_uq", 3, HEADS, lambda k: cc[:, k, :], T1, up_ready, up_out, rows=96)
                    pe_tiles(pe, None, "w_uk", 2, HEADS, lambda k: cc[:, 3 + k, :], T1, up_ready, up_out, rows=64, first=8)
                    pe.wait_ge(up_out, 16)
                    n = SLAB0["w_uv"]
                    slab_wait(pe, n)
                    for tok in range(4):
                        for k in range(2):
                            mm = nc.tensor.matmul(acc[tok][:, 0, :], cc[:, 3 + k, tok * P:(tok + 1) * P],
                                                  ring[n % RING][:, k * 512:k * 512 + 512],
                                                  start=(k == 0), stop=(k == 1))
                        mm.then_inc(va_ready, 1)
                    freed_by[n] = (va_ready, 4)

                @b.scalar
                def _(act):
                    for i in range(16):
                        act.wait_ge(up_ready, i + 1)
                        d, rows = (qa, 96) if i < 8 else (ka, 64)
                        nc.scalar.activation(d[0:rows, i % 8, :], acc[i % 4][0:rows, 0, :], ACT.Copy).then_inc(up_out, 1)
                    for tok in range(4):
                        act.wait_ge(va_ready, tok + 1)
                        nc.scalar.activation(va[:, tok, :], acc[tok][:, 0, :], ACT.Copy)

                @b.sync
                def _(sp):
                    load_slabs(sp, "w_uv")

            rope_tiles = ([(qb[:, i, :], 0) for i in range(4)] + [(kb[:, i, :], 0) for i in range(4)]
                          + [(qi[:, i, :], 0) for i in range(4)] + [(ki[:, :], 0)]
                          + [(kr[0:96, :], 1)] + [(qa[0:96, i, :], 1) for i in range(8)])
            turned, cosed, sined, roped = sem("turned"), sem("cosed"), sem("sined"), sem("roped")
            with ExitStack() as rx, block() as b:
                prod = [sbt(rx, f"rope_prod{i}", [P, T1]) for i in range(2)]

                @b.tensor
                def _(pe):
                    for i, (x, kind) in enumerate(rope_tiles):
                        rows = 96 if kind else P
                        if i >= 4:
                            pe.wait_ge(sined, i - 3)
                        rot = k1("rot96" if kind else "rot64")
                        nc.tensor.matmul(acc[i % 4][0:rows, 0, :], rot[0:rows, 0:rows], x, start=True,
                                         stop=True).then_inc(turned, 1)

                @b.vector
                def _(dve):
                    for i, (x, kind) in enumerate(rope_tiles):
                        rows = 96 if kind else P
                        dve.wait_ge(turned, i + 1)
                        if i >= 2:
                            dve.wait_ge(roped, i - 1)
                        nc.vector.tensor_tensor(prod[i % 2][0:rows, :], acc[i % 4][0:rows, 0, :],
                                                k1("sin96" if kind else "sin64", T1)[0:rows, :],
                                                ALU.mult).then_inc(sined, 1)
                        nc.vector.tensor_tensor(x, x, k1("cos96" if kind else "cos64", T1)[0:rows, :],
                                                ALU.mult).then_inc(cosed, 1)

                @b.gpsimd
                def _(pool):
                    for i, (x, kind) in enumerate(rope_tiles):
                        rows = 96 if kind else P
                        pool.wait_ge(sined, i + 1)
                        pool.wait_ge(cosed, i + 1)
                        nc.gpsimd.tensor_tensor(x, x, prod[i % 2][0:rows, :], ALU.add).then_inc(roped, 1)
                    pool.wait_ge(roped, len(rope_tiles))
                    for hd in range(HEADS):
                        link("pool", pool, nc.gpsimd.tensor_copy(ka[64:96, hd, :], kr[64:96, :]))

            sel = [None] + [sbt(late, f"sel{i}", [P, (i + 1) * P]) for i in range(1, 4)]
            logit_ready, logit_out, rel_used = sem("logit_ready"), sem("logit_out"), sem("rel_used")
            score_seen = sem("score_seen")
            with ExitStack() as ix, block() as b:
                rel = [sbt(ix, f"rel{i}", [P, T1]) for i in range(4)]
                best = sbt(ix, "best", [P, 8])
                units = [(qt, hd) for qt in range(1, 4) for hd in range(HEADS)]

                @b.tensor
                def _(pe):
                    for u, (qt, hd) in enumerate(units):
                        nk, r0 = (qt + 1) * P, 64 * (hd % 2)
                        if u >= 4:
                            pe.wait_ge(logit_out, u - 3)
                        nc.tensor.matmul(acc[u % 4][:, 0, 0:nk], qi[r0:r0 + 64, hd // 2, qt * P:(qt + 1) * P],
                                         ki[r0:r0 + 64, 0:nk], start=True, stop=True).then_inc(logit_ready, 1)

                @b.scalar
                def _(act):
                    for u, (qt, hd) in enumerate(units):
                        nk = (qt + 1) * P
                        act.wait_ge(logit_ready, u + 1)
                        if u >= 4:
                            act.wait_ge(rel_used, u - 3)
                        nc.scalar.activation(rel[u % 4][:, 0:nk], acc[u % 4][:, 0, 0:nk], ACT.Relu,
                                             scale=HD ** -0.5).then_inc(logit_out, 1)

                @b.vector
                def _(dve):
                    for u, (qt, hd) in enumerate(units):
                        nk, s = (qt + 1) * P, sel[qt]
                        dve.wait_ge(logit_out, u + 1)
                        w = wi[:, qt, hd:hd + 1]
                        if hd == 0:
                            ins = nc.vector.tensor_scalar(s[:, :], rel[u % 4][:, 0:nk], w, None, ALU.mult)
                        else:
                            dve.wait_ge(rel_used, u)
                            ins = nc.vector.scalar_tensor_tensor(out=s[:, :], in0=rel[u % 4][:, 0:nk], scalar=w,
                                                                 in1=s[:, :], op0=ALU.mult, op1=ALU.add)
                        ins.then_inc(rel_used, 1)
                        if hd < HEADS - 1:
                            continue
                        dve.wait_ge(rel_used, u + 1)
                        link("dve", dve, nc.vector.memset(s[0:64, nk - 64:nk], NEG))
                        for _r in range(TOPK // 8):
                            link("dve", dve, nc.vector.max(best[:, :], s[:, :]))
                            link("dve", dve, nc.vector.match_replace(s[:, :], best[:, :], s[:, :], TAKEN))
                        link("dve", dve, nc.vector.tensor_scalar(s[:, :], s[:, :], TAKEN / 2, NEG, ALU.is_gt, ALU.mult))

            oa, ob = cc, qi
            causal = lambda qt: k1("causal", (qt + 1) * P, T1 - (qt + 1) * P)
            attend("mla", lambda hd, lo, hi: qa[0:96, hd, lo:hi], lambda hd, n: ka[0:96, hd, 0:n], va,
                   causal, (NOPE + ROPE_D) ** -0.5, oa)
            attend("dsa", lambda hd, lo, hi: qb[64 * (hd % 2):64 * (hd % 2) + 64, hd // 2, lo:hi],
                   lambda hd, n: kb[64 * (hd % 2):64 * (hd % 2) + 64, hd // 2, 0:n], vb,
                   lambda qt: sel[qt][:, :] if qt else causal(0), HD ** -0.5, ob)
            late.close()
            oy_ready, oy_out, y_sum = sem("oy_ready"), sem("oy_out"), sem("y_sum")
            with ExitStack() as px, block() as b:
                ax, bx = Operand(px, "oa", 4, T1), Operand(px, "ob", 4, T1)
                w = Weights(px, "wo", 2)
                ax.start(lambda k: oa[:, k, :])
                bx.start(lambda k: ob[:, k, :])

                @b.tensor
                def _(pe):
                    pe_tiles(pe, w, "w_o_a", 4, KD, ax, T1, oy_ready, oy_out)
                    pe_tiles(pe, w, "w_o_b", 4, KD, bx, T1, oy_ready, oy_out, first=8)

                @b.scalar
                def _(act):
                    w.begin(act, ["w_o_a"], ax, bx)
                    w.all_act(act, ["w_o_a", "w_o_b"])

                @b.vector
                def _(dve):
                    ax.dve(dve)
                    bx.dve(dve)
                    for i in range(16):
                        dve.wait_ge(oy_ready, i + 1)
                        d, g = (h, ga) if i < 8 else (gb, gb)
                        nc.vector.tensor_tensor(d[:, i % 8, :], acc[i % 4][:, 0, :], g[:, i % 8, :],
                                                ALU.mult).then_inc(oy_out, 1)

                @b.gpsimd
                def _(pool):
                    w.all_pool(pool, ["w_o_a", "w_o_b"])
                    for i in range(8):
                        pool.wait_ge(oy_out, 9 + i)
                        link("pool", pool, nc.gpsimd.tensor_tensor(h[:, i, :], h[:, i, :], gb[:, i, :], ALU.add))

                @b.sync
                def _(sp):
                    load_slabs(sp, "w_o_b")

        def out_projection(xt, h):
            xo_ready, xo_out = sem("xo_ready"), sem("xo_out")
            with ExitStack() as px, block() as b:
                yx = Operand(px, "yo", KD, T1)
                w = Weights(px, "wout")
                yx.start(lambda k: h[:, k, :])

                @b.tensor
                def _(pe):
                    pe_tiles(pe, w, "w_out", KD, KD, yx, T1, xo_ready, xo_out)

                @b.scalar
                def _(act):
                    w.begin(act, ["w_out"], yx)
                    w.all_act(act, ["w_out"])

                @b.vector
                def _(dve):
                    yx.dve(dve)
                    for i in range(8):
                        dve.wait_ge(xo_ready, i + 1)
                        nc.vector.tensor_tensor(xt[:, i, :], xt[:, i, :], acc[i % 4][:, 0, :],
                                                ALU.add).then_inc(xo_out, 1)

                @b.gpsimd
                def _(pool):
                    w.all_pool(pool, ["w_out"])

                @b.sync
                def _(sp):
                    load_slabs(sp, "w_out")

        attend_sems = [sem("att_" + n) for n in ("s_ready", "s_out", "probs", "scaled", "pt_ready", "pt_out", "o_ready", "o_out")]
        attend_base = [0]

        def attend(tag, q, key, v, bias, scale, o):
            s_ready, s_out, probs, scaled, pt_ready, pt_out, o_ready, o_out = attend_sems
            u0 = attend_base[0]
            attend_base[0] += 4 * HEADS
            units = [(qt, hd) for qt in range(4) for hd in range(HEADS)]
            NU = len(units)
            NS = 4
            with ExitStack() as ax, block() as b:
                sc = [sbt(ax, f"{tag}_sc{i}", [P, T1]) for i in range(NS)]
                pt = [sbt(ax, f"{tag}_pt{i}", [P, T1]) for i in range(2)]
                mx = sbt(ax, f"{tag}_mx", [P, NU])
                nm = sbt(ax, f"{tag}_nm", [P, NU])
                rs = sbt(ax, f"{tag}_rs", [P, NU])
                ri = sbt(ax, f"{tag}_ri", [P, NU])
                sbank = lambda u: acc[u % 4 // 2][:, u % 2, :]

                @b.tensor
                def _(pe):
                    def scores(u):
                        qt, hd = units[u]
                        if u >= 4:
                            pe.wait_ge(s_out, u0 + u - 3)
                        nc.tensor.matmul(sbank(u)[:, 0:(qt + 1) * P], q(hd, qt * P, (qt + 1) * P),
                                         key(hd, (qt + 1) * P), start=True, stop=True).then_inc(s_ready, 1)

                    def turn(u):
                        qt, hd = units[u]
                        pe.wait_ge(scaled, u0 + u + 1)
                        if u >= 2:
                            pe.wait_ge(pt_out, u0 + u - 1)
                        for kt in range(qt + 1):
                            mm = nc.tensor.transpose(acc[2][:, u % 2, kt * P:(kt + 1) * P],
                                                     sc[u % NS][:, kt * P:(kt + 1) * P], k0("ident"))
                        mm.then_inc(pt_ready, 1)

                    def values(u):
                        qt, hd = units[u]
                        r0 = 64 * (hd % 2)
                        pe.wait_ge(pt_out, u0 + u + 1)
                        if u >= 2:
                            pe.wait_ge(o_out, u0 + u - 1)
                        for kt in range(qt + 1):
                            mm = nc.tensor.matmul(acc[3][r0:r0 + 64, u % 2, 0:P], v[:, kt, hd * 64:hd * 64 + 64],
                                                  pt[u % 2][:, kt * P:(kt + 1) * P], start=(kt == 0), stop=(kt == qt))
                        mm.then_inc(o_ready, 1)

                    scores(0)
                    scores(1)
                    for u in range(NU + 1):
                        if u + 2 < NU:
                            scores(u + 2)
                        if u < NU:
                            turn(u)
                        if u >= 1:
                            values(u - 1)

                @b.vector
                def _(dve):
                    def add_bias(u):
                        nk = (units[u][0] + 1) * P
                        dve.wait_ge(s_ready, u0 + u + 1)
                        if u >= NS:
                            dve.wait_ge(pt_ready, u0 + u - NS + 1)
                        nc.vector.tensor_tensor_reduce(sc[u % NS][:, 0:nk], sbank(u)[:, 0:nk], bias(units[u][0]),
                                                       1.0, -3e38, ALU.add, ALU.max, mx[:, u:u + 1]).then_inc(s_out, 1)

                    def normal(u):
                        nk = (units[u][0] + 1) * P
                        dve.wait_ge(probs, u0 + u + 1)
                        link("dve", dve, nc.vector.reciprocal(ri[:, u:u + 1], rs[:, u:u + 1]))
                        nc.vector.tensor_scalar(sc[u % NS][:, 0:nk], sc[u % NS][:, 0:nk], ri[:, u:u + 1], None,
                                                ALU.mult).then_inc(scaled, 1)

                    add_bias(0)
                    for u in range(NU):
                        if u + 1 < NU:
                            add_bias(u + 1)
                        normal(u)

                @b.scalar
                def _(act):
                    def exps(u):
                        nk = (units[u][0] + 1) * P
                        act.wait_ge(s_out, u0 + u + 1)
                        link("act", act, nc.scalar.activation(nm[:, u:u + 1], mx[:, u:u + 1], ACT.Copy, scale=-scale))
                        nc.scalar.activation(sc[u % NS][:, 0:nk], sc[u % NS][:, 0:nk], ACT.Exp, bias=nm[:, u:u + 1],
                                             scale=scale, accum_out=rs[:, u:u + 1]).then_inc(probs, 1)

                    def evacuate(u):
                        nk = (units[u][0] + 1) * P
                        act.wait_ge(pt_ready, u0 + u + 1)
                        if u >= 2:
                            act.wait_ge(o_ready, u0 + u - 1)
                        nc.scalar.activation(pt[u % 2][:, 0:nk], acc[2][:, u % 2, 0:nk], ACT.Copy).then_inc(pt_out, 1)

                    def store(u):
                        qt, hd = units[u]
                        r0 = 64 * (hd % 2)
                        act.wait_ge(o_ready, u0 + u + 1)
                        nc.scalar.activation(o[r0:r0 + 64, hd // 2, qt * P:(qt + 1) * P], acc[3][r0:r0 + 64, u % 2, 0:P],
                                             ACT.Copy).then_inc(o_out, 1)

                    exps(0)
                    for u in range(NU + 1):
                        if u + 1 < NU:
                            exps(u + 1)
                        if u < NU:
                            evacuate(u)
                        if u >= 1:
                            store(u - 1)

        def route(h, k1, h_hi, h_lo, comb, rank, passes):
            logits_ready, biased, hot_made, ranked = sem("rt_logits"), sem("rt_biased"), sem("rt_hot"), sem("rt_ranked")
            shifted, exped, paired, exped2 = sem("rt_shifted"), sem("rt_exped"), sem("rt_paired"), sem("rt_exped2")
            turned, rounded, parted = sem("rt_turned"), sem("rt_rounded"), sem("rt_parted")
            with ExitStack() as rx, block() as b:
                rb = sbt(rx, "rt_bias", [P, 40])
                lg = sbt(rx, "rt_lg", [P, 4, 40])
                df, e1 = sbt(rx, "rt_df", [P, 4, 8]), sbt(rx, "rt_e1", [P, 4, 8])
                g8, hot = sbt(rx, "rt_g8", [P, 4, 8]), sbt(rx, "rt_hot8", [P, 4, 8])
                t32, a32, b32 = (sbt(rx, f"rt_{n}32", [P, 4, 32]) for n in "tab")
                small = sbt(rx, "rt_small", [P, 10, 4])
                cnt = sbt(rx, "rt_cnt", [P, 4])

                def bc(i, n):
                    return small[:, i, :].unsqueeze(2).to_broadcast([P, 4, n])

                @b.sync
                def _(sp):
                    sp.dma_start(rb[:, :], router_bias.to_broadcast([P, 40])).then_inc(biased, 16)
                    sp.wait_ge(biased, 16)

                @b.tensor
                def _(pe):
                    for tok in range(4):
                        for k in range(KD):
                            o = PCOL["router"] + 40 * k
                            mm = nc.tensor.matmul(acc[tok][:, 0, 0:40], h[:, k, tok * P:(tok + 1) * P],
                                                  par[:, o:o + 40], start=(k == 0), stop=(k == KD - 1))
                        mm.then_inc(logits_ready, 1)
                    for i in range(8):
                        if i >= 4:
                            pe.wait_ge(parted, i - 3)
                        tok, half = i // 2, i % 2
                        for q in range(4):
                            mm = nc.tensor.transpose(acc[i % 4][:, 1, q * P:(q + 1) * P],
                                                     h[:, 4 * half + q, tok * P:(tok + 1) * P], k0("ident"))
                        mm.then_inc(turned, 1)
                    pe.wait_ge(hot_made, 1)
                    for tok in range(4):
                        for t in range(tok + 1):
                            nc.tensor.matmul(acc[0][:, 0, 8 * tok:8 * tok + 8], k1("before" if t == tok else "ones"),
                                             hot[:, t, :], start=(t == 0), stop=(t == tok))
                    for t in range(4):
                        mm = nc.tensor.matmul(acc[0][:, 0, 32:40], k1("ones"), hot[:, t, :], start=(t == 0), stop=(t == 3))
                    mm.then_inc(ranked, 1)

                @b.vector
                def _(dve):
                    v = nc.vector
                    L = lambda ins: link("dve", dve, ins)
                    dve.wait_ge(biased, 16)
                    for tok in range(4):
                        dve.wait_ge(logits_ready, tok + 1)
                        L(v.tensor_tensor(lg[:, tok, :], acc[tok][:, 0, 0:40], rb[:, :], ALU.add))
                    for i in range(8):
                        dve.wait_ge(rounded, i + 1)
                        at = slice(i % 2 * 512, i % 2 * 512 + 512)
                        v.tensor_tensor(h_lo[:, i // 2, at], acc[i % 4][:, 1, :], h_hi[:, i // 2, at].bitcast(F32),
                                        ALU.subtract).then_inc(parted, 1)
                    G = lg[:, :, 0:8]
                    row = lambda i: small[:, i, :]

                    def first_best(x, top, n, rev, tmp, best, signal=None):
                        L(v.tensor_reduce(row(top), x, AX, ALU.max))
                        L(v.tensor_tensor(tmp, x, bc(top, n), ALU.is_equal))
                        L(v.tensor_tensor(tmp, tmp, rev.unsqueeze(1).to_broadcast([P, 4, n]), ALU.mult))
                        L(v.tensor_reduce(row(9), tmp, AX, ALU.max))
                        ins = v.tensor_tensor(best, tmp, bc(9, n), ALU.is_equal)
                        if signal is None:
                            L(ins)
                        else:
                            ins.then_inc(signal, 1)
                            dve.wait_ge(signal, 1)

                    first_best(G, 0, 8, k1("rev8", 8), g8[:, :, :], hot[:, :, :], hot_made)
                    v.tensor_tensor(df[:, :, :], G, bc(0, 8), ALU.subtract).then_inc(shifted, 1)
                    L(v.tensor_scalar(g8[:, :, :], hot[:, :, :], -NEG, NEG, ALU.mult, ALU.add))
                    for tok in range(4):
                        L(v.tensor_tensor(comb[:, tok, 0:N_EXP].rearrange("p (g e) -> p g e", g=8),
                                          lg[:, tok, 8:40].rearrange("p (g e) -> p g e", g=8),
                                          g8[:, tok, :].unsqueeze(2).to_broadcast([P, 8, 4]), ALU.add))
                    first_best(comb[:, :, 0:N_EXP], 1, 32, k1("rev32", 32), t32[:, :, :], a32[:, :, :])
                    L(v.tensor_scalar(t32[:, :, :], a32[:, :, :], 2 * NEG, None, ALU.mult))
                    L(v.tensor_tensor(comb[:, :, 0:N_EXP], comb[:, :, 0:N_EXP], t32[:, :, :], ALU.add))
                    first_best(comb[:, :, 0:N_EXP], 2, 32, k1("rev32", 32), t32[:, :, :], b32[:, :, :])
                    v.tensor_tensor(row(3), row(2), row(1), ALU.subtract).then_inc(paired, 1)
                    dve.wait_ge(exped, 1)
                    L(v.tensor_reduce(row(4), e1[:, :, :], AX, ALU.add))
                    L(v.reciprocal(row(4), row(4)))
                    dve.wait_ge(exped2, 1)
                    L(v.tensor_scalar(row(6), row(5), 1.0, None, ALU.add))
                    L(v.reciprocal(row(6), row(6)))
                    L(v.tensor_tensor(row(6), row(6), row(4), ALU.mult))
                    L(v.tensor_tensor(row(7), row(6), row(5), ALU.mult))
                    L(v.tensor_tensor(a32[:, :, :], a32[:, :, :], bc(6, 32), ALU.mult))
                    L(v.tensor_tensor(b32[:, :, :], b32[:, :, :], bc(7, 32), ALU.mult))
                    L(v.tensor_tensor(comb[:, :, 0:N_EXP], a32[:, :, :], b32[:, :, :], ALU.add))
                    L(v.tensor_copy(comb[:, :, N_EXP:], comb[:, :, 0:4]))
                    dve.wait_ge(ranked, 1)
                    L(v.tensor_scalar(rank[:, :, 0:8], acc[0][:, 0, 0:32].rearrange("p (t g) -> p t g", t=4), AWAY, None, ALU.add))
                    L(v.tensor_tensor(rank[:, :, 0:8], rank[:, :, 0:8], hot[:, :, :], ALU.mult))
                    L(v.tensor_scalar(rank[:, :, 0:8], rank[:, :, 0:8], -AWAY, None, ALU.add))
                    L(v.tensor_scalar(rank[:, :, 8:9], rank[:, :, 0:1], -float(P), None, ALU.add))
                    L(v.tensor_reduce(cnt[:, 0:1], acc[0][:, 0, 32:40], AX, ALU.max))
                    for i in range(1, 4):
                        L(v.tensor_scalar(cnt[:, i:i + 1], cnt[:, 0:1], i * P + 0.5, None, ALU.is_gt))
                    L(v.tensor_reduce(cnt[:, 0:1], cnt[:, 1:4], AX, ALU.add))
                    L(v.tensor_scalar(passes[:, :], cnt[:, 0:1], 1.0, None, ALU.add))

                @b.scalar
                def _(act):
                    for i in range(8):
                        act.wait_ge(turned, i + 1)
                        nc.scalar.activation(h_hi[:, i // 2, i % 2 * 512:i % 2 * 512 + 512], acc[i % 4][:, 1, :],
                                             ACT.Copy).then_inc(rounded, 1)
                    act.wait_ge(shifted, 1)
                    nc.scalar.activation(e1[:, :, :], df[:, :, :], ACT.Exp).then_inc(exped, 1)
                    act.wait_ge(paired, 1)
                    nc.scalar.activation(small[:, 5, :], small[:, 3, :], ACT.Exp).then_inc(exped2, 1)

        def experts(mx, xt, h, k1):
            h_hi, h_lo = (sbt(mx, "h_tok_" + n, [P, 4, D], F32R) for n in ("hi", "lo"))
            comb, rank = sbt(mx, "comb", [P, 4, N_EXP + 4]), sbt(mx, "rank", [P, 4, GROUPS + 1])
            passes = mx.enter_context(nc.sbuf_tensor("passes", [P, 1], mybir.dt.int32))
            route(h, k1, h_hi, h_lo, comb, rank, passes)
            PER = len(MOE_ORDER)
            AHEAD = MOE_AHEAD
            number = {key: u for u, key in enumerate(MOE_ORDER)}
            slab_here = [sem(f"moe_in{j}") for j in range(AHEAD)]
            w_hi, w_lo, w_used = sem("moe_w_hi"), [sem("moe_w_lo_even"), sem("moe_w_lo_odd")], sem("moe_w_used")
            onehot, onehot_t, onehot_tc = sem("onehot_made"), sem("onehot_turned"), sem("onehot_copied")
            gathered, g_hi, g_lo, c_ready, c_copied = sem("gathered"), sem("g_hi"), sem("g_lo"), sem("c_ready"), sem("c_copied")
            silued, hid_made, hid_turned = sem("silued"), sem("hid_made"), sem("hid_turned")
            hid_hi, hid_lo, y_hi, y_lo = sem("hid_hi"), sem("hid_lo"), sem("y_hi"), sem("y_lo")
            scattered, added, moved_on = sem("scattered"), sem("moe_added"), sem("moved_on")
            bank = lambda i: acc[i // 2][:, i % 2, :]
            SCAT = [2, 3, 7]
            with ExitStack() as ex, block() as b:
                ringm = [sbt(ex, f"moe_ring{j}", [P, 1024]) for j in range(AHEAD)]
                whi = [sbt(ex, f"moe_whi{j}", [P, 1024], F32R) for j in range(AHEAD)]
                wlo = [sbt(ex, f"moe_wlo{j}", [P, 1024], F32R) for j in range(AHEAD)]
                gm, gmt = sbt(ex, "onehot", [P, 4, P], F32R), sbt(ex, "onehot_t", [P, T1], F32R)
                hg = [sbt(ex, "h_slots_" + n, [P, KD * P], F32R) for n in ("hi", "lo")]
                ys = [sbt(ex, "y_slots_" + n, [P, D], F32R) for n in ("hi", "lo")]
                cs = sbt(ex, "comb_slots", [P, 4])
                sl, hid = [[sbt(ex, f"{n}{i}", [P, FF]) for i in range(2)] for n in ("silu", "hid")]
                hidt = [[sbt(ex, f"hid_t{i}_{n}", [P, FF], F32R) for n in ("hi", "lo")] for i in range(2)]

                def groups(eng, body, end=None):
                    count = eng.value_load(passes[0:1, 0:1], min_val=1, max_val=T1 // P)
                    with eng.Fori(0, count) as ps:
                        with eng.Fori(0, GROUPS) as g:
                            body(ps * GROUPS + g, g)
                        if end:
                            end(ps)

                def round_slab(act, n, u, first=False):
                    act.wait_ge(slab_here[u % AHEAD], n * (16 * PER // AHEAD) + 16 * (u // AHEAD + 1))
                    if not first:
                        act.wait_ge(w_used, n * PER + u - AHEAD + 1)
                    nc.scalar.activation(whi[u % AHEAD][:, :], ringm[u % AHEAD][:, :], ACT.Copy).then_inc(w_hi, 1)

                def rest_slab(eng, tensor_tensor, n, u):
                    eng.wait_ge(w_hi, n * PER + u + 1)
                    tensor_tensor(wlo[u % AHEAD][:, :], ringm[u % AHEAD][:, :], whi[u % AHEAD][:, :].bitcast(F32),
                                  ALU.subtract).then_inc(w_lo[u % 2], 1)

                def rest_made(eng, n, u):
                    eng.wait_ge(w_lo[u % 2], n * (PER // 2) + u // 2 + 1)

                @b.sync
                def _(sp):
                    sp.sem_inc(added, 1)

                    def load(g, u):
                        sp.dma_start(ringm[u % AHEAD][:, :], moe_slabs[bass.ds(g * PER + u, 1)]
                                     .rearrange("a p n -> (a p) n")).then_inc(slab_here[u % AHEAD], 16)

                    for u in range(AHEAD):
                        sp.dma_start(ringm[u][:, :], moe_slabs[u]).then_inc(slab_here[u], 16)

                    def body(n, g):
                        for u in range(PER):
                            rest_made(sp, n, u)
                            load(g, u + AHEAD)

                    groups(sp, body)

                @b.tensor
                def _(pe):
                    mmul = nc.tensor.matmul

                    def gather(n, columns):
                        pe.wait_ge(onehot, n + 1)
                        for k in range(KD):
                            for t in range(4):
                                for m, x in enumerate((h_hi, h_lo)):
                                    mm = mmul(bank(5 + k // 4)[:, k % 4 * P:k % 4 * P + P], x[:, t, k * P:(k + 1) * P],
                                              gm[:, t, :], start=(t == 0 and m == 0), stop=(t == 3 and m == 1))
                            if k % 4 == 3:
                                mm.then_inc(gathered, 1)
                        for t in range(4):
                            mm = mmul(bank(4)[:, 0:4], gm[:, t, :].bitcast(F32), comb[:, t, columns], start=(t == 0), stop=(t == 3))
                        mm.then_inc(c_ready, 1)

                    def turn_onehot():
                        for t in range(4):
                            mm = nc.tensor.transpose(bank(7)[:, t * P:(t + 1) * P], gm[:, t, :].bitcast(F32), k0("ident"))
                        mm.then_inc(onehot_t, 1)

                    def body(n, g):
                        def slab(u):
                            rest_made(pe, n, u)
                            return whi[u % AHEAD], wlo[u % AHEAD]

                        def gate_up(e):
                            if e >= 2:
                                pe.wait_ge(hid_made, n * 4 + e - 1)
                            for i in range(4):
                                hi, lo = slab(number["gate_up", e, i])
                                for q in range(2):
                                    k = 2 * i + q
                                    for m, (x, w) in enumerate(((hg[0], hi), (hg[1], hi), (hg[0], lo))):
                                        mm = mmul(bank(e % 2), x[:, k * P:(k + 1) * P], w[:, q * 512:q * 512 + 512],
                                                  start=(k == 0 and m == 0), stop=(k == KD - 1 and m == 2))
                                mm.then_inc(w_used, 1)

                        def turn(e):
                            pe.wait_ge(hid_made, n * 4 + e + 1)
                            if e == 0:
                                pe.wait_ge(c_copied, n + 1)
                            else:
                                pe.wait_ge(hid_lo, n * 4 + e)
                            for f in range(2):
                                mm = nc.tensor.transpose(bank(4)[:, f * P:(f + 1) * P], hid[e % 2][:, f * P:(f + 1) * P], k0("ident"))
                            mm.then_inc(hid_turned, 1)

                        def down(e):
                            if e == 0:
                                pe.wait_ge(added, n * KD + 1)
                            pe.wait_ge(hid_lo, n * 4 + e + 1)
                            for f in range(2):
                                hi, lo = slab(number["down", e, f])
                                x_hi_, x_lo_ = hidt[e % 2]
                                for half in range(2):
                                    for m, (x, w) in enumerate(((x_hi_, hi), (x_lo_, hi), (x_hi_, lo))):
                                        mm = mmul(bank(2 + half), x[:, f * P:(f + 1) * P], w[:, half * 512:half * 512 + 512],
                                                  start=(e == 0 and f == 0 and m == 0), stop=(e == 3 and f == 1 and m == 2))
                                mm.then_inc(w_used, 1)

                        pe.wait_ge(g_lo, n * 2 + 2)
                        gate_up(0)
                        gate_up(1)
                        turn(0)
                        gate_up(2)
                        down(0)
                        turn(1)
                        gate_up(3)
                        turn(2)
                        down(1)
                        turn(3)
                        down(2)
                        down(3)
                        gather(n + 1, bass.ds(g * 4 + 4, 4))
                        pe.wait_ge(y_lo, n * 2 + 2)
                        pe.wait_ge(onehot_tc, n + 1)
                        for k in range(KD):
                            if k >= 3:
                                pe.wait_ge(added, n * KD + k - 1)
                            for m in range(2):
                                mm = mmul(bank(SCAT[k % 3]), ys[m][:, k * P:(k + 1) * P], gmt[:, :], start=(m == 0), stop=(m == 1))
                            mm.then_inc(scattered, 1)
                        pe.wait_ge(added, n * KD + 7)
                        turn_onehot()

                    gather(0, slice(0, 4))
                    turn_onehot()
                    groups(pe, body)

                @b.scalar
                def _(act):
                    cp_ = lambda d, s_: nc.scalar.activation(d, s_, ACT.Copy)

                    def slots(n):
                        for i in range(2):
                            act.wait_ge(gathered, n * 2 + i + 1)
                            cp_(hg[0][:, 512 * i:512 * i + 512], bank(5 + i)).then_inc(g_hi, 1)
                        act.wait_ge(c_ready, n + 1)
                        cp_(cs[:, :], bank(4)[:, 0:4]).then_inc(c_copied, 1)

                    def copy_onehot(n):
                        act.wait_ge(onehot_t, n + 1)
                        cp_(gmt[:, :], bank(7)).then_inc(onehot_tc, 1)

                    def body(n, g):
                        def rounds(lo, hi):
                            for u in range(lo, hi):
                                round_slab(act, n, u + AHEAD)

                        def silu(e):
                            act.wait_ge(w_used, n * PER + number["gate_up", e, 3] + 1)
                            if e >= 2:
                                act.wait_ge(hid_made, n * 4 + e - 1)
                            nc.scalar.activation(sl[e % 2][:, :], bank(e % 2)[:, 0:FF], ACT.Silu).then_inc(silued, 1)

                        def turn(e):
                            act.wait_ge(hid_turned, n * 4 + e + 1)
                            cp_(hidt[e % 2][0][:, :], bank(4)[:, 0:FF]).then_inc(hid_hi, 1)

                        rounds(0, 4)
                        silu(0)
                        rounds(4, 8)
                        silu(1)
                        turn(0)
                        rounds(8, 12)
                        silu(2)
                        rounds(12, 14)
                        turn(1)
                        rounds(14, 18)
                        silu(3)
                        turn(2)
                        rounds(18, 20)
                        turn(3)
                        rounds(20, 22)
                        act.wait_ge(w_used, n * PER + PER)
                        for i in range(2):
                            cp_(ys[0][:, i * 512:i * 512 + 512], bank(2 + i)).then_inc(y_hi, 1)
                        slots(n + 1)
                        rounds(22, 24)
                        copy_onehot(n + 1)

                    for u in range(AHEAD):
                        round_slab(act, 0, u, first=True)
                    slots(0)
                    copy_onehot(0)
                    groups(act, body)

                @b.gpsimd
                def _(pool):
                    def body(n, g):
                        for u in range(0, PER, 2):
                            rest_slab(pool, nc.gpsimd.tensor_tensor, n, u + AHEAD)

                    for u in range(0, AHEAD, 2):
                        rest_slab(pool, nc.gpsimd.tensor_tensor, 0, u)
                    groups(pool, body, lambda ps: pool.wait_ge(w_lo[0], ps * (GROUPS * PER // 2) + (GROUPS * PER + AHEAD) // 2))

                @b.vector
                def _(dve):
                    tt = nc.vector.tensor_tensor

                    def make_onehot(col):
                        for t in range(4):
                            ins = nc.vector.tensor_scalar(gm[:, t, :], k1("iota"), rank[:, t, col], None, ALU.is_equal)
                        ins.then_inc(onehot, 1)

                    def slots(n):
                        for i in range(2):
                            dve.wait_ge(g_hi, n * 2 + i + 1)
                            at = slice(512 * i, 512 * i + 512)
                            tt(hg[1][:, at], bank(5 + i), hg[0][:, at].bitcast(F32), ALU.subtract).then_inc(g_lo, 1)

                    def body(n, g):
                        def rests(lo, hi):
                            for u in range(lo, hi):
                                if u % 2:
                                    rest_slab(dve, tt, n, u + AHEAD)

                        def hidden(e):
                            dve.wait_ge(silued, n * 4 + e + 1)
                            if e == 0:
                                dve.wait_ge(c_copied, n + 1)
                            if e >= 2:
                                dve.wait_ge(hid_turned, n * 4 + e - 1)
                            nc.vector.scalar_tensor_tensor(out=hid[e % 2][:, :], in0=sl[e % 2][:, :], scalar=cs[:, e:e + 1],
                                                           in1=bank(e % 2)[:, FF:2 * FF], op0=ALU.mult,
                                                           op1=ALU.mult).then_inc(hid_made, 1)

                        def turn(e):
                            dve.wait_ge(hid_hi, n * 4 + e + 1)
                            tt(hidt[e % 2][1][:, :], bank(4)[:, 0:FF], hidt[e % 2][0][:, :].bitcast(F32),
                               ALU.subtract).then_inc(hid_lo, 1)

                        dve.wait_ge(onehot_t, n + 1)
                        make_onehot(bass.ds(g + 1, 1))
                        rests(0, 4)
                        hidden(0)
                        rests(4, 8)
                        hidden(1)
                        turn(0)
                        rests(8, 12)
                        hidden(2)
                        rests(12, 14)
                        turn(1)
                        rests(14, 18)
                        hidden(3)
                        turn(2)
                        rests(18, 20)
                        turn(3)
                        rests(20, 22)
                        for i in range(2):
                            dve.wait_ge(y_hi, n * 2 + i + 1)
                            at = slice(512 * i, 512 * i + 512)
                            tt(ys[1][:, at], bank(2 + i), ys[0][:, at].bitcast(F32), ALU.subtract).then_inc(y_lo, 1)
                        slots(n + 1)
                        for k in range(KD):
                            dve.wait_ge(scattered, n * KD + k + 1)
                            tt(xt[:, k, :], xt[:, k, :], bank(SCAT[k % 3]), ALU.add).then_inc(added, 1)
                        rests(22, 24)

                    def next_pass(ps):
                        dve.wait_ge(onehot, ps * GROUPS + GROUPS + 1)
                        nc.vector.tensor_scalar(rank[:, :, :], rank[:, :, :], -float(P), None, ALU.add).then_inc(moved_on, 1)
                        dve.wait_ge(moved_on, ps + 1)

                    make_onehot(slice(0, 1))
                    for u in range(1, AHEAD, 2):
                        rest_slab(dve, tt, 0, u)
                    slots(0)
                    groups(dve, body, next_pass)

        def second_block(h):
            with ExitStack() as sx:
                c2 = sbt(sx, "c2", [P, N2])

                def k2(name, n=P, at=0):
                    return c2[:, C2[name] + at:C2[name] + at + n]

                ht = lambda k: h[:, k, :]
                const2_in, meta_in = sem("const2_in"), sem("meta_in")
                with block() as b:
                    @b.sync
                    def _(sp):
                        sp.dma_start(c2[:, :], const2).then_inc(const2_in, 16)
                        sp.wait_ge(const2_in, 16)

                    @b.vector
                    def _(dve):
                        o = PCOL["meta"]
                        nc.vector.tensor_copy(h[:, :, 0:META], par[:, o:o + 8 * META].rearrange("p (k t) -> p k t", k=8))
                normalize("lnin", ht, ht, KD, T2, k0("mean1024"), lambda k: pcol("ln_in_g", k),
                          lambda k: pcol("ln_in_b", k), EPS_LN)
                with ExitStack() as rx:
                    mixers(rx, h, k2)
            ffn(h)

        def mixers(rx, h, k2):
            spilled = sem("spilled")
            wa, xg = sbt(rx, "wa", [P, T2]), sbt(rx, "xg", [P, 2, T2])
            r, k, v = (sbt(rx, n, [P, KD, T2]) for n in ("rw_r", "rw_k", "rw_v"))
            with ExitStack() as cx:
                cp, cv = sbt(cx, "cp", [P, KD, TAPS - 1 + T2]), sbt(cx, "cv", [P, KD, T2])
                glu_ready, glu_sig, glu_out = sem("glu_ready"), sem("glu_sig"), sem("glu_out")
                px = cx.enter_context(ExitStack())
                hx = Operand(px, "h", KD, T2)
                w = Weights(px, "h", 3)
                hx.start(lambda q: h[:, q, :])
                with ExitStack() as gx, block() as b:
                    sg = [sbt(gx, f"glu_sg{i}", [P, T2]) for i in range(2)]

                    @b.tensor
                    def _(pe):
                        pe_tiles(pe, w, "conv_in", KD, 16, hx, T2, glu_ready, glu_out)

                    @b.scalar
                    def _(act):
                        w.begin(act, ["conv_in"], hx)

                        def take(t):
                            i = t // 2
                            if t % 2 == 0:
                                return
                            act.wait_ge(glu_ready, 2 * i + 2)
                            if i >= 2:
                                act.wait_ge(glu_out, 2 * i - 2)
                            nc.scalar.activation(fold(sg[i % 2][:, :], T2), A(2 * i % 4 + 1, T2),
                                                 ACT.Sigmoid).then_inc(glu_sig, 1)

                        tile_loop(act, w, [("conv_in", KD, 16)], take)

                    @b.vector
                    def _(dve):
                        hx.dve(dve)
                        nc.vector.memset(cp[:, :, 0:TAPS - 1], 0.0)
                        for i in range(8):
                            dve.wait_ge(glu_sig, i + 1)
                            nc.vector.tensor_tensor(fold(cp[:, i, TAPS - 1:], T2), fold(sg[i % 2][:, :], T2),
                                                    A(2 * i % 4, T2), ALU.mult).then_inc(glu_out, 2)

                    @b.gpsimd
                    def _(pool):
                        w.all_pool(pool, ["conv_in"])

                    @b.sync
                    def _(sp):
                        load_slabs(sp, "conv_in")
                y1 = lambda q: cp[:, q, 0:T2]
                tap_done = sem("tap_done")
                rw_ready, rw_read, rw_mixed, zeroed = sem("rw_ready"), sem("rw_read"), sem("rw_mixed"), sem("rw_zeroed")
                rw_names = (("rw_r", 8), ("rw_k", 8), ("rw_v", 8), ("rw_wa", 1), ("rw_g", 2), ("gate_a", 8))
                rw_dest = ([r[:, i, :] for i in range(8)] + [k[:, i, :] for i in range(8)]
                           + [v[:, i, :] for i in range(8)] + [wa[:, :]] + [xg[:, i, :] for i in range(2)])
                with ExitStack() as tx, block() as b:
                    sh = [sbt(tx, f"shift{i}", [P, T2 + 1]) for i in range(3)]
                    keep = sbt(tx, "keep", [P, 27])
                    o_mu = PCOL["mu"]

                    @b.tensor
                    def _(pe):
                        i = 0
                        for name, n in rw_names:
                            pe_tiles(pe, w, name, KD, n, hx, T2, rw_ready, rw_read, first=i)
                            i += n

                    @b.scalar
                    def _(act):
                        act.wait_ge(zeroed, 4)

                        def take(i):
                            act.wait_ge(rw_ready, i + 1)
                            if i >= 27:
                                act.wait_ge(tap_done, 8 * TAPS - 7 + i - 27)
                                nc.scalar.activation(fold(y1(i - 27), T2), A(i % 4, T2), ACT.Sigmoid,
                                                     bias=pcol("b_gate", i - 27)).then_inc(rw_read, 1)
                                return
                            nc.scalar.activation(fold(rw_dest[i], T2), A(i % 4, T2), ACT.Copy, scale=keep[:, i:i + 1])
                            if i >= 3:
                                act.wait_ge(rw_mixed, i - 2)
                            nc.scalar.activation(fold(sh[i % 3][:, 1:T2 + 1], T2), A(i % 4, T2), ACT.Copy,
                                                 scale=par[:, o_mu + i:o_mu + i + 1]).then_inc(rw_read, 1)

                        tile_loop(act, w, [(name, KD, n) for name, n in rw_names], take)

                    @b.gpsimd
                    def _(pool):
                        nc.gpsimd.tensor_scalar(keep[:, :], par[:, o_mu:o_mu + 27], -1.0, 1.0, ALU.mult,
                                                ALU.add).then_inc(zeroed, 1)
                        for i in range(3):
                            nc.gpsimd.memset(sh[i][:, 0:1], 0.0).then_inc(zeroed, 1)
                        pool.wait_ge(zeroed, 4)
                        parts = slab_range(*(name for name, n in rw_names))
                        for n in parts[:3]:
                            w.pool(pool, n)
                        for i, d in enumerate(rw_dest):
                            pool.wait_ge(rw_read, i + 1)
                            nc.gpsimd.tensor_tensor(d, d, sh[i % 3][:, 0:T2], ALU.add).then_inc(rw_mixed, 1)
                            w.pool(pool, parts[i + 3])
                        for n in parts[30:]:
                            w.pool(pool, n)
                        pool.wait_ge(rw_mixed, 27)
                        pool.wait_ge(lo_made, split_rank[n] + 1)

                    @b.vector
                    def _(dve):
                        o_w, o_b = PCOL["conv_dw"], PCOL["conv_dw_b"]
                        for q in range(8):
                            nc.vector.tensor_scalar(cv[:, q, :], cp[:, q, 0:T2], par[:, o_w + TAPS * q:o_w + TAPS * q + 1],
                                                    par[:, o_b + q:o_b + q + 1], ALU.mult, ALU.add).then_inc(tap_done, 1)
                        with dve.Fori(1, TAPS) as j:
                            for q in range(8):
                                dve.wait_ge(tap_done, j * 8 + q - 7)
                                nc.vector.scalar_tensor_tensor(
                                    out=cv[:, q, :], in0=cp[:, q, bass.ds(j, T2)],
                                    scalar=par[:, bass.ds(j + (o_w + TAPS * q), 1)], in1=cv[:, q, :],
                                    op0=ALU.mult, op1=ALU.add).then_inc(tap_done, 1)

                    @b.sync
                    def _(sp):
                        load_slabs(sp, "gate_a")
                px.close()
                normalize("lnconv", lambda q: cv[:, q, :], lambda q: cv[:, q, :], KD, T2, k0("mean1024"),
                          lambda q: pcol("conv_ln_g", q), lambda q: pcol("conv_ln_b", q), EPS_LN, ACT.Silu)
                ya_out, ya_done = sem("ya_out"), sem("ya_done")
                with ExitStack() as px, block() as b:
                    vx = Operand(px, "cv", KD, T2)
                    w = Weights(px, "cv")
                    vx.start(lambda q: cv[:, q, :])

                    @b.tensor
                    def _(pe):
                        pe_tiles(pe, w, "conv_out", KD, 8, vx, T2, ya_out, ya_done)

                    @b.scalar
                    def _(act):
                        w.begin(act, ["conv_out"], vx)
                        w.all_act(act, ["conv_out"])

                    @b.vector
                    def _(dve):
                        vx.dve(dve)
                        for i in range(8):
                            dve.wait_ge(ya_out, i + 1)
                            nc.vector.tensor_tensor(fold(y1(i), T2), fold(y1(i), T2), A(i % 4, T2),
                                                    ALU.mult).then_inc(ya_done, 1)

                    @b.gpsimd
                    def _(pool):
                        w.all_pool(pool, ["conv_out"])

                    @b.sync
                    def _(sp):
                        load_slabs(sp, "conv_out")
                        sp.dma_start(h_d, h[:, :, :]).then_inc(spilled, 16)
                        sp.wait_ge(ya_done, 8)
                        sp.dma_start(y_d, cp[:, :, 0:T2]).then_inc(spilled, 16)
                        sp.wait_ge(spilled, 32)
            with ExitStack() as wx:
                lw, a = sbt(wx, "rw_lw", [P, KD, T2]), sbt(wx, "rw_a", [P, KD, T2])
                xt = sbt(wx, "scratch", [P, KD, T1])
                kk = h
                wc = sbt(wx, "rw_wc", [P, KD, 9])
                decay_and_keys(xt, wa, r, k, v, kk, a, lw, wc, k2)
                recurrence(xt, wa, r, k, v, kk, a, lw, wc, k2)
                group_norm_and_gate(xt, r, k, v, lw, xg)
                merge(h, r, k, lw)

        def decay_and_keys(xt, wa, r, k, v, kk, a, lw, wc, k2):
            tanhed, up_ready, up_read = sem("tanhed"), sem("wu_ready"), sem("wu_read")
            with block() as b:
                @b.scalar
                def _(act):
                    nc.scalar.activation(wa[0:64, :], wa[0:64, :], ACT.Tanh).then_inc(tanhed, 1)
                    for i in range(16):
                        act.wait_ge(up_ready, i + 1)
                        d, name = (lw, "w0") if i % 2 == 0 else (a, "a0")
                        nc.scalar.activation(fold(d[:, i // 2, :], T2), A(i % 4, T2), ACT.Sigmoid,
                                             bias=pcol(name, i // 2)).then_inc(up_read, 1)

                @b.tensor
                def _(pe):
                    pe.wait_ge(tanhed, 1)
                    n = SLAB0["wa_up"]
                    slab_wait(pe, n)
                    for i in range(16):
                        r0 = 64 * (i % 2)
                        if i >= 4:
                            pe.wait_ge(up_read, i - 3)
                        for s, (lo, hi) in enumerate(halves(T2)):
                            mm = nc.tensor.matmul(acc[i % 4][:, s, 0:hi - lo], ring[n % RING][r0:r0 + 64, i // 2 * P:i // 2 * P + P],
                                                  wa[r0:r0 + 64, lo:hi], start=True, stop=True)
                        mm.then_inc(up_ready, 1)
                    freed_by[n] = (up_ready, 16)

                @b.sync
                def _(sp):
                    load_slabs(sp, "wa_up")
            kk_made, kk_sq, sq_summed, kk_root, key_done = (sem("kk_made"), sem("kk_sq"), sem("kk_summed"),
                                                          sem("kk_root"), sem("key_done"))
            normed = sem("kk_normed")
            with ExitStack() as nx, block() as b:
                sq = [xt[:, 2 * i:2 * i + 2, :].rearrange("p a t -> p (a t)")[:, 0:T2] for i in range(4)]
                root = [sbt(nx, f"kk_root{i}", [P, T2]) for i in range(2)]
                scr = sbt(nx, "key_scr", [P, T2])
                omk = sbt(nx, "omk", [P, KD])

                @b.vector
                def _(dve):
                    o = PCOL["k_a"]
                    link("dve", dve, nc.vector.tensor_scalar(omk[:, :], par[:, o:o + 8], -1.0, 1.0, ALU.mult, ALU.add))
                    for i in range(8):
                        nc.vector.tensor_scalar(kk[:, i, :], k[:, i, :], pcol("k_k", i), None, ALU.mult).then_inc(kk_made, 1)
                    for i in range(8):
                        link("dve", dve, nc.vector.tensor_scalar(scr[:, :], a[:, i, :], pcol("k_a", i), omk[:, i:i + 1],
                                                                 ALU.mult, ALU.add))
                        link("dve", dve, nc.vector.tensor_tensor(k[:, i, :], k[:, i, :], scr[:, :], ALU.mult))
                        dve.wait_ge(kk_root, i + 1)
                        link("dve", dve, nc.vector.tensor_scalar(root[i % 2][:, :], root[i % 2][:, :], 1e-12, None, ALU.max))
                        link("dve", dve, nc.vector.reciprocal(root[i % 2][:, :], root[i % 2][:, :]))
                        nc.vector.tensor_tensor(kk[:, i, :], kk[:, i, :], root[i % 2][:, :], ALU.mult).then_inc(normed, 1)

                def root_of(act, i):
                    act.wait_ge(sq_summed, i + 1)
                    if i >= 2:
                        act.wait_ge(normed, i - 1)
                    nc.scalar.activation(fold(root[i % 2][:, :], T2), A(i % 4, T2), ACT.Sqrt).then_inc(kk_root, 1)

                @b.scalar
                def _(act):
                    for i in range(8):
                        act.wait_ge(kk_made, i + 1)
                        if i >= 4:
                            act.wait_ge(sq_summed, i - 3)
                        nc.scalar.activation(sq[i % 4], kk[:, i, :], ACT.Square).then_inc(kk_sq, 1)
                        if i >= 1:
                            root_of(act, i - 1)
                    root_of(act, 7)

                @b.tensor
                def _(pe):
                    for i in range(8):
                        pe.wait_ge(kk_sq, i + 1)
                        if i >= 4:
                            pe.wait_ge(kk_root, i - 3)
                        for s, (lo, hi) in enumerate(halves(T2)):
                            mm = nc.tensor.matmul(acc[i % 4][:, s, 0:hi - lo], k0("ones64"), sq[i % 4][:, lo:hi],
                                                  start=True, stop=True)
                        mm.then_inc(sq_summed, 1)
            scanned, e_up, e_dn, up_used, b_made, dn_used = (sem("scanned"), sem("e_up"), sem("e_dn"), sem("up_used"),
                                                            sem("b_made"), sem("dn_used"))
            with ExitStack() as nx, block() as b:
                eu = [sbt(nx, f"eu{i}", [P, T2]) for i in range(2)]
                ed = [sbt(nx, f"ed{i}", [P, T2]) for i in range(2)]
                first = sbt(nx, "first", [P, 9])

                @b.vector
                def _(dve):
                    def scan(i):
                        link("dve", dve, nc.vector.tensor_scalar(lw[:, i, :], lw[:, i, :], -float(np.exp(-0.5)), None, ALU.mult))
                        nc.vector.tensor_tensor_scan(lw[:, i, :], k2("resets", T2), lw[:, i, :], 0.0, ALU.mult,
                                                     ALU.add).then_inc(scanned, 1)

                    scan(0)
                    for i in range(8):
                        if i < 7:
                            scan(i + 1)
                        dve.wait_ge(e_up, i + 1)
                        e = eu[i % 2]
                        nc.vector.tensor_tensor(r[:, i, :], r[:, i, :], e[:, :], ALU.mult)
                        nc.vector.tensor_copy(wc[:, i, 0:8], e[:, CH - 1:T1:CH])
                        nc.vector.tensor_copy(wc[:, i, 8:9], e[:, T2 - 1:T2])
                        dve.wait_ge(b_made, i + 1)
                        link("dve", dve, nc.vector.tensor_scalar(first[:, :], kk[:, i, 0:T2:CH], -1.0, None, ALU.mult))
                        link("dve", dve, nc.vector.scalar_tensor_tensor(out=kk[:, i, 1:T2], in0=kk[:, i, 1:T2], scalar=-1.0,
                                                                        in1=e[:, 0:T2 - 1], op0=ALU.mult, op1=ALU.mult))
                        nc.vector.tensor_copy(kk[:, i, 0:T2:CH], first[:, :]).then_inc(up_used, 1)
                        dve.wait_ge(up_used, i + 1)

                @b.scalar
                def _(act):
                    for i in range(8):
                        act.wait_ge(scanned, i + 1)
                        if i >= 2:
                            act.wait_ge(up_used, i - 1)
                            act.wait_ge(dn_used, i - 1)
                        nc.scalar.activation(eu[i % 2][:, :], lw[:, i, :], ACT.Exp).then_inc(e_up, 1)
                        nc.scalar.activation(ed[i % 2][:, :], lw[:, i, :], ACT.Exp, scale=-1.0).then_inc(e_dn, 1)

                @b.gpsimd
                def _(pool):
                    for i in range(8):
                        nc.gpsimd.tensor_tensor(a[:, i, :], a[:, i, :], kk[:, i, :], ALU.mult).then_inc(b_made, 1)
                    for i in range(8):
                        pool.wait_ge(e_dn, i + 1)
                        nc.gpsimd.tensor_tensor(k[:, i, :], k[:, i, :], ed[i % 2][:, :], ALU.mult)
                        pool.wait_ge(b_made, i + 1)
                        nc.gpsimd.tensor_tensor(a[:, i, :], a[:, i, :], ed[i % 2][:, :], ALU.mult).then_inc(dn_used, 1)
                    pool.wait_ge(dn_used, 8)

        def recurrence(xt, wa, r, k, v, kk, a, o, wc, k2):
            bank = lambda i: acc[i // 2][:, i % 2, :]
            tiles = [(i * P, P, [(0, CH), (CH, CH)], 6) for i in range(T2 // P)] + [(T1, META, [(0, META)], 4)]
            pe_did, act_did, dve_did, pool_did = sem("rec_pe"), sem("rec_act"), sem("rec_dve"), sem("rec_pool")
            arrays = [kk, a, k, v]
            gram_bank = lambda m, p: 2 * min(m, 3) + p

            def events(chunks, nl):
                two = range(2)
                pe = [("tm", g) for g in range(8)]
                act = [("tm", g) for g in range(0, 8, 2)]
                dve = [("tm", g) for g in range(1, 8, 2)]
                pool = []
                for bp in two:
                    grams = [("gram", bp, p, m) for m in range(5) for p in two]
                    pe += grams[:8]
                    dve += grams
                    for l in range(1, nl):
                        pe += [("x", bp, l, p) for p in two]
                        if l == 1:
                            pe += grams[8:]
                        pe += [("m", bp, l, p) for p in two]
                        act += [("x", bp, l, p) for p in two]
                        dve += [("m", bp, l, p) for p in two]
                        pool += [("ot", bp, l, p) for p in two]
                        if l == 1:
                            pool += [("mt", bp, p) for p in two]
                    pe += [("z", bp, p) for p in two] + [("ug", bp, p) for p in two]
                    act += [("z", bp, p) for p in two] + [("gt", bp, p) for p in two]
                    dve += [("uv", bp, p) for p in two]
                for j in range(len(chunks)):
                    pe += [("u", j), ("s", j)]
                    dve += [("u", j), ("s", j)]
                pe += [("y", 0), ("y", 1)]
                act += [("y", 0), ("y", 1)]
                return {"pe": pe, "act": act, "dve": dve, "pool": pool}

            plans, base = [], {"pe": 0, "act": 0, "dve": 0, "pool": 0}
            sems = {"pe": pe_did, "act": act_did, "dve": dve_did, "pool": pool_did}
            for t0, n, chunks, nl in tiles:
                ev = events(chunks, nl)
                plans.append({(e, name): base[e] + i + 1 for e in ev for i, name in enumerate(ev[e])})
                for e in ev:
                    base[e] += len(ev[e])

            def after(eng, ti, who, *name):
                eng.wait_ge(sems[who], plans[ti][(who, name)])

            sent = {e: 0 for e in sems}

            def did(ins, ti, who, *name):
                sent[who] += 1
                assert plans[ti][(who, name)] == sent[who], (ti, who, name)
                ins.then_inc(sems[who], 1)

            with ExitStack() as nx, block() as b:
                tm = [sbt(nx, f"tm{i}", [P, D]) for i in range(4)]
                tm_a, tm_b, tm_k, tm_v = tm
                arb, ark = sbt(nx, "arb", [P, 8, 2, P]), sbt(nx, "ark", [P, 8, 2, P])
                gt, uv = sbt(nx, "gt", [P, 8, P]), sbt(nx, "uv", [P, 8, 2, 64])
                S = [sbt(nx, f"S{i}", [P, 8, 64]) for i in range(3)]
                at = [sbt(nx, f"at{p}", [P, 4, P]) for p in range(2)]
                aak = [sbt(nx, f"aak{p}", [P, 4, P]) for p in range(2)]
                M = [xt[:, 2 * p, :].rearrange("p (q t) -> p q t", q=4) for p in range(2)]
                MT = [xt[:, 2 * p + 1, :].rearrange("p (q t) -> p q t", q=4) for p in range(2)]
                X = [xt[:, 4 + p, :].rearrange("p (q t) -> p q t", q=4) for p in range(2)]
                four = lambda ap: ap.rearrange("p (q t) -> p q t", q=4)
                OT = [[four(xt[:, 7, :]), four(wa[:, 0:512])], [four(k2("resets", 512)), sbt(nx, "ot", [P, 4, P])]]
                z = [four(xt[:, 6, 256 * p:256 * p + 256]) for p in range(2)]
                grid = lambda i, n, w=P: bank(i)[:, 0:4 * w].rearrange("p (q t) -> p q t", q=4)[0:n, :, 0:min(n, w)]
                mask = lambda ap, n: ap[0:n, 0:n].unsqueeze(1).to_broadcast([n, 4, n])

                @b.tensor
                def _(pe):
                    mmul = nc.tensor.matmul
                    chunk0 = 0
                    for ti, (t0, n, chunks, nl) in enumerate(tiles):
                        for g in range(8):
                            if g == 0 and ti:
                                after(pe, ti - 1, "act", "y", 1)
                                after(pe, ti - 1, "dve", "s", len(tiles[ti - 1][2]) - 1)
                            for q in range(4):
                                mm = nc.tensor.transpose(bank(g)[0:n, q * P:(q + 1) * P],
                                                         arrays[g // 2][:, 4 * (g % 2) + q, t0:t0 + n], k0("ident"))
                            did(mm, ti, "pe", "tm", g)
                        for bp in range(2):
                            def gram(m, p):
                                rows = slice(64 * p, 64 * p + 64)
                                left, right = [(a, kk), (kk, a), (k, kk), (a, r), (k, r)][m]
                                for q in range(4):
                                    mm = mmul(bank(gram_bank(m, p))[0:n, q * P:q * P + n], left[rows, 4 * bp + q, t0:t0 + n],
                                              right[rows, 4 * bp + q, t0:t0 + n], start=True, stop=True)
                                did(mm, ti, "pe", "gram", bp, p, m)

                            if bp == 0:
                                after(pe, ti, "act", "tm", 6)
                                after(pe, ti, "dve", "tm", 7)
                            else:
                                after(pe, ti, "act", "gt", 0, 1)
                                after(pe, ti, "dve", "uv", 0, 1)
                            for m in range(4):
                                for p in range(2):
                                    gram(m, p)
                            for l in range(1, nl):
                                for p in range(2):
                                    if l == 1:
                                        after(pe, ti, "dve", "gram", bp, p, 1)
                                    after(pe, ti, "pool", "ot", bp, l, p)
                                    if l > 1:
                                        after(pe, ti, "dve", "m", bp, l - 1, p)
                                    for q in range(4):
                                        mm = mmul(bank(p)[0:n, q * P:q * P + n], OT[l % 2][p][0:n, q, 0:n], M[p][0:n, q, 0:n],
                                                  start=True, stop=True)
                                    did(mm, ti, "pe", "x", bp, l, p)
                                if l == 1:
                                    for p in range(2):
                                        after(pe, ti, "dve", "gram", bp, p, 3)
                                        gram(4, p)
                                for p in range(2):
                                    after(pe, ti, "act", "x", bp, l, p)
                                    if l == 1:
                                        after(pe, ti, "pool", "mt", bp, p)
                                    if l < nl - 1:
                                        for q in range(4):
                                            mmul(bank(2 + p)[0:n, q * P:q * P + n], MT[p][0:n, q, 0:n], X[p][0:n, q, 0:n],
                                                 start=True, stop=True)
                                    for q in range(4):
                                        mm = mmul(bank(4 + p)[0:n, q * P:q * P + n], X[p][0:n, q, 0:n], MT[p][0:n, q, 0:n],
                                                  start=True, stop=True)
                                    did(mm, ti, "pe", "m", bp, l, p)
                            for p in range(2):
                                after(pe, ti, "dve", "gram", bp, p, 4)
                                for q in range(4):
                                    hd = 64 * (2 * (4 * bp + q) + p)
                                    mm = mmul(bank(6 + p)[0:n, q * 64:q * 64 + 64], aak[p][0:n, q, 0:n],
                                              tm_v[0:n, hd:hd + 64], start=True, stop=True)
                                did(mm, ti, "pe", "z", bp, p)
                            for p in range(2):
                                after(pe, ti, "act", "z", bp, p)
                                after(pe, ti, "dve", "m", bp, nl - 1, p)
                                for q in range(4):
                                    mmul(bank(p)[0:n, q * 64:q * 64 + 64], MT[p][0:n, q, 0:n], z[p][0:n, q, :],
                                         start=True, stop=True)
                                for q in range(4):
                                    hd = 64 * (2 * (4 * bp + q) + p)
                                    mm = mmul(bank(2 + p)[64 * p:64 * p + 64, q * P:q * P + n], tm_a[0:n, hd:hd + 64],
                                              MT[p][0:n, q, 0:n], start=True, stop=True)
                                did(mm, ti, "pe", "ug", bp, p)
                        after(pe, ti, "act", "gt", 1, 1)
                        after(pe, ti, "dve", "uv", 1, 1)
                        for j, (c0_, cn) in enumerate(chunks):
                            s = S[(chunk0 + j) % 3]
                            if j:
                                after(pe, ti, "dve", "s", j - 1)
                            for p in range(2):
                                rows = slice(64 * p, 64 * p + 64)
                                for q in range(8):
                                    mm = mmul(bank(p)[c0_:c0_ + cn, q * 64:q * 64 + 64], gt[rows, q, c0_:c0_ + cn],
                                              s[rows, q, :], start=True, stop=True)
                            did(mm, ti, "pe", "u", j)
                            after(pe, ti, "dve", "u", j)
                            cr = slice(c0_, c0_ + cn)
                            for q in range(8):
                                for p in range(2):
                                    hd = 64 * (2 * q + p)
                                    d = bank(2)[64 * p:64 * p + 64, q * 64:q * 64 + 64]
                                    mmul(d, tm_b[cr, hd:hd + 64], uv[cr, q, p, :], start=True, stop=False)
                                    mm = mmul(d, tm_k[cr, hd:hd + 64], tm_v[cr, hd:hd + 64], start=False, stop=True)
                            did(mm, ti, "pe", "s", j)
                        for half in range(2):
                            for q in range(4 * half, 4 * half + 4):
                                for p in range(2):
                                    hd = 64 * (2 * q + p)
                                    rows = slice(64 * p, 64 * p + 64)
                                    at0 = q % 4 * P
                                    d = bank(4 + half)[rows, at0:at0 + n]
                                    mmul(d, uv[0:n, q, p, :], arb[0:n, q, p, 0:n], start=True, stop=False)
                                    mmul(d, tm_v[0:n, hd:hd + 64], ark[0:n, q, p, 0:n], start=False, stop=False)
                                    for j, (c0_, cn) in enumerate(chunks):
                                        mm = mmul(bank(4 + half)[rows, at0 + c0_:at0 + c0_ + cn], S[(chunk0 + j) % 3][rows, q, :],
                                                  r[rows, q, t0 + c0_:t0 + c0_ + cn], start=False, stop=j == len(chunks) - 1)
                            did(mm, ti, "pe", "y", half)
                        chunk0 += len(chunks)

                @b.scalar
                def _(act):
                    cp_ = lambda d, s_: nc.scalar.activation(d, s_, ACT.Copy)
                    for ti, (t0, n, chunks, nl) in enumerate(tiles):
                        for g in range(0, 8, 2):
                            after(act, ti, "pe", "tm", g)
                            did(cp_(tm[g // 2][0:n, 0:512], bank(g)[0:n, :]), ti, "act", "tm", g)
                        for bp in range(2):
                            for l in range(1, nl):
                                for p in range(2):
                                    after(act, ti, "pe", "x", bp, l, p)
                                    did(cp_(X[p][0:n, :, 0:n], grid(p, n)), ti, "act", "x", bp, l, p)
                            for p in range(2):
                                after(act, ti, "pe", "z", bp, p)
                                did(cp_(z[p][0:n, :, :], bank(6 + p)[0:n, 0:256].rearrange("p (q t) -> p q t", q=4)),
                                    ti, "act", "z", bp, p)
                            for p in range(2):
                                after(act, ti, "pe", "ug", bp, p)
                                rows = slice(64 * p, 64 * p + 64)
                                src = bank(2 + p).rearrange("p (q t) -> p q t", q=4)[rows, :, 0:n]
                                did(cp_(gt[rows, 4 * bp:4 * bp + 4, 0:n], src), ti, "act", "gt", bp, p)
                        for half in range(2):
                            after(act, ti, "pe", "y", half)
                            src = bank(4 + half).rearrange("p (q t) -> p q t", q=4)[:, :, 0:n]
                            did(cp_(o[:, 4 * half:4 * half + 4, t0:t0 + n], src), ti, "act", "y", half)

                @b.vector
                def _(dve):
                    tt = nc.vector.tensor_tensor
                    link("dve", dve, nc.vector.memset(S[0][:, :, :], 0.0))
                    chunk0 = 0
                    for ti, (t0, n, chunks, nl) in enumerate(tiles):
                        for g in range(1, 8, 2):
                            after(dve, ti, "pe", "tm", g)
                            did(nc.vector.tensor_copy(tm[g // 2][0:n, 512:1024], bank(g)[0:n, :]), ti, "dve", "tm", g)
                        for bp in range(2):
                            if bp:
                                after(dve, ti, "pool", "ot", 0, nl - 1, 1)
                            for m in range(5):
                                for p in range(2):
                                    after(dve, ti, "pe", "gram", bp, p, m)
                                    src = grid(gram_bank(m, p), n)
                                    d, mk = [(at[p][0:n, :, 0:n], "strict"), (M[p][0:n, :, 0:n], "level0_low"),
                                             (aak[p][0:n, :, 0:n], "strict"), (arb[0:n, 4 * bp:4 * bp + 4, p, 0:n], "incl"),
                                             (ark[0:n, 4 * bp:4 * bp + 4, p, 0:n], "incl")][m]
                                    ins = tt(d, src, mask(k2(mk), n), ALU.mult)
                                    if m == 1:
                                        link("dve", dve, ins)
                                        ins = tt(d, d, mask(k0("ident"), n), ALU.add)
                                    did(ins, ti, "dve", "gram", bp, p, m)
                            for l in range(1, nl):
                                for p in range(2):
                                    after(dve, ti, "pe", "m", bp, l, p)
                                    if l < nl - 1:
                                        tt(M[p][0:n, :, 0:n], M[p][0:n, :, 0:n], grid(2 + p, n), ALU.add)
                                    did(tt(MT[p][0:n, :, 0:n], MT[p][0:n, :, 0:n], grid(4 + p, n), ALU.add),
                                        ti, "dve", "m", bp, l, p)
                            for p in range(2):
                                after(dve, ti, "pe", "ug", bp, p)
                                did(nc.vector.tensor_copy(uv[0:n, 4 * bp:4 * bp + 4, p, :],
                                                          bank(p)[0:n, 0:256].rearrange("p (q t) -> p q t", q=4)),
                                    ti, "dve", "uv", bp, p)
                        for j, (c0_, cn) in enumerate(chunks):
                            after(dve, ti, "pe", "u", j)
                            cr = slice(c0_, c0_ + cn)
                            for p in range(2):
                                ins = tt(uv[cr, :, p, :], uv[cr, :, p, :], bank(p)[cr, :].rearrange("p (q t) -> p q t", q=8), ALU.add)
                            did(ins, ti, "dve", "u", j)
                            after(dve, ti, "pe", "s", j)
                            cg = chunk0 + j
                            s, sn = S[cg % 3], S[(cg + 1) % 3]
                            link("dve", dve, tt(sn[:, :, :], s[:, :, :], bank(2).rearrange("p (q t) -> p q t", q=8), ALU.add))
                            did(tt(sn[:, :, :], sn[:, :, :], wc[:, :, cg:cg + 1].to_broadcast([P, 8, 64]), ALU.mult),
                                ti, "dve", "s", j)
                            after(dve, ti, "dve", "s", j)
                        chunk0 += len(chunks)

                @b.gpsimd
                def _(pool):
                    tt = nc.gpsimd.tensor_tensor
                    for ti, (t0, n, chunks, nl) in enumerate(tiles):
                        for bp in range(2):
                            def off_diagonal(l, p):
                                did(tt(OT[l % 2][p][0:n, :, 0:n], at[p][0:n, :, 0:n], mask(k2("levels", P, l * P), n), ALU.mult),
                                    ti, "pool", "ot", bp, l, p)

                            for p in range(2):
                                after(pool, ti, "dve", "gram", bp, p, 0)
                                if bp or ti:
                                    after(pool, *((ti, "pe", "ug", 0, p) if bp else (ti - 1, "pe", "ug", 1, p)))
                                off_diagonal(1, p)
                            for p in range(2):
                                d = MT[p][0:n, :, 0:n]
                                link("pool", pool, tt(d, at[p][0:n, :, 0:n], mask(k2("levels"), n), ALU.mult))
                                did(tt(d, d, mask(k0("ident"), n), ALU.add), ti, "pool", "mt", bp, p)
                            for l in range(2, nl):
                                for p in range(2):
                                    if l > 2:
                                        after(pool, ti, "pe", "x", bp, l - 2, p)
                                    off_diagonal(l, p)
                    pool.wait_ge(pool_did, base["pool"])

        def group_norm_and_gate(xt, r, k, v, o, xg):
            meaned, centred, squared, varred, rooted = (sem("gn_" + n) for n in ("meaned", "centred", "squared", "varred", "rooted"))
            scaled, shifted, prod_made, bonus, bonus_read = (sem("gn_" + n) for n in ("scaled", "shifted", "prod", "bonus", "bonus_read"))
            added, g_ready, gated, sig = (sem("gn_" + n) for n in ("added", "g_ready", "gated", "sig"))
            with ExitStack() as nx, block() as b:
                view = lambda i: xt[:, 2 * i:2 * i + 2, :].rearrange("p a t -> p (a t)")[:, 0:T2]
                sq, prod = [view(0), view(1)], [view(2), view(3)]
                root = [sbt(nx, f"gn_root{i}", [P, T2]) for i in range(2)]
                bon = [sbt(nx, f"gn_bon{i}", [P, T2]) for i in range(2)]

                @b.tensor
                def _(pe):
                    def over(j, mat, x):
                        for s, (lo, hi) in enumerate(halves(T2)):
                            mm = nc.tensor.matmul(acc[j][:, s, 0:hi - lo], mat, x[:, lo:hi], start=True, stop=True)
                        return mm

                    n = SLAB0["g_up"]
                    for i in range(8):
                        if i >= 1:
                            pe.wait_ge(centred, i)
                        over(0, k0("mean64"), o[:, i, :]).then_inc(meaned, 1)
                        pe.wait_ge(prod_made, i + 1)
                        if i >= 1:
                            pe.wait_ge(bonus_read, i)
                        over(2, k0("ones64"), prod[i % 2]).then_inc(bonus, 1)
                        pe.wait_ge(squared, i + 1)
                        if i >= 1:
                            pe.wait_ge(rooted, i)
                        over(1, k0("mean64"), sq[i % 2]).then_inc(varred, 1)
                        if i == 0:
                            pe.wait_ge(sig, 1)
                            slab_wait(pe, n)
                            slab_wait(pe, n + 1)
                        else:
                            pe.wait_ge(gated, i)
                        for q in range(2):
                            for s, (lo, hi) in enumerate(halves(T2)):
                                mm = nc.tensor.matmul(acc[3][:, s, 0:hi - lo], ring[(n + q) % RING][:, i * P:(i + 1) * P],
                                                      xg[:, q, lo:hi], start=(q == 0), stop=(q == 1))
                        mm.then_inc(g_ready, 1)
                    freed_by[n] = freed_by[n + 1] = (g_ready, 8)

                @b.scalar
                def _(act):
                    nc.scalar.activation(xg[:, :, :], xg[:, :, :], ACT.Sigmoid).then_inc(sig, 1)
                    for i in range(8):
                        act.wait_ge(centred, i + 1)
                        if i >= 2:
                            act.wait_ge(varred, i - 1)
                        nc.scalar.activation(sq[i % 2], o[:, i, :], ACT.Square).then_inc(squared, 1)
                        act.wait_ge(varred, i + 1)
                        if i >= 2:
                            act.wait_ge(scaled, i - 1)
                        nc.scalar.activation(fold(root[i % 2][:, :], T2), A(1, T2), ACT.Sqrt,
                                             bias=k0("eps", 1, EPS_GN)).then_inc(rooted, 1)
                        act.wait_ge(scaled, i + 1)
                        nc.scalar.activation(o[:, i, :], o[:, i, :], ACT.Identity, scale=pcol("lnx_g", i),
                                             bias=pcol("lnx_b", i)).then_inc(shifted, 1)

                @b.vector
                def _(dve):
                    tt = nc.vector.tensor_tensor
                    for i in range(8):
                        dve.wait_ge(meaned, i + 1)
                        tt(fold(o[:, i, :], T2), fold(o[:, i, :], T2), A(0, T2), ALU.subtract).then_inc(centred, 1)
                        if i >= 2:
                            dve.wait_ge(bonus, i - 1)
                        nc.vector.scalar_tensor_tensor(out=prod[i % 2], in0=r[:, i, :], scalar=pcol("r_k", i), in1=k[:, i, :],
                                                       op0=ALU.mult, op1=ALU.mult).then_inc(prod_made, 1)
                        dve.wait_ge(bonus, i + 1)
                        if i >= 2:
                            dve.wait_ge(added, i - 1)
                        tt(fold(bon[i % 2][:, :], T2), fold(v[:, i, :], T2), A(2, T2), ALU.mult).then_inc(bonus_read, 1)
                        dve.wait_ge(rooted, i + 1)
                        link("dve", dve, nc.vector.reciprocal(root[i % 2][:, :], root[i % 2][:, :]))
                        tt(o[:, i, :], o[:, i, :], root[i % 2][:, :], ALU.mult).then_inc(scaled, 1)
                        dve.wait_ge(added, i + 1)
                        dve.wait_ge(g_ready, i + 1)
                        tt(fold(o[:, i, :], T2), fold(o[:, i, :], T2), A(3, T2), ALU.mult).then_inc(gated, 1)

                @b.gpsimd
                def _(pool):
                    for i in range(8):
                        pool.wait_ge(shifted, i + 1)
                        pool.wait_ge(bonus_read, i + 1)
                        nc.gpsimd.tensor_tensor(o[:, i, :], o[:, i, :], bon[i % 2][:, :], ALU.add).then_inc(added, 1)
                    pool.wait_ge(added, 8)

                @b.sync
                def _(sp):
                    load_slabs(sp, "g_up")

        def merge(h, y, gb, o):
            back = sem("unspilled")
            g_ready, g_out, o_ready, o_out, y_done = (sem("mg_" + n) for n in ("g_ready", "g_out", "o_ready", "o_out", "y_done"))
            with ExitStack() as px, block() as b:
                hx = Operand(px, "mg", KD, T2)
                w = Weights(px, "mg")
                hx.start(lambda q: h[:, q, :])

                @b.sync
                def _(sp):
                    sp.dma_start(h[:, :, :], h_d).then_inc(back, 16)
                    sp.wait_ge(back, 16)
                    sp.dma_start(y[:, :, :], y_d).then_inc(back, 16)
                    load_slabs(sp, "gate_b")
                    sp.wait_ge(back, 32)

                @b.tensor
                def _(pe):
                    pe_tiles(pe, w, "gate_b", KD, 8, hx, T2, g_ready, g_out)

                @b.scalar
                def _(act):
                    act.wait_ge(back, 16)
                    w.begin(act, ["gate_b"], hx)

                    def take(i):
                        act.wait_ge(g_ready, i + 1)
                        nc.scalar.activation(fold(gb[:, i, :], T2), A(i % 4, T2), ACT.Sigmoid,
                                             bias=pcol("b_gate", 8 + i)).then_inc(g_out, 1)

                    tile_loop(act, w, [("gate_b", KD, 8)], take)

                @b.vector
                def _(dve):
                    hx.dve(dve)

                @b.gpsimd
                def _(pool):
                    w.all_pool(pool, ["gate_b"])
            with ExitStack() as px, block() as b:
                ox = Operand(px, "rwo", KD, T2)
                w = Weights(px, "rwo")
                ox.start(lambda q: o[:, q, :])

                @b.tensor
                def _(pe):
                    pe_tiles(pe, w, "rw_out", KD, 8, ox, T2, o_ready, o_out)

                @b.scalar
                def _(act):
                    w.begin(act, ["rw_out"], ox)
                    w.all_act(act, ["rw_out"])

                @b.vector
                def _(dve):
                    ox.dve(dve)
                    for i in range(8):
                        dve.wait_ge(o_ready, i + 1)
                        nc.vector.tensor_tensor(fold(gb[:, i, :], T2), fold(gb[:, i, :], T2), A(i % 4, T2),
                                                ALU.mult).then_inc(o_out, 1)

                @b.gpsimd
                def _(pool):
                    parts = slab_range("rw_out")
                    for n in parts[:3]:
                        w.pool(pool, n)
                    for i in range(8):
                        if i + 3 < 8:
                            w.pool(pool, parts[i + 3])
                        pool.wait_ge(o_out, i + 1)
                        nc.gpsimd.tensor_tensor(y[:, i, :], y[:, i, :], gb[:, i, :], ALU.add).then_inc(y_done, 1)
                    pool.wait_ge(y_done, 8)

                @b.sync
                def _(sp):
                    load_slabs(sp, "rw_out")
            w_ready, w_out = sem("mg_w_ready"), sem("mg_w_out")
            with ExitStack() as px, block() as b:
                yx = Operand(px, "wo2", KD, T2)
                w = Weights(px, "wo2")
                yx.start(lambda q: y[:, q, :])

                @b.tensor
                def _(pe):
                    pe_tiles(pe, w, "w_o2", KD, 8, yx, T2, w_ready, w_out)

                @b.scalar
                def _(act):
                    w.begin(act, ["w_o2"], yx)
                    w.all_act(act, ["w_o2"])

                @b.vector
                def _(dve):
                    yx.dve(dve)
                    for i in range(8):
                        dve.wait_ge(w_ready, i + 1)
                        nc.vector.scalar_tensor_tensor(out=fold(h[:, i, :], T2), in0=fold(h[:, i, :], T2), scalar=ALPHA,
                                                       in1=A(i % 4, T2), op0=ALU.mult, op1=ALU.add).then_inc(w_out, 1)

                @b.gpsimd
                def _(pool):
                    w.all_pool(pool, ["w_o2"])

                @b.sync
                def _(sp):
                    load_slabs(sp, "w_o2")
            ht = lambda q: h[:, q, :]
            normalize("ln1", ht, ht, KD, T2, k0("mean1024"), lambda q: pcol("ln1_g", q), lambda q: pcol("ln1_b", q), EPS_LN)

        def ffn(h):
            up_ready, up_read, tapped, silued, hid_made = (sem("ff_" + n) for n in ("up_ready", "up_read", "tapped", "silued", "hid"))
            dn_ready, dn_out, stored = sem("ff_dn_ready"), sem("ff_dn_out"), sem("out_stored")
            with ExitStack() as fx:
                hid = sbt(fx, "ff_hid", [P, NF, T2])
                with ExitStack() as ux, block() as b:
                    up = [sbt(ux, f"ff_up{i}", [P, 2 + T2]) for i in range(4)]
                    t = [sbt(ux, f"ff_t{i}", [P, T2]) for i in range(4)]
                    padded = sem("ff_padded")
                    hx = Operand(ux, "ff", KD, T2)
                    w = Weights(ux, "ff")
                    hx.start(lambda q: h[:, q, :])

                    @b.tensor
                    def _(pe):
                        pe_tiles(pe, w, "ffn_up", KD, 2 * NF, hx, T2, up_ready, up_read)

                    def silu(act, f):
                        act.wait_ge(tapped, 2 * f + 2)
                        g = t[(2 * f + 1) % 4]
                        nc.scalar.activation(g[:, :], g[:, :], ACT.Silu).then_inc(silued, 1)

                    @b.scalar
                    def _(act):
                        w.begin(act, ["ffn_up"], hx)
                        act.wait_ge(padded, 4)

                        def take(i):
                            act.wait_ge(up_ready, i + 1)
                            if i >= 4:
                                act.wait_ge(tapped, i - 3)
                            nc.scalar.activation(fold(up[i % 4][:, 2:2 + T2], T2), A(i % 4, T2), ACT.Copy).then_inc(up_read, 1)
                            if i % 2 and i >= 3:
                                silu(act, i // 2 - 1)

                        tile_loop(act, w, [("ffn_up", KD, 2 * NF)], take)
                        silu(act, NF - 1)

                    @b.vector
                    def _(dve):
                        hx.dve(dve)
                        o_w = PCOL["ffn_dw"]
                        for i in range(4):
                            nc.vector.memset(up[i][:, 0:2], 0.0).then_inc(padded, 1)
                        for i in range(2 * NF):
                            f = i // 2 + NF * (i % 2)
                            tap = lambda j: par[:, o_w + 3 * f + j:o_w + 3 * f + j + 1]
                            d = t[i % 4][:, :]
                            dve.wait_ge(up_read, i + 1)
                            if i >= 4:
                                dve.wait_ge(hid_made, i // 2 - 1)
                            link("dve", dve, nc.vector.tensor_scalar(d, up[i % 4][:, 0:T2], tap(0), None, ALU.mult))
                            link("dve", dve, nc.vector.scalar_tensor_tensor(out=d, in0=up[i % 4][:, 1:1 + T2], scalar=tap(1), in1=d,
                                                                            op0=ALU.mult, op1=ALU.add))
                            nc.vector.scalar_tensor_tensor(out=d, in0=up[i % 4][:, 2:2 + T2], scalar=tap(2), in1=d,
                                                           op0=ALU.mult, op1=ALU.add).then_inc(tapped, 1)

                    @b.gpsimd
                    def _(pool):
                        parts = slab_range("ffn_up")
                        for n in parts[:4]:
                            w.pool(pool, n)
                        for f in range(NF):
                            for n in parts[2 * f + 4:2 * f + 6]:
                                w.pool(pool, n)
                            pool.wait_ge(silued, f + 1)
                            nc.gpsimd.tensor_tensor(hid[:, f, :], t[2 * f % 4][:, :], t[(2 * f + 1) % 4][:, :],
                                                    ALU.mult).then_inc(hid_made, 1)
                        pool.wait_ge(hid_made, NF)

                    @b.sync
                    def _(sp):
                        load_slabs(sp, "ffn_up")
                with ExitStack() as dx, block() as b:
                    ux = Operand(dx, "fd", NF, T2)
                    w = Weights(dx, "fd", 2)
                    ux.start(lambda q: hid[:, q, :])

                    @b.tensor
                    def _(pe):
                        pe_tiles(pe, w, "ffn_down", NF, 8, ux, T2, dn_ready, dn_out)

                    @b.scalar
                    def _(act):
                        parts = slab_range("ffn_down")
                        for n in parts[:2]:
                            w.act(act, n)
                        ux.act(act, 0, 16)
                        w.act(act, parts[2])
                        ux.act(act, 16, NF)
                        for n in parts[3:]:
                            w.act(act, n)

                    @b.vector
                    def _(dve):
                        ux.dve(dve)
                        for i in range(8):
                            dve.wait_ge(dn_ready, i + 1)
                            nc.vector.scalar_tensor_tensor(out=fold(h[:, i, :], T2), in0=fold(h[:, i, :], T2), scalar=ALPHA,
                                                           in1=A(i % 4, T2), op0=ALU.mult, op1=ALU.add).then_inc(dn_out, 1)

                    @b.gpsimd
                    def _(pool):
                        w.all_pool(pool, ["ffn_down"])

                    @b.sync
                    def _(sp):
                        load_slabs(sp, "ffn_down")
            ht = lambda q: h[:, q, :]
            normalize("ln2", ht, ht, KD, T2, k0("mean1024"), lambda q: pcol("ln2_g", q), lambda q: pcol("ln2_b", q), EPS_LN)
            with block() as b:
                @b.sync
                def _(sp):
                    sp.dma_start(out, h[:, :, META:T2]).then_inc(stored, 16)
                    sp.wait_ge(stored, 16)

        with ExitStack() as second:
            with ExitStack() as first:
                xt = first.enter_context(nc.sbuf_tensor("xt", [P, KD, T1], F32, side="right"))
                x2 = first_block(xt, lambda: sbt(second, "x2", [P, KD, T2]))
            second_block(x2)


def kernel(**inputs):
    import numpy as _np
    import concourse.bacc as _bacc
    from concourse.bass_utils import run_bass_kernel_spmd as _run

    nc = _bacc.Bacc("TRN2", target_bir_lowering=False, num_devices=1)
    a = {k: _np.asarray(v) for k, v in inputs.items()}
    arrays = lay_out(a)
    args = [nc.dram_tensor(name, v.shape, mybir.dt.from_np(v.dtype), kind="ExternalInput").ap()
            for name, v in arrays.items()]
    args.append(nc.dram_tensor("out_t", (P, KD, T1), F32, kind="ExternalOutput").ap())
    program(nc, *args)
    got = _run(nc, [arrays], core_ids=[0]).results[0]["out_t"]
    return _np.ascontiguousarray(_np.asarray(got).transpose(2, 1, 0).reshape(1, T1, D))
```
